# Optimizing a Trainium2 kernel written in Bass

```python
import math
import jax, jax.numpy as jnp
from jax import lax
import numpy as np

D_MODEL = 1024
BATCH = 1
SEQ = 512
DEPTH = 1

D_INNER = D_MODEL
M_WIDTH = D_INNER // 2
M_HEADS = 4
M_HEAD_DIM = M_WIDTH // M_HEADS
H_WIDTH = D_INNER - M_WIDTH
H_GROUPS = 8
HYENA_ORDER = 2
N_DIR = 2
CHUNK = 128
FILTER_EMB = 33
FILTER_HIDDEN = 64
N_SIN = 3
DECAY_TARGET = 1e-2
FAST_DECAY_PCT = 0.3
SLOW_DECAY_PCT = 1.5
D_FF = 4 * D_MODEL
N_GATE = 2 * N_DIR * M_HEADS
EPS = 1e-6

OFF_MQ = 0
OFF_MK = OFF_MQ + M_WIDTH
OFF_HV = OFF_MK + M_WIDTH
OFF_HX1 = OFF_HV + H_WIDTH
OFF_HX2 = OFF_HX1 + H_WIDTH
N_CONV = OFF_HX2 + H_WIDTH
OFF_MV = N_CONV
OFF_MO = OFF_MV + M_WIDTH
OFF_GATE = OFF_MO + M_WIDTH
N_IN = OFF_GATE + N_GATE


def rms_norm(x, w):
    xf = x.astype(jnp.float32)
    y = xf * lax.rsqrt(jnp.mean(xf * xf, axis=-1, keepdims=True) + EPS)
    return (y * w.astype(jnp.float32)).astype(x.dtype)

def short_conv3(u, w, b):
    up = jnp.pad(u, ((0, 0), (1, 1), (0, 0)))
    return up[:, :-2] * w[0] + up[:, 1:-1] * w[1] + up[:, 2:] * w[2] + b

def mlstm_chunkwise(q, k, v, log_i, log_f):
    B, H, S, D = q.shape
    L = CHUNK
    NC = S // L
    qc = q.reshape(B, H, NC, L, D)
    kc = k.reshape(B, H, NC, L, D)
    vc = v.reshape(B, H, NC, L, D)
    li = log_i.reshape(B, H, NC, L)
    bcum = jnp.cumsum(log_f.reshape(B, H, NC, L), axis=-1)
    g = bcum[..., -1]
    a = g[..., None] - bcum + li

    def step(carry, xs):
        C, n, m = carry
        k_c, v_c, a_c, g_c = xs
        m_new = jnp.maximum(g_c + m, jnp.max(a_c, axis=-1))
        decay = jnp.exp(g_c + m - m_new)
        w = jnp.exp(a_c - m_new[..., None])
        C_new = decay[..., None, None] * C + jnp.einsum('bhl,bhld,bhle->bhde', w, k_c, v_c)
        n_new = decay[..., None] * n + jnp.einsum('bhl,bhld->bhd', w, k_c)
        return (C_new, n_new, m_new), (C, n, m)

    init = (jnp.zeros((B, H, D, D), jnp.float32),
            jnp.zeros((B, H, D), jnp.float32),
            jnp.zeros((B, H), jnp.float32))
    xs = (jnp.moveaxis(kc, 2, 0), jnp.moveaxis(vc, 2, 0),
          jnp.moveaxis(a, 2, 0), jnp.moveaxis(g, 2, 0))
    _, (C_s, n_s, m_s) = lax.scan(step, init, xs)
    C_s = jnp.moveaxis(C_s, 0, 2)
    n_s = jnp.moveaxis(n_s, 0, 2)
    m_s = jnp.moveaxis(m_s, 0, 2)

    causal = jnp.tril(jnp.ones((L, L), dtype=bool))
    dmat = bcum[..., :, None] - bcum[..., None, :] + li[..., None, :]
    dmat = jnp.where(causal, dmat, -jnp.inf)
    inter_log = bcum + m_s[..., None]
    m_t = jnp.maximum(inter_log, jnp.max(dmat, axis=-1))
    wts = jnp.exp(dmat - m_t[..., None])
    s_qk = jnp.einsum('bhctd,bhcsd->bhcts', qc, kc) * wts
    inter_scale = jnp.exp(inter_log - m_t)
    num = (jnp.einsum('bhcts,bhcse->bhcte', s_qk, vc)
           + inter_scale[..., None] * jnp.einsum('bhctd,bhcde->bhcte', qc, C_s))
    den = s_qk.sum(-1) + inter_scale * jnp.einsum('bhctd,bhcd->bhct', qc, n_s)
    h = num / jnp.maximum(jnp.abs(den), jnp.exp(-m_t))[..., None]
    return h.reshape(B, H, S, D)

def hyena_filters(L, w1, b1, w2, b2, w3, b3, w4, freq):
    bands = (FILTER_EMB - 1) // 2
    t = jnp.linspace(0.0, 1.0, L, dtype=jnp.float32)[:, None]
    t_resc = jnp.arange(L, dtype=jnp.float32)[:, None]
    ang = 2.0 * math.pi * t_resc / L
    f = jnp.linspace(1e-4, bands - 1, bands, dtype=jnp.float32)[None, :]
    z = jnp.concatenate([t, jnp.cos(f * ang), -jnp.sin(f * ang)], axis=-1)
    fr = freq.astype(jnp.float32)
    h = jnp.sin(fr[0] * (z @ w1.astype(jnp.float32) + b1.astype(jnp.float32)))
    h = jnp.sin(fr[1] * (h @ w2.astype(jnp.float32) + b2.astype(jnp.float32)))
    h = jnp.sin(fr[2] * (h @ w3.astype(jnp.float32) + b3.astype(jnp.float32)))
    h = (h @ w4.astype(jnp.float32)).reshape(L, N_DIR, HYENA_ORDER, H_WIDTH)
    max_decay = math.log(DECAY_TARGET) / FAST_DECAY_PCT
    min_decay = math.log(DECAY_TARGET) / SLOW_DECAY_PCT
    deltas = jnp.linspace(min_decay, max_decay, H_WIDTH, dtype=jnp.float32)
    window = jnp.exp(-t[:, :, None, None] * jnp.abs(deltas))
    return h * window

def two_sided_fft_conv(u, k_fwd, k_bwd, bias):
    S = u.shape[1]
    kern = jnp.concatenate([k_fwd, jnp.zeros_like(k_fwd[:1]), k_bwd[:0:-1]], axis=0)
    K = jnp.fft.rfft(kern, axis=0)
    U = jnp.fft.rfft(u, n=2 * S, axis=1)
    y = jnp.fft.irfft(U * K[None], n=2 * S, axis=1)[:, :S]
    return y + u * bias

def group_rms(u, n_groups, w):
    B, S, C = u.shape
    ug = u.reshape(B, S, n_groups, C // n_groups)
    ug = ug * lax.rsqrt(jnp.mean(ug * ug, axis=-1, keepdims=True) + EPS)
    return ug.reshape(B, S, C) * w.astype(jnp.float32)

def first_inputs(seed: int = 0) -> dict:
    key = jax.random.key(seed)
    ks = jax.random.split(key, 32)
    f32 = jnp.float32
    nrm = lambda k, shape, scale: jax.random.normal(k, shape, f32) * scale
    gain = lambda k, n: 1.0 + 0.05 * jax.random.normal(k, (n,), f32)
    i_bias = nrm(ks[6], (M_HEADS,), 0.1)
    f_bias = jnp.linspace(3.0, 6.0, M_HEADS, dtype=f32) + nrm(ks[7], (M_HEADS,), 0.1)
    i_bias_b = nrm(ks[8], (M_HEADS,), 0.1)
    f_bias_b = jnp.linspace(3.0, 6.0, M_HEADS, dtype=f32) + nrm(ks[9], (M_HEADS,), 0.1)
    return {
        "x": jax.random.normal(ks[0], (BATCH, SEQ, D_MODEL), f32),
        "norm_mix_pre": gain(ks[1], D_MODEL),
        "norm_mix_post": gain(ks[2], D_MODEL),
        "norm_mlp_pre": gain(ks[3], D_MODEL),
        "norm_mlp_post": gain(ks[4], D_MODEL),
        "w_in": nrm(ks[5], (D_MODEL, N_IN), D_MODEL ** -0.5),
        "b_gates": jnp.concatenate([i_bias, f_bias, i_bias_b, f_bias_b]),
        "conv_w": nrm(ks[10], (3, N_CONV), 3 ** -0.5),
        "conv_b": nrm(ks[11], (N_CONV,), 0.02),
        "mlstm_norm_w": gain(ks[12], M_WIDTH),
        "hyena_norm_w": gain(ks[13], H_WIDTH),
        "filt_w1": nrm(ks[14], (FILTER_EMB, FILTER_HIDDEN), FILTER_EMB ** -0.5),
        "filt_b1": nrm(ks[15], (FILTER_HIDDEN,), 0.02),
        "filt_w2": nrm(ks[16], (FILTER_HIDDEN, FILTER_HIDDEN), FILTER_HIDDEN ** -0.5),
        "filt_b2": nrm(ks[17], (FILTER_HIDDEN,), 0.02),
        "filt_w3": nrm(ks[18], (FILTER_HIDDEN, FILTER_HIDDEN), FILTER_HIDDEN ** -0.5),
        "filt_b3": nrm(ks[19], (FILTER_HIDDEN,), 0.02),
        "filt_w4": nrm(ks[20], (FILTER_HIDDEN, N_DIR * HYENA_ORDER * H_WIDTH), FILTER_HIDDEN ** -0.5),
        "filt_freq": 1.0 + 0.05 * jax.random.normal(ks[21], (N_SIN, FILTER_HIDDEN), f32),
        "filt_bias": nrm(ks[22], (HYENA_ORDER, H_WIDTH), 0.1),
        "w_out": nrm(ks[23], (D_INNER, D_MODEL), D_INNER ** -0.5),
        "w_mlp_in": nrm(ks[24], (D_MODEL, D_FF), D_MODEL ** -0.5),
        "w_mlp_out": nrm(ks[25], (D_FF, D_MODEL), D_FF ** -0.5),
    }

def first_block(x, norm_mix_pre, norm_mix_post, norm_mlp_pre, norm_mlp_post, w_in, b_gates,
              conv_w, conv_b, mlstm_norm_w, hyena_norm_w, filt_w1, filt_b1, filt_w2, filt_b2,
              filt_w3, filt_b3, filt_w4, filt_freq, filt_bias, w_out, w_mlp_in, w_mlp_out):
    B, S, _ = x.shape
    f32 = jnp.float32
    for _layer in range(DEPTH):
        hn = rms_norm(x, norm_mix_pre)
        proj = (hn @ w_in).astype(f32)
        cv = short_conv3(proj[..., :N_CONV], conv_w.astype(f32), conv_b.astype(f32))

        def heads(u):
            return u.reshape(B, S, M_HEADS, M_HEAD_DIM).transpose(0, 2, 1, 3)
        q = heads(jax.nn.silu(cv[..., OFF_MQ:OFF_MQ + M_WIDTH]))
        k = heads(jax.nn.silu(cv[..., OFF_MK:OFF_MK + M_WIDTH])) * (M_HEAD_DIM ** -0.5)
        v = heads(proj[..., OFF_MV:OFF_MV + M_WIDTH])
        o_gate = jax.nn.sigmoid(proj[..., OFF_MO:OFF_MO + M_WIDTH])
        gates = (proj[..., OFF_GATE:OFF_GATE + N_GATE] + b_gates.astype(f32)).transpose(0, 2, 1)
        gates = gates.reshape(B, 2 * N_DIR, M_HEADS, S)
        h_fwd = mlstm_chunkwise(q, k, v, gates[:, 0], jax.nn.log_sigmoid(gates[:, 1]))
        flip = lambda u: jnp.flip(u, axis=2)
        h_bwd = flip(mlstm_chunkwise(flip(q), flip(k), flip(v), flip(gates[:, 2]),
                                     flip(jax.nn.log_sigmoid(gates[:, 3]))))
        h_m = (h_fwd + h_bwd).transpose(0, 2, 1, 3).reshape(B, S, M_WIDTH) * o_gate
        y_m = group_rms(h_m, M_HEADS, mlstm_norm_w)

        filt = hyena_filters(S, filt_w1, filt_b1, filt_w2, filt_b2, filt_w3, filt_b3,
                             filt_w4, filt_freq)
        fb = filt_bias.astype(f32)
        z = cv[..., OFF_HV:OFF_HV + H_WIDTH]
        z = cv[..., OFF_HX1:OFF_HX1 + H_WIDTH] * two_sided_fft_conv(z, filt[:, 0, 0], filt[:, 1, 0], fb[0])
        z = cv[..., OFF_HX2:OFF_HX2 + H_WIDTH] * two_sided_fft_conv(z, filt[:, 0, 1], filt[:, 1, 1], fb[1])
        y_h = group_rms(z, H_GROUPS, hyena_norm_w)

        mix = jnp.concatenate([y_m, y_h], axis=-1).astype(x.dtype) @ w_out
        x = x + rms_norm(mix, norm_mix_post)

        hm = rms_norm(x, norm_mlp_pre)
        ff = jnp.square(jax.nn.relu(hm @ w_mlp_in)) @ w_mlp_out
        x = x + rms_norm(ff, norm_mlp_post)
    return x


CHUNK_2 = 64
HEAD_DIM = 64
POOL_WINDOWS = (2, 4, 8, 16)
POOL_WIDTH = D_MODEL // 4
POOL_GROUP = POOL_WIDTH // len(POOL_WINDOWS)
DSA_WIDTH = 3 * D_MODEL // 8
DSA_HEADS = DSA_WIDTH // HEAD_DIM
FOX_WIDTH = 3 * D_MODEL // 8
FOX_HEADS = FOX_WIDTH // HEAD_DIM
MIX_WIDTH = POOL_WIDTH + DSA_WIDTH + FOX_WIDTH
IDX_HEADS = 8
IDX_DIM = 32
DSA_TOPK_MAX = 256
DSA_QBLOCK = 32
FOX_QBLOCK = 128
RMS_EPS = 1e-6
IN_SIZES = (
    POOL_WIDTH, POOL_WIDTH,
    DSA_WIDTH, DSA_WIDTH, DSA_WIDTH, DSA_WIDTH,
    IDX_HEADS * IDX_DIM, IDX_DIM, IDX_HEADS,
    FOX_WIDTH, FOX_WIDTH, FOX_WIDTH, FOX_WIDTH,
    FOX_HEADS,
)
IN_COLS = 2 * POOL_WIDTH + 4 * DSA_WIDTH + IDX_HEADS * IDX_DIM + IDX_DIM + IDX_HEADS + 4 * FOX_WIDTH + FOX_HEADS


def rmsnorm(x, g):
    xf = x.astype(jnp.float32)
    y = xf * lax.rsqrt(jnp.mean(xf * xf, axis=-1, keepdims=True) + RMS_EPS)
    return (y * g.astype(jnp.float32)).astype(x.dtype)

def split_columns(z):
    parts = []
    off = 0
    for n in IN_SIZES:
        parts.append(z[..., off:off + n])
        off += n
    return parts

def pool_mixer(v, w_grp, scale):
    B, L, _ = v.shape
    vf = v.astype(jnp.float32)
    cs = jnp.pad(jnp.cumsum(vf, axis=1), ((0, 0), (1, 0), (0, 0)))
    t = jnp.arange(L)
    outs = []
    for gi, w in enumerate(POOL_WINDOWS):
        sl = slice(gi * POOL_GROUP, (gi + 1) * POOL_GROUP)
        c = cs[:, :, sl]
        lo = jnp.maximum(t + 1 - w, 0)
        win_sum = c[:, t + 1] - c[:, lo]
        cnt = (t + 1 - lo).astype(jnp.float32)[None, :, None]
        outs.append(win_sum / cnt - vf[:, :, sl])
    p = jnp.stack(outs, axis=2).astype(v.dtype)
    y = jnp.einsum('blgc,gcd->blgd', p, w_grp).reshape(B, L, POOL_WIDTH)
    return y * scale

def dsa_mixer(q, k, v, iq, ik, iw, topk):
    B, L, H, dh = q.shape
    n_blocks = L // DSA_QBLOCK
    key_pos = jnp.arange(L)
    sm_scale = 1.0 / math.sqrt(dh)
    gather = jax.vmap(lambda arr, idx: arr[idx])

    def block(bi):
        start = bi * DSA_QBLOCK
        qb = lax.dynamic_slice_in_dim(q, start, DSA_QBLOCK, axis=1)
        iqb = lax.dynamic_slice_in_dim(iq, start, DSA_QBLOCK, axis=1)
        iwb = lax.dynamic_slice_in_dim(iw, start, DSA_QBLOCK, axis=1)
        qpos = start + jnp.arange(DSA_QBLOCK)
        limit = (qpos // CHUNK_2 + 1) * CHUNK_2
        dots = jnp.einsum('bqhd,bsd->bqhs', iqb, ik).astype(jnp.float32)
        score = jnp.einsum('bqh,bqhs->bqs', iwb.astype(jnp.float32), jax.nn.relu(dots))
        admissible = key_pos[None, None, :] < limit[None, :, None]
        score = jnp.where(admissible, score, -jnp.inf)
        _, sel = lax.top_k(score, topk)
        valid = sel < limit[None, :, None]
        kg = gather(k, sel)
        vg = gather(v, sel)
        s = jnp.einsum('bqhd,bqkhd->bqhk', qb, kg).astype(jnp.float32) * sm_scale
        s = jnp.where(valid[:, :, None, :], s, -jnp.inf)
        p = jax.nn.softmax(s, axis=-1).astype(v.dtype)
        return jnp.einsum('bqhk,bqkhd->bqhd', p, vg)

    o = lax.map(block, jnp.arange(n_blocks))
    return jnp.transpose(o, (1, 0, 2, 3, 4)).reshape(B, L, H, dh)

def fox_mixer(q, k, v, log_f):
    B, L, H, dh = q.shape
    sm_scale = 1.0 / math.sqrt(dh)
    F = jnp.transpose(jnp.cumsum(log_f, axis=1), (0, 2, 1))
    outs = []
    for bi in range(L // FOX_QBLOCK):
        s0 = bi * FOX_QBLOCK
        e = s0 + FOX_QBLOCK
        s = jnp.einsum('bqhd,bkhd->bhqk', q[:, s0:e], k[:, :e]).astype(jnp.float32) * sm_scale
        s = s + F[:, :, s0:e, None] - F[:, :, None, :e]
        mask = jnp.arange(s0, e)[:, None] >= jnp.arange(e)[None, :]
        s = jnp.where(mask[None, None], s, -jnp.inf)
        p = jax.nn.softmax(s, axis=-1).astype(v.dtype)
        outs.append(jnp.einsum('bhqk,bkhd->bqhd', p, v[:, :e]))
    return jnp.concatenate(outs, axis=1)

def second_inputs(seed: int = 0) -> dict:
    key = jax.random.key(seed)
    ks = jax.random.split(key, 9)
    x = jax.random.normal(ks[0], (BATCH, SEQ, D_MODEL), jnp.float32)
    w_in = jax.random.normal(ks[1], (DEPTH, D_MODEL, IN_COLS), jnp.float32) * D_MODEL ** -0.5
    norm_g = 1.0 + 0.02 * jax.random.normal(ks[2], (DEPTH, D_MODEL), jnp.float32)
    pool_w = jax.random.normal(ks[3], (DEPTH, len(POOL_WINDOWS), POOL_GROUP, POOL_GROUP), jnp.float32) * POOL_GROUP ** -0.5
    pool_scale = 1.0 + 0.1 * jax.random.normal(ks[4], (DEPTH, POOL_WIDTH), jnp.float32)
    fox_bf = 3.0 + 0.5 * jax.random.normal(ks[5], (DEPTH, FOX_HEADS), jnp.float32)
    w_out = jax.random.normal(ks[6], (DEPTH, MIX_WIDTH, D_MODEL), jnp.float32) * MIX_WIDTH ** -0.5
    final_g = 1.0 + 0.02 * jax.random.normal(ks[7], (D_MODEL,), jnp.float32)
    return {'x': x, 'w_in': w_in, 'norm_g': norm_g, 'pool_w': pool_w, 'pool_scale': pool_scale,
            'fox_bf': fox_bf, 'w_out': w_out, 'final_g': final_g}

def second_block(x, w_in, norm_g, pool_w, pool_scale, fox_bf, w_out, final_g):
    B, L, _ = x.shape
    topk = min(DSA_TOPK_MAX, L // 4)
    idx_w_scale = IDX_HEADS ** -0.5
    for layer in range(DEPTH):
        h = rmsnorm(x, norm_g[layer])
        z = jnp.einsum('bld,dc->blc', h, w_in[layer])
        (pv, pg, dq, dk, dv, dg, iq, ik, iw, fq, fk, fv, fg, ff) = split_columns(z)
        a_out = pool_mixer(pv, pool_w[layer], pool_scale[layer]) * jax.nn.silu(pg)
        b_o = dsa_mixer(dq.reshape(B, L, DSA_HEADS, HEAD_DIM), dk.reshape(B, L, DSA_HEADS, HEAD_DIM),
                        dv.reshape(B, L, DSA_HEADS, HEAD_DIM), iq.reshape(B, L, IDX_HEADS, IDX_DIM),
                        ik, iw * idx_w_scale, topk)
        b_out = b_o.reshape(B, L, DSA_WIDTH) * jax.nn.silu(dg)
        log_f = jax.nn.log_sigmoid(ff.astype(jnp.float32) + fox_bf[layer].astype(jnp.float32))
        c_o = fox_mixer(fq.reshape(B, L, FOX_HEADS, HEAD_DIM), fk.reshape(B, L, FOX_HEADS, HEAD_DIM),
                        fv.reshape(B, L, FOX_HEADS, HEAD_DIM), log_f)
        c_out = c_o.reshape(B, L, FOX_WIDTH) * jax.nn.silu(fg)
        mixed = jnp.concatenate([a_out, b_out, c_out], axis=-1)
        x = x + jnp.einsum('blc,cd->bld', mixed, w_out[layer])
    return rmsnorm(x, final_g)


def setup_inputs(seed=0):
    out = dict(first_inputs(seed))
    for name, value in second_inputs(seed + 1).items():
        if name != "x":
            out[name + "_2"] = value
    return out


def reference(
    x, norm_mix_pre, norm_mix_post, norm_mlp_pre, norm_mlp_post, w_in, b_gates, conv_w, conv_b,
    mlstm_norm_w, hyena_norm_w, filt_w1, filt_b1, filt_w2, filt_b2, filt_w3, filt_b3, filt_w4,
    filt_freq, filt_bias, w_out, w_mlp_in, w_mlp_out, w_in_2, norm_g_2, pool_w_2, pool_scale_2,
    fox_bf_2, w_out_2, final_g_2,
):
    x = first_block(
        x, norm_mix_pre, norm_mix_post, norm_mlp_pre, norm_mlp_post, w_in, b_gates, conv_w,
        conv_b, mlstm_norm_w, hyena_norm_w, filt_w1, filt_b1, filt_w2, filt_b2, filt_w3,
        filt_b3, filt_w4, filt_freq, filt_bias, w_out, w_mlp_in, w_mlp_out,
    )
    return second_block(
        x, w_in_2, norm_g_2, pool_w_2, pool_scale_2, fox_bf_2, w_out_2, final_g_2,
    )


_drawn_inputs = setup_inputs


def setup_inputs(seed=0):
    import zlib

    import numpy as np

    out = dict(_drawn_inputs(seed))
    spreads = {}
    factors = {'norm_g_2': 8.0, 'pool_scale_2': 4.036, 'fox_bf_2': 2.813, 'final_g_2': 2.805}
    for name, (base, spread) in spreads.items():
        noise = np.random.default_rng([zlib.crc32(name.encode()), seed]).standard_normal(out[name].shape)
        drawn = base * np.exp(spread * noise) if base else spread * noise
        out[name] = __import__('jax').numpy.asarray(drawn.astype(out[name].dtype))
    for name, factor in factors.items():
        out[name] = (out[name] * factor).astype(out[name].dtype)
    return out
```

```python
from contextlib import ExitStack

import numpy as np

import concourse.bass as bass
from concourse import mybir

F32 = mybir.dt.float32
ALU = mybir.AluOpType
ACT = mybir.ActivationFunctionType
AX_X = mybir.AxisListType.X

P = 128
S = 512
NT = S // P
D = 1024
ND = D // P
HALF = D // 2
MH = 4
ND2 = 2 * MH
NCONV = 5 * HALF
NCT = NCONV // P
OFF_MV, OFF_MO, OFF_GATE = NCONV, NCONV + HALF, NCONV + 2 * HALF
HG = 8
EMB, FHID = 33, 64
DFF = 4 * D
NFF = DFF // P
EPS = 1e-6
HD = 64
AW = 384
AH = AW // HD
PW = 256
IH, ID = 8, 32
TOPK = 128
OFF_DQ, OFF_DK, OFF_DV, OFF_DG = 512, 896, 1280, 1664
OFF_IQ = 2048
OFF_FQ, OFF_FK, OFF_FV, OFF_FG = 2344, 2728, 3112, 3496
NIN2 = 3886
GF = 32
NEG = -1e30
LOWEST = -3e38
TAKEN = -3.3e38
MAGIC = 12582912.0
TWO_PI_HI = 6.28125
TWO_PI_LO = 2 * np.pi - 6.28125
PI = float(np.nextafter(np.float32(np.pi), np.float32(0)))

ROW_CONV_W, ROW_CONV_B = 0, 3 * NCT
ROW_MIX_PRE = ROW_CONV_B + NCT
ROW_MLP_PRE = ROW_MIX_PRE + ND
ROW_MLSTM_W = ROW_MLP_PRE + ND
ROW_HYENA_W = ROW_MLSTM_W + MH
ROW_NORM2 = ROW_HYENA_W + MH
ROW_POOL = ROW_NORM2 + ND
N_ROWS = ROW_POOL + PW // P

NSLOT = 3


def weight_groups():
    def ch(n0, cols):
        return [(("cv", n0 + j), "ch", P * j, P) for j in range(cols // P)]

    def tok(name, c0, n):
        return [((name, t), f"tok{t}", c0, n) for t in range(NT)]

    def many(name, cols, c0=0):
        return [((name, j), "ch", c0 + P * j, P) for j in range(cols // P)]

    return {
        "hv": ("w_in", 1024, 512, ch(8, 512)),
        "hx1": ("w_in", 1536, 512, ch(12, 512)),
        "hx2": ("w_in", 2048, 512, ch(16, 512)),
        "mq": ("w_in", 0, 512, ch(0, 512)),
        "mk": ("w_in", 512, 512, ch(4, 512)),
        "mv": ("w_in", OFF_MV, 512, tok("mv", 0, 512)),
        "mo": ("w_in", OFF_MO, 512, tok("mo", 0, 512)),
        "out0": ("w_out", 0, 512, tok("mx00", 0, 512)),
        "out1": ("w_out", 512, 512, tok("mx01", 0, 512)),
        "index": ("w_in_2", OFF_IQ, 296, many("iq", IH * ID) + [(("ik", 0), "rep", 256, P)] + tok("iw", 288, IH)),
        "fq": ("w_in_2", OFF_FQ, AW, many("fq", AW)),
        "fk": ("w_in_2", OFF_FK, AW, many("fk", AW)),
        "fg": ("w_in_2", OFF_FG, AW + AH, [(("ff", 0), "ch", AW, AH)] + tok("fg", 0, AW)),
        "fv": ("w_in_2", OFF_FV, AW, tok("fv", 0, AW)),
        "dq": ("w_in_2", OFF_DQ, AW, many("dq", AW)),
        "dk": ("w_in_2", OFF_DK, AW, many("dk", AW)),
        "dv": ("w_in_2", OFF_DV, AW, tok("dv", 0, AW)),
        "dg": ("w_in_2", OFF_DG, AW, tok("dg", 0, AW)),
        "pool": ("w_in_2", 0, 512, many("pv", PW) + many("pg", PW, PW)),
        "fin0": ("w_out_2", 0, 512, tok("fx0", 0, 512)),
        "fin1": ("w_out_2", 512, 512, tok("fx1", 0, 512)),
    }


GROUPS = weight_groups()
GROUP_ORDER = ["hv", "hx1", "hx2", "mq", "mk", "mv", "mo", "out0", "out1", "index", "fq", "fk", "fg", "fv",
               "dq", "dk", "dv", "pool", "dg", "fin0", "fin1"]
BETWEEN = {0: "dq", 1: "dk", 3: "dv", 5: "pool", 8: "dg"}
LAG = 2
HEADS = [("f", h) for h in range(AH)] + [("d", h) for h in range(AH)]


def psum_order():
    def group(g):
        return [name for name, *_ in GROUPS[g][3]]

    def turned(lo, hi):
        return [("cvT", n) for n in range(lo, hi)]

    def norm(s):
        return [("nT", s, t, half) for t in range(NT) for half in range(2)]

    o = [("cols",), ("fcols",), ("f", 0)] + norm(0)[:4] + [("f", 1)] + norm(0)[4:] + [("gate",), ("f", 2)] + group("hv")
    o += [("ft", q, t, d) for q in range(2) for t in range(NT) for d in range(2)]
    o += [("K", q, c, f) for q in range(2) for c in range(2) for f in range(NT)]
    o += group("hx1") + turned(8, 12) + group("hx2") + turned(12, 16) + group("mq") + turned(16, 20)
    o += group("mk") + group("mv") + group("mo")
    o += [(c, 0, f) for f in range(NT) for c in "US"] + [("y", 0, t) for t in range(NT)]
    o += [("gcol",), ("decay",)]
    for h in range(MH):
        o += [("kt", h), ("s", h)]
        for d in range(2):
            o += [("bc", h, d), ("up", h, d)]
        o += conv2_chunk(h)
        for d in range(2):
            o += [("in", h, d), ("nd", h, d, 0), ("nd", h, d, 1)]
    o += [("yT", j) for j in range(MH, ND)] + [("yT", j) for j in range(MH)]
    o += group("out0") + group("out1") + norm(1)
    o += [("ff1", f) for f in range(NFF)] + [("ff2", n) for n in range(2 * NT)]
    o += norm(2) + group("index")
    o += [("ix", i, h) for i in range(1, NT) for h in range(IH)]
    for g in ("fq", "fk", "fg", "fv"):
        o += group(g)
    for n, (kind, h) in enumerate(HEADS):
        o += scores_of(kind, h)
        if n >= LAG:
            o += values_of(*HEADS[n - LAG])
        if n in BETWEEN:
            o += group(BETWEEN[n])
    for head in HEADS[-LAG:]:
        o += values_of(*head)
    o += [("mix_pool", j) for j in range(PW // P)] + [("mT", j) for j in (3, 4, 5)]
    o += group("fin0") + [("mT", j) for j in (0, 1, 2)] + group("fin1")
    return o


def conv2_chunk(h):
    if h < 2:
        return [(c, 1, f) for f in (2 * h, 2 * h + 1) for c in "US"]
    return [("y", 1, t) for t in (2 * h - 4, 2 * h - 3)]


def scores_of(kind, h):
    return ([("nF", h)] if kind == "f" else []) + [(kind + "s", h, i) for i in range(NT)]


def values_of(kind, h):
    return [(kind + "T", h, i) for i in range(NT)] + [(kind + "o", h)]


def bank_table():
    order = psum_order()
    assert len(set(order)) == len(order)
    return {name: (n % 8, n // 8) for n, name in enumerate(order)}


def constants():
    f32 = np.float32
    n = np.arange(S)
    odd = 2 * n[None, :] + 1
    ang = np.pi * ((odd * n[:, None]) % (4 * S)) / (2 * S)
    sym = np.pi * ((odd * (2 * n[:, None] + 1)) % (8 * S)) / (4 * S)
    bands = (EMB - 1) // 2
    t = np.linspace(0.0, 1.0, S, dtype=f32)[:, None]
    turn = (f32(2.0 * np.pi) * np.arange(S, dtype=f32)[:, None] / f32(S)).astype(f32)
    fr = np.linspace(1e-4, bands - 1, bands, dtype=f32)[None, :]
    z = np.concatenate([t, np.cos(fr * turn), -np.sin(fr * turn)], axis=-1).astype(f32)
    lo, hi = np.log(1e-2) / 1.5, np.log(1e-2) / 0.3
    deltas = np.abs(np.linspace(lo, hi, HALF, dtype=f32))
    window = np.exp(-t * deltas[None, :]).astype(f32)
    window_b = window[:P].copy()
    window_b[0] = 0
    i, j = np.arange(P)[:, None], np.arange(P)[None, :]
    masks = np.stack([np.eye(P), i <= j, i >= j, np.where(j <= i, 0.0, NEG),
                      np.where((i < HD) & (j >= HD), NEG, 0.0)]).astype(f32)
    count = np.minimum(np.arange(S) + 1, np.array([2, 4, 8, 16])[:, None])
    inv_count = (1.0 / np.repeat(count, HD, axis=0)).astype(f32)
    rows = np.zeros((ND2, S + ND2 + 2), f32)
    rows[:, 0:S] = np.arange(S) % P != 0
    rows[:, S:S + ND2] = np.eye(ND2)
    rows[:MH, -2] = 1
    rows[MH:, -1] = 1
    return {
        "c_kernel_dft": np.stack([np.cos(ang), np.sin(ang)]).astype(f32),
        "c_signal_dft": np.stack([np.cos(sym), np.sin(sym)]).astype(f32),
        "c_z": np.ascontiguousarray(z.T), "c_window": window, "c_window_b": window_b,
        "c_masks": masks, "c_inv_count": inv_count, "c_rows": rows,
    }


def build_program(nc, a, out):
    BANK = bank_table()
    with ExitStack() as ctx:
        def sb(name, shape):
            return ctx.enter_context(nc.sbuf_tensor(name, shape, F32))

        def sem(name):
            return ctx.enter_context(nc.semaphore(name))

        slots = sb("weight_slots", [P, NSLOT, 4, 512])
        x = sb("x", [P, NT, D])
        xT = sb("xT", [P, ND, S])
        masks = sb("masks", [P, 5, P])
        ident, keep_f, keep_b, causal, chunk_bias = (masks[:, n, :] for n in range(5))
        colv = sb("colv", [P, N_ROWS])
        fcol = sb("fcol", [FHID, 6])
        row_bc = sb("row_bc", [P, D])
        rows_c = sb("rows_c", [ND2, S + ND2 + 2])
        chunk_reset = rows_c[:, 0:S]
        ident8 = rows_c[:, S:S + ND2]
        is_f, is_b = rows_c[:, S + ND2:S + ND2 + 1], rows_c[:, S + ND2 + 1:]
        gbias = sb("gbias", [ND2, 2])
        fbias = sb("fbias", [AH, 1])
        ones8 = sb("ones8", [ND2, P])
        one_col = sb("one_col", [P, 1])
        minus_half = sb("minus_half", [P, NT * HG])
        sumsq = sb("sumsq", [P, 6, 2, NT])
        rstd = sb("rstd", [P, 6, NT])
        sumsq_h, rstd_h = sb("sumsq_h", [P, NT * HG]), sb("rstd_h", [P, NT * HG])
        sumsq_m, rstd_m = sb("sumsq_m", [P, NT * MH]), sb("rstd_m", [P, NT * MH])
        gcol = sb("gcol", [P, 4, NT, ND2])
        decay = sb("decay", [P, ND2, NT])
        m_start = sb("m_start", [ND2, NT + 1])
        dec8 = sb("dec8", [ND2, NT])
        dblk = sb("dblk", [ND2, ND2, NT])
        den = sb("den", [P, 2, NT])
        gate_w = sb("gate_w", [P, ND, 16])
        gate_w2 = sb("gate_w2", [P, ND, GF + ND2])
        iw = sb("iw", [P, NT, IH])
        top8 = sb("top8", [P, 8])
        smax = sb("smax", [P, 3, NT])
        ssum = sb("ssum", [P, 3, NT])
        pool_w = sb("pool_w", [P, 2, P])
        main_kb = 136.25
        main = sb("main", [P, int(main_kb * 256)])

        def at(kb, *shape, parts=P):
            n = int(np.prod(shape))
            o = int(round(kb * 256))
            assert o + n <= main_kb * 256, (kb, shape)
            v = main[0:parts, o:o + n]
            if len(shape) == 2:
                v = v.rearrange("p (a b) -> p a b", b=shape[1])
            if len(shape) == 3:
                v = v.rearrange("p (a b c) -> p a b c", b=shape[1], c=shape[2])
            return v

        spec = [[at(16 * q + 8 * c, NT, S) for c in range(2)] for q in range(2)]
        sdft = at(32, 2, NT, S)
        tap_sum = [at(48, NT, S), at(64, NT, S)]
        tap_dif = [at(56, NT, S), at(72, NT, S)]
        sig = [at(48, NT, S), at(56, NT, S), at(64, NT, S)]
        kdft = at(80, 2, NT, S)
        window = at(96, NT, S)
        filt_w4 = at(104, 2 * S * 2, parts=FHID)
        xn_first = at(112.25, NT, D)
        window_b = at(128.25, S)
        zT = at(130.25, S, parts=EMB)
        hidden = at(132.25, S, parts=FHID)
        filt_w = [at(134.25, FHID, parts=EMB), at(134.5, FHID, parts=FHID), at(134.75, FHID, parts=FHID)]
        colrows = at(135, P, parts=N_ROWS)
        frows = at(135.5, FHID, parts=6)
        sin_arg, sin_turn = at(48, S, parts=FHID), at(50, S, parts=FHID)
        taps_b = [at(28 + 2 * n, S) for n in range(2)]
        conv_buf = [at(112.25 + 2 * n, S) for n in range(8)]
        conv = {n: conv_buf[n % 8 if n >= 8 else (n + 4) % 8] for n in range(NCT)}
        prod = [[at(128.25 + 4 * n + 2 * c, S) for c in range(2)] for n in range(2)]
        qT, kT = at(80, MH, S), at(88, MH, S)
        ktok = at(96, MH, NT, P)
        v1 = at(104, NT, MH * (P + 1)).rearrange("p t (h c) -> p t h c", h=MH)
        o_gate = x[:, 0:2, :].rearrange("p a b -> p (a b)").rearrange("p (t c) -> p t c", t=NT)
        hm = at(0, NT, HALF)
        x_rows = x[0:ND2, 2:4, :].rearrange("p a b -> p (a b)").rearrange("p (t c) -> p t c", c=S)
        r_e, r_lf = (at(72 + 2 * n, S, parts=ND2) for n in range(2))
        r_den, r_in, r_w, r_m = (at(8 + 2 * n, S, parts=ND2) for n in range(4))
        r_a, r_b, r_i, r_f = (x_rows[:, n, :] for n in range(4))
        s_mask = [[at(48 + 4 * n + 2 * d, NT, P) for d in range(2)] for n in range(2)]
        wts = [at(112.25 + 2 * n, NT, P) for n in range(2)]
        kw = [[at(116.25 + 1.5 * d + 0.5 * c, P) for c in range(3)] for d in range(2)]
        state = [at(119.25 + 1.75 * d, 3, P + 1) for d in range(2)]
        inter = at(122.75, NT, P + 1)
        nd = at(125, NT, P + 1)
        sq_h, sq_m = at(16, NT, HALF), at(24, NT, HALF)
        act = at(0, NFF, S)
        mlp_slot = [at(64 + 16 * n, 4096) for n in range(2)]
        xn_mlp = at(96, NT, D)
        mixed = at(112, NT, D)
        relu = [at(128 + 2 * n, S) for n in range(4)]
        iqT, ikT = at(0, 2, S), at(4, S)
        pvT, pgT = at(6, 2, S), at(10, 2, S)
        qkT = {"fq": at(14, 3, S), "fk": at(20, 3, S), "dq": at(26, 3, S), "dk": at(32, 3, S)}
        vtok = {"f": at(38, NT, AW), "d": at(50, NT, AW)}
        gtok = {"f": at(44, NT, AW), "d": at(56, NT, AW)}
        score, work = at(62, 3, S), at(68, 3, S)
        prob = [at(kb, 10 * P) for kb in (74, 79, 110)]
        probT = [at(84 + 5 * n, 10, P) for n in range(2)]
        nf_bc = [at(94 + 2 * n, S) for n in range(2)]
        otok = {"f": at(98, NT, AW), "d": at(104, NT, AW)}
        rdot = [at(112 + 2 * n, S) for n in range(2)]
        f_f, f_a, f_n = (at(116 + 2 * n, S, parts=AH) for n in range(3))
        win = [at(122, S), at(124, S), at(126, S), at(132, S), at(134, S)]
        wik = at(128, ND, P)
        inv_count = at(128, 2, S)

        ps = [ctx.enter_context(nc.psum_tensor(f"bank{n}", [P, 512], F32)) for n in range(8)]

        bank_full = [sem(f"bank_full{n}") for n in range(8)]
        bank_free = [sem(f"bank_free{n}") for n in range(8)]
        slot_loaded = [sem(f"slot_loaded{n}") for n in range(NSLOT)]
        mlp_loaded = [sem(f"mlp_loaded{n}") for n in range(2)]
        (ld_cols, ld_masks, ld_filter, ld_window, ld_kdft, ld_sdft, ld_rows, ld_gate, ld_fb, ld_mix_post,
         ld_mlp_post, ld_final, ld_pool, ld_count, stored) = (sem("ld_" + n) for n in (
             "cols masks filter window kdft sdft rows gate fb mix_post mlp_post final pool count stored").split())
        dve_step, act_step, pool_step = sem("dve_step"), sem("act_step"), sem("pool_step")
        consts_set, v1_ones = sem("consts_set"), sem("v1_ones")
        ld_x = [sem(f"ld_x{t}") for t in range(NT)]
        sumsq_ready = [sem(f"sumsq_ready{s}") for s in range(6)]
        rstd_ready = [sem(f"rstd_ready{s}") for s in range(6)]
        rstd_h_ready, rstd_m_ready = sem("rstd_h_ready"), sem("rstd_m_ready")
        mix_ready, x_ready, xn_ready = sem("mix_ready"), sem("x_ready"), sem("xn_ready")
        sin_arg_ready, hidden_ready, taps_ready = (sem(n) for n in "sin_arg_ready hidden_ready taps_ready".split())
        conv_bias_ready, q_ready, k_silu, k_ready = (sem(n) for n in "conv_bias_ready q_ready k_silu k_ready".split())
        prod_ready, spec_ready, skip_ready, long_ready = (
            sem(n) for n in "prod_ready spec_ready skip_ready long_ready".split())
        gate_w_ready, gate_abs, softplus_ready, exp_args, exps_ready, rows_ready, dblk_ready = (
            sem(n) for n in "gate_w_ready gate_abs softplus_ready exp_args exps_ready rows_ready dblk_ready".split())
        kw_ready, wts_ready, p_ready, h_ready = (sem(n) for n in "kw_ready wts_ready p_ready h_ready".split())
        sq_ready, gsum_ready, gated, yn_ready = (sem(n) for n in "sq_ready gsum_ready gated yn_ready".split())
        relu_ready, act_ready, act_used = sem("relu_ready"), sem("act_ready"), sem("act_used")
        wik_ready, rdot_used = sem("wik_ready"), sem("rdot_used")
        sel_ready = sem("sel_ready")
        fgate_abs, fsoft_ready, nf_ready = sem("fgate_abs"), sem("fsoft_ready"), sem("nf_ready")
        smax_ready, prob_ready, og_ready = (sem(n) for n in "smax_ready prob_ready og_ready".split())
        win_ready, pool_w_ready = sem("win_ready"), sem("pool_w_ready")
        out_ready = sem("out_ready")

        def full(eng, name):
            b, k = BANK[name]
            eng.wait_ge(bank_full[b], k + 1)
            return ps[b]

        def free(ins, name):
            return ins.then_inc(bank_free[BANK[name][0]], 1)

        def taken(eng, name):
            b, k = BANK[name]
            eng.wait_ge(bank_free[b], k + 1)

        def stepper(eng, step):
            count = [0]

            def done(ins):
                count[0] += 1
                ins.then_inc(step, 1)
                eng.wait_ge(step, count[0])
            return done

        def scol(row, n=1):
            return colv[:, row:row + n]

        NORMS = {0: (ROW_MIX_PRE, 0, xn_first), 1: (ROW_MLP_PRE, 2, xn_mlp), 2: (ROW_NORM2, 4, mixed)}
        x_tok = a["x"].rearrange("b (t p) d -> p (b t) d", p=P)
        out_tok = out.rearrange("b (t p) d -> p (b t) d", p=P)

        def vec(name, n):
            return a[name].rearrange("(r p) -> r p", p=P) if n else a[name]

        group_at = {g: n for n, g in enumerate(GROUP_ORDER)}
        block = ctx.enter_context(nc.Block())

        @block.sync
        def _(sp):
            def weights(g):
                weight, c0, n, tiles = GROUPS[g]
                src = a[weight] if weight[-2:] != "_2" else a[weight].rearrange("l k n -> (l k) n")
                src = src.rearrange("(k p) n -> p k n", p=P)[:, :, c0:c0 + n]
                for half in range(2):
                    use = 2 * group_at[g] + half
                    if use >= NSLOT:
                        before = GROUPS[GROUP_ORDER[(use - NSLOT) // 2]][3]
                        full(sp, before[0 if (use - NSLOT) % 2 == 0 and g != "fin1" else -1][0])
                    sp.dma_start(slots[:, use % NSLOT, :, 0:n], src[:, 4 * half:4 * half + 4, :])\
                      .then_inc(slot_loaded[use % NSLOT], 16)

            for t in range(NT):
                sp.dma_start(x[:, t, :], x_tok[:, t, :]).then_inc(ld_x[t], 16)
            for name, row in (("conv_b", ROW_CONV_B), ("norm_mix_pre", ROW_MIX_PRE), ("norm_mlp_pre", ROW_MLP_PRE),
                              ("mlstm_norm_w", ROW_MLSTM_W), ("hyena_norm_w", ROW_HYENA_W), ("norm_g_2", ROW_NORM2),
                              ("pool_scale_2", ROW_POOL)):
                src = a[name] if name[-2:] != "_2" else a[name].rearrange("l n -> (l n)")
                src = src.rearrange("(r p) -> r p", p=P)
                sp.dma_start(colrows[row:row + src.shape[0], :], src).then_inc(ld_cols, 16)
            sp.dma_start(colrows[0:3 * NCT, :], a["conv_w"].rearrange("w (r p) -> (w r) p", p=P)).then_inc(ld_cols, 16)
            for n in range(3):
                sp.dma_start(frows[n:n + 1, :], a[f"filt_b{n + 1}"].rearrange("(a n) -> a n", a=1)).then_inc(ld_cols, 16)
            sp.dma_start(frows[3:6, :], a["filt_freq"]).then_inc(ld_cols, 16)
            sp.dma_start(masks[:, :, :], a["c_masks"].rearrange("m p n -> p m n")).then_inc(ld_masks, 16)
            sp.dma_start(zT, a["c_z"]).then_inc(ld_filter, 16)
            for n in range(3):
                sp.dma_start(filt_w[n], a[f"filt_w{n + 1}"]).then_inc(ld_filter, 16)
            sp.dma_start(gate_w[:, :, :], a["w_in"].rearrange("(k p) n -> p k n", p=P)[:, :, OFF_GATE:OFF_GATE + 16])\
              .then_inc(ld_gate, 16)
            weights("hv")
            sp.dma_start(filt_w4, a["filt_w4"]).then_inc(ld_filter, 16)
            sp.dma_start(window, a["c_window"].rearrange("(t p) c -> p t c", p=P)).then_inc(ld_window, 16)
            sp.dma_start(window_b, a["c_window_b"]).then_inc(ld_window, 16)
            for c in range(2):
                sp.dma_start(kdft[:, c], a["c_kernel_dft"][c].rearrange("(t p) f -> p t f", p=P)).then_inc(ld_kdft, 16)
            sp.dma_start(rows_c[:, :], a["c_rows"]).then_inc(ld_rows, 16)
            for kind in range(2):
                for d in range(2):
                    o = (2 * d + kind) * MH
                    sp.dma_start(gbias[d * MH:(d + 1) * MH, kind:kind + 1],
                                 a["b_gates"][o:o + MH].rearrange("(r o) -> r o", o=1)).then_inc(ld_rows, 16)
            sp.dma_start(fbias[:, :], a["fox_bf_2"].rearrange("l (r o) -> (l r) o", o=1)).then_inc(ld_rows, 16)
            for c in range(2):
                sp.dma_start(sdft[:, c], a["c_signal_dft"][c].rearrange("(t p) f -> p t f", p=P)).then_inc(ld_sdft, 16)
            sp.dma_start(row_bc[:, :], a["filt_bias"].rearrange("o c -> (o c)").partition_broadcast(P)).then_inc(ld_fb, 16)

            for g in GROUP_ORDER[1:7]:
                weights(g)
            sp.wait_ge(long_ready, 2 * NT)
            sp.wait_ge(skip_ready, 2 * NT)
            sp.dma_start(row_bc[:, :], a["norm_mix_post"].partition_broadcast(P)).then_inc(ld_mix_post, 16)
            weights("out0")
            sp.wait_ge(gated, NT)
            full(sp, ("bc", MH - 1, 1))
            for t in range(NT):
                sp.dma_start(x[:, t, :], x_tok[:, t, :]).then_inc(ld_x[t], 16)
            weights("out1")
            full(sp, ("yT", MH - 1))
            w_up = a["w_mlp_in"].rearrange("(k p) n -> p k n", p=P)
            first = [BANK[("ff1", f)] for f in range(8)]
            for n in range(2):
                sp.dma_start(mlp_slot[n].rearrange("p (k n) -> p k n", k=ND), w_up[:, :, 512 * n:512 * (n + 1)])\
                  .then_inc(mlp_loaded[n], 16)
            with sp.Fori(1, NFF // 8) as i:
                for n in range(2):
                    b, k = first[4 * n + 3]
                    sp.wait_ge(bank_full[b], k + i)
                    sp.dma_start(mlp_slot[n].rearrange("p (k n) -> p k n", k=ND),
                                 w_up[:, :, bass.ds(i * 1024 + 512 * n, 512)]).then_inc(mlp_loaded[n], 16)
            w_down = a["w_mlp_out"].rearrange("(g f p) n -> g p f n", p=P, f=4)
            for g in range(NFF // 4):
                if g < 2:
                    full(sp, ("ff1", NFF - 5 + 4 * g))
                else:
                    sp.wait_ge(act_used, g - 1)
                sp.dma_start(mlp_slot[g % 2].rearrange("p (f n) -> p f n", f=4), w_down[g]).then_inc(mlp_loaded[g % 2], 16)
            sp.wait_ge(x_ready, 2 * NT)
            sp.dma_start(row_bc[:, :], a["norm_mlp_post"].partition_broadcast(P)).then_inc(ld_mlp_post, 16)
            weights("index")
            weights("fq")
            full(sp, ("iw", NT - 1))
            sp.dma_start(inv_count, a["c_inv_count"].rearrange("(j p) s -> p j s", p=P)).then_inc(ld_count, 16)
            sp.wait_ge(x_ready, 4 * NT)
            sp.dma_start(row_bc[:, :], a["final_g_2"].partition_broadcast(P)).then_inc(ld_final, 16)
            sp.wait_ge(pool_w_ready, 1)
            for j in range(PW // P):
                for n in range(2):
                    sp.dma_start(pool_w[n * HD:(n + 1) * HD, j, n * HD:(n + 1) * HD], a["pool_w_2"][0, 2 * j + n])\
                      .then_inc(ld_pool, 16)
            for g in GROUP_ORDER[group_at["fk"]:]:
                weights(g)
            for t in range(NT):
                sp.wait_ge(out_ready, t + 1)
                sp.dma_start(out_tok[:, t, :], mixed[:, t, :]).then_inc(stored, 16)
            sp.wait_ge(stored, 16 * NT)

        @block.tensor
        def _(pe):
            order = psum_order()
            at_tile = [0]

            def tile(name):
                assert order[at_tile[0]] == name, (order[at_tile[0]], name)
                at_tile[0] += 1
                b, k = BANK[name]
                if k:
                    pe.wait_ge(bank_free[b], k)
                return ps[b]

            def made(ins, name):
                ins.then_inc(bank_full[BANK[name][0]], 1)

            def project(g):
                _, _, _, tiles = GROUPS[g]
                banks = {}
                for half in range(2):
                    use = 2 * group_at[g] + half
                    w = slots[:, use % NSLOT]
                    pe.wait_ge(slot_loaded[use % NSLOT], 16 * (use // NSLOT + 1))
                    for name, kind, c0, n in tiles:
                        if half == 0:
                            banks[name] = tile(name)
                        for kk in range(4):
                            k = 4 * half + kk
                            if kind == "ch":
                                o, l, r = banks[name][0:n, :], w[:, kk, c0:c0 + n], xT[:, k, :]
                            elif kind == "rep":
                                if kk == 0:
                                    pe.wait_ge(wik_ready, half + 1)
                                o, l, r = banks[name][:, :], wik[:, k, :], xT[:, k, :]
                            else:
                                t = int(kind[3:])
                                o, l, r = banks[name][:, 0:n], xT[:, k, t * P:(t + 1) * P], w[:, kk, c0:c0 + n]
                            mm = pe.matmul(o, l, r, start=(k == 0), stop=(k == ND - 1))
                        if half == 1:
                            made(mm, name)

            def turn_norm(s, t):
                pe.wait_ge(xn_ready, NT * s + t + 1)
                xn = NORMS[s][2]
                for half in range(2):
                    o = tile(("nT", s, t, half))
                    for d in range(4):
                        mm = pe.transpose(o[:, d * P:(d + 1) * P], xn[:, t, (4 * half + d) * P:(4 * half + d + 1) * P], ident)
                    made(mm, ("nT", s, t, half))

            def wait_norm(s):
                wait_xT([("nT", s, t, half) for t in range(NT) for half in range(2)])

            def wait_xT(names):
                for n in names:
                    taken(pe, n)

            pe.wait_ge(ld_cols, 16 * 12)
            pe.wait_ge(ld_masks, 16)
            made(pe.transpose(tile(("cols",))[:, 0:N_ROWS], colrows, ident[0:N_ROWS, 0:N_ROWS]), ("cols",))
            made(pe.transpose(tile(("fcols",))[0:FHID, 0:6], frows, ident[0:6, 0:6]), ("fcols",))
            pe.wait_ge(ld_filter, 16 * 5)
            made(pe.matmul(tile(("f", 0))[0:FHID, :], filt_w[0], zT, start=True, stop=True), ("f", 0))
            for n in (1, 2):
                turn_norm(0, 2 * n - 2)
                turn_norm(0, 2 * n - 1)
                if n == 2:
                    wait_norm(0)
                    pe.wait_ge(gate_w_ready, 3)
                    o = tile(("gate",))
                    for k in range(ND):
                        mm = pe.matmul(o[0:GF + ND2, :], gate_w2[:, k, :], xT[:, k, :], start=(k == 0), stop=(k == ND - 1))
                    made(mm, ("gate",))
                pe.wait_ge(hidden_ready, n)
                made(pe.matmul(tile(("f", n))[0:FHID, :], filt_w[n], hidden, start=True, stop=True), ("f", n))
            project("hv")
            pe.wait_ge(hidden_ready, 3)
            for q in range(2):
                for t in range(NT):
                    for d in range(2):
                        j = 2 * d + q
                        made(pe.matmul(tile(("ft", q, t, d))[:, :], hidden[:, t * P:(t + 1) * P],
                                       filt_w4[:, j * HALF:(j + 1) * HALF], start=True, stop=True), ("ft", q, t, d))
            pe.wait_ge(ld_kdft, 32)
            for q in range(2):
                pe.wait_ge(taps_ready, NT * (q + 1))
                for c in range(2):
                    taps = (tap_sum, tap_dif)[c][q]
                    for f in range(NT):
                        o = tile(("K", q, c, f))
                        for t in range(NT):
                            mm = pe.matmul(o[:, :], kdft[:, c, t, f * P:(f + 1) * P], taps[:, t, :],
                                           start=(t == 0), stop=(t == NT - 1))
                        made(mm, ("K", q, c, f))
            def turn_conv(lo):
                for n in range(lo, lo + 4):
                    taken(pe, ("cv", n))
                    o = tile(("cvT", n))
                    for t in range(NT):
                        mm = pe.transpose(o[:, t * P:(t + 1) * P], conv[n][:, t * P:(t + 1) * P], ident)
                    made(mm, ("cvT", n))

            project("hx1")
            turn_conv(8)
            project("hx2")
            turn_conv(12)
            project("mq")
            turn_conv(16)
            project("mk")
            project("mv")
            project("mo")

            def spectrum(q, f):
                for c, name in enumerate((("U", q, f), ("S", q, f))):
                    o = tile(name)
                    for t in range(NT):
                        mm = pe.matmul(o[:, :], sdft[:, c, t, f * P:(f + 1) * P], sig[q][:, t, :],
                                       start=(t == 0), stop=(t == NT - 1))
                    made(mm, name)

            def back(q, t):
                pe.wait_ge(spec_ready, NT * (q + 1))
                o = tile(("y", q, t))
                for c in range(2):
                    for f in range(NT):
                        mm = pe.matmul(o[:, :], sdft[:, c, f, t * P:(t + 1) * P], spec[q][1 - c][:, f, :],
                                       start=(c + f == 0), stop=(c == 1 and f == NT - 1))
                made(mm, ("y", q, t))

            pe.wait_ge(ld_sdft, 32)
            for n in range(8, 12):
                taken(pe, ("cvT", n))
            for f in range(NT):
                spectrum(0, f)
            for t in range(NT):
                back(0, t)

            pe.wait_ge(rows_ready, 1)
            o = tile(("gcol",))
            for n, row in enumerate((r_i, r_a, r_b, r_lf)):
                for c in range(NT):
                    k = (n * NT + c) * ND2
                    mm = pe.transpose(o[:, k:k + ND2], row[:, c * P:(c + 1) * P], ident8)
            made(mm, ("gcol",))
            pe.wait_ge(dblk_ready, 1)
            made(pe.matmul(tile(("decay",))[:, 0:ND2 * NT], ones8[:, :], dblk[:, :, :].rearrange("k r c -> k (r c)"),
                           start=True, stop=True), ("decay",))

            def head_begin(h):
                o = tile(("kt", h))
                pe.wait_ge(k_ready, h + 1)
                for c in range(NT):
                    mm = pe.transpose(o[:, c * P:(c + 1) * P], kT[:, h, c * P:(c + 1) * P], ident)
                made(mm, ("kt", h))
                o = tile(("s", h))
                pe.wait_ge(q_ready, h + 1)
                for c in range(NT):
                    cs = slice(c * P, (c + 1) * P)
                    mm = pe.matmul(o[:, cs], kT[:, h, cs], qT[:, h, cs], start=True, stop=True)
                made(mm, ("s", h))
                for d in range(2):
                    r = d * MH + h
                    made(pe.matmul(tile(("bc", h, d))[:, :], ident8[:, r:r + 1].broadcast_to([ND2, P]), r_f, start=True, stop=True), ("bc", h, d))
                    o = tile(("up", h, d))
                    pe.wait_ge(kw_ready, 2 * h + d + 1)
                    for c in range(3):
                        n = c if d == 0 else NT - 1 - c
                        mm = pe.matmul(o[:, c * (P + 1):(c + 1) * (P + 1)], kw[d][c], v1[:, n, h, :], start=True, stop=True)
                    made(mm, ("up", h, d))

            def head_end(h):
                for d in range(2):
                    o = tile(("in", h, d))
                    taken(pe, ("up", h, d))
                    for c in range(1, NT):
                        n = c if d == 0 else NT - 1 - c
                        mm = pe.matmul(o[:, (c - 1) * (P + 1):c * (P + 1)], qT[:, h, n * P:(n + 1) * P], state[d][:, c - 1, :],
                                       start=True, stop=True)
                    made(mm, ("in", h, d))
                    pe.wait_ge(p_ready, 2 * h + d + 1)
                    for m in range(2):
                        o = tile(("nd", h, d, m))
                        for j in range(2):
                            n = 2 * m + j
                            mm = pe.matmul(o[:, j * (P + 1):(j + 1) * (P + 1)], wts[d][:, n, :], v1[:, n, h, :],
                                           start=True, stop=True)
                        made(mm, ("nd", h, d, m))

            for n in range(12, 16):
                taken(pe, ("cvT", n))
            pe.wait_ge(long_ready, NT)
            for t in range(NT):
                taken(pe, ("mv", t))
            for h in range(MH):
                head_begin(h)
                for name in conv2_chunk(h):
                    if name[0] == "U":
                        spectrum(1, name[2])
                    elif name[0] == "y":
                        back(1, name[2])
                head_end(h)
            for part, source in ((1, sig[2]), (0, hm)):
                pe.wait_ge(yn_ready, NT * (2 - part))
                for j in range(MH):
                    name = ("yT", j + MH * part)
                    o = tile(name)
                    for t in range(NT):
                        mm = pe.transpose(o[:, t * P:(t + 1) * P], source[:, t, j * P:(j + 1) * P], ident)
                    made(mm, name)
            wait_xT([("yT", j) for j in range(ND)])
            project("out0")
            project("out1")

            for t in range(NT):
                turn_norm(1, t)
            wait_norm(1)
            first = [BANK[("ff1", f)] for f in range(8)]
            at_tile[0] += NFF
            with pe.Fori(0, NFF // 8) as i:
                for j in range(8):
                    b, k = first[j]
                    if j % 4 == 0:
                        pe.wait_ge(mlp_loaded[j // 4], 16 * i + 16)
                    pe.wait_ge(bank_free[b], k + i)
                    w = mlp_slot[j // 4].rearrange("p (k n) -> p k n", k=ND)
                    for k in range(ND):
                        mm = pe.matmul(ps[b][:, :], w[:, k, (j % 4) * P:(j % 4 + 1) * P], xT[:, k, :],
                                       start=(k == 0), stop=(k == ND - 1))
                    mm.then_inc(bank_full[b], 1)
            down = [tile(("ff2", n)) for n in range(2 * NT)]
            for g in range(NFF // 4):
                pe.wait_ge(mlp_loaded[g % 2], 16 * (NFF // 8 + g // 2 + 1))
                w = mlp_slot[g % 2].rearrange("p (f n) -> p f n", f=4)
                tiles = [(j, n) for j in range(4) for n in range(2 * NT)]
                if g == NFF // 4 - 1:
                    tiles = [(j, n) for n in range(2 * NT) for j in range(4)]
                for j, n in tiles:
                    f, t, half = 4 * g + j, n // 2, n % 2
                    pe.wait_ge(act_ready, 4 + f + 1)
                    mm = pe.matmul(down[n][:, :], act[:, f, t * P:(t + 1) * P], w[:, j, half * 512:(half + 1) * 512],
                                   start=(f == 0), stop=(f == NFF - 1))
                    if f == NFF - 1:
                        made(mm, ("ff2", n))
                if g < NFF // 4 - 1:
                    mm.then_inc(act_used, 1)

            for t in range(NT):
                turn_norm(2, t)
            wait_norm(2)
            project("index")
            for n in (("iq", 0), ("iq", 1), ("ik", 0)):
                taken(pe, n)
            for i in range(1, NT):
                for h in range(IH):
                    o = tile(("ix", i, h))
                    r = ID * (h % 4)
                    made(pe.matmul(o[:, 0:(i + 1) * P], iqT[r:r + ID, h // 4, i * P:(i + 1) * P],
                                   ikT[r:r + ID, 0:(i + 1) * P], start=True, stop=True), ("ix", i, h))
            for g in ("fq", "fk", "fg", "fv"):
                project(g)

            def scores(kind, h):
                if kind == "f":
                    pe.wait_ge(nf_ready, 1)
                    made(pe.matmul(tile(("nF", h))[:, :], ident8[0:AH, h:h + 1].broadcast_to([AH, P]), f_n, start=True, stop=True), ("nF", h))
                if h % 2 == 0:
                    taken(pe, (kind + "q", h // 2))
                    taken(pe, (kind + "k", h // 2))
                r = HD * (h % 2)
                q, k = qkT[kind + "q"], qkT[kind + "k"]
                for i in range(NT):
                    o = tile((kind + "s", h, i))
                    mm = pe.matmul(o[:, 0:(i + 1) * P], q[r:r + HD, h // 2, i * P:(i + 1) * P],
                                   k[r:r + HD, h // 2, 0:(i + 1) * P], start=True, stop=(kind == "d"))
                    if kind == "f":
                        mm = pe.matmul(o[:, i * P:(i + 1) * P], ident, causal, start=False, stop=True)
                    made(mm, (kind + "s", h, i))

            def values(n, kind, h):
                pr, pt = prob[n % 3], probT[n % 2]
                at0 = 0
                for i in range(NT):
                    o = tile((kind + "T", h, i))
                    pe.wait_ge(prob_ready, NT * n + i + 1)
                    for s in range(i + 1):
                        mm = pe.transpose(o[:, s * P:(s + 1) * P], pr[:, (at0 + s) * P:(at0 + s + 1) * P], ident)
                    made(mm, (kind + "T", h, i))
                    at0 += i + 1
                if h == 0:
                    for t in range(NT):
                        taken(pe, (kind + "v", t))
                o = tile((kind + "o", h))
                at0 = 0
                for i in range(NT):
                    taken(pe, (kind + "T", h, i))
                    for s in range(i + 1):
                        mm = pe.matmul(o[:, i * HD:(i + 1) * HD], pt[:, at0 + s, :], vtok[kind][:, s, h * HD:(h + 1) * HD],
                                       start=(s == 0), stop=(s == i))
                    at0 += i + 1
                made(mm, (kind + "o", h))

            for n, (kind, h) in enumerate(HEADS):
                scores(kind, h)
                if n >= LAG:
                    values(n - LAG, *HEADS[n - LAG])
                if n in BETWEEN:
                    project(BETWEEN[n])
            for n in range(len(HEADS) - LAG, len(HEADS)):
                values(n, *HEADS[n])
            pe.wait_ge(ld_pool, 16 * 4)
            for j in range(PW // P):
                pe.wait_ge(win_ready, j + 1)
                made(pe.matmul(tile(("mix_pool", j))[:, :], pool_w[:, j, :], win[3 + j], start=True, stop=True),
                     ("mix_pool", j))

            def turn_heads(kind, count, lo):
                pe.wait_ge(og_ready, count)
                for j in range(lo, lo + 3):
                    o = tile(("mT", j))
                    for t in range(NT):
                        mm = pe.transpose(o[:, t * P:(t + 1) * P], otok[kind][:, t, (j - lo) * P:(j - lo + 1) * P], ident)
                    made(mm, ("mT", j))

            turn_heads("f", AH, 3)
            wait_xT([("mix_pool", j) for j in range(2)] + [("mT", j) for j in (3, 4, 5)])
            uses = [2 * group_at["fin0"] + half for half in range(2)]
            fin = [tile(("fx0", t)) for t in range(NT)]
            for use in uses:
                pe.wait_ge(slot_loaded[use % NSLOT], 16 * (use // NSLOT + 1))

            def finish(ks):
                for t in range(NT):
                    for k in ks:
                        mm = pe.matmul(fin[t][:, :], xT[:, k, t * P:(t + 1) * P], slots[:, uses[k // 4] % NSLOT, k % 4, :],
                                       start=(k == 0), stop=(k == 4))
                    if k == 4:
                        made(mm, ("fx0", t))

            finish((0, 1, 5, 6, 7))
            turn_heads("d", 2 * AH, 0)
            wait_xT([("mT", j) for j in (0, 1, 2)])
            finish((2, 3, 4))
            project("fin1")
            assert at_tile[0] == len(order)

        @block.scalar
        def _(ac):
            done = stepper(ac, act_step)

            done_squares = []

            def square(s, half, t, source):
                m = len(done_squares)
                junk = at(0 if s == 0 else 128.25, 4, 512)[:, m % 4, :]
                if m >= 4:
                    ac.wait_ge(*done_squares[m - 4])
                ac.activation(junk, source, ACT.Square, scale=D ** -0.5, accum_out=sumsq[:, s, half, t:t + 1])\
                  .then_inc(sumsq_ready[s], 1)
                done_squares.append((sumsq_ready[s], 1 + sum(d[0] is sumsq_ready[s] for d in done_squares)))

            def square_x(s, t):
                for half in range(2):
                    if s:
                        ac.wait_ge(x_ready, 2 * NT * (s // 2 - 1) + 2 * t + half + 1)
                    square(s, half, t, x[:, t, half * 512:(half + 1) * 512])

            def normed(s, t):
                _, n, xn = NORMS[s]
                ac.wait_ge(rstd_ready[n], t + 1)
                ac.activation(xn[:, t, :], x[:, t, :], ACT.Copy, scale=rstd[:, n, t:t + 1]).then_inc(xn_ready, 1)

            def renew(s, halves):
                for t in range(NT + 2):
                    if t < NT:
                        for half, name in halves(t):
                            square(2 * s - 1, half, t, full(ac, name)[:, :])
                    if 1 <= t <= NT:
                        square_x(2 * s, t - 1)
                    if t >= 2:
                        normed(s, t - 2)

            def sine(n):
                ac.wait_ge(sin_arg_ready, n + 1)
                ac.activation(hidden, sin_arg, ACT.Sin).then_inc(hidden_ready, 1)

            def conv_bias(n):
                if n >= 16:
                    full(ac, ("cvT", n - 8))
                if n < 8:
                    full(ac, ("cvT", n + 12))
                name = ("cv", n)
                ac.activation(conv[n], full(ac, name)[:, :], ACT.Identity, bias=scol(ROW_CONV_B + n),
                              scale=scol(ROW_CONV_W + NCT + n)).then_inc(conv_bias_ready, 1)

            def take_turned(n):
                name = ("cvT", n)
                q, j = (n - 8) // 4, n % 4
                if n < 12:
                    full(ac, ("K", 0, 1, NT - 1))
                else:
                    full(ac, ("K", 1, 1, NT - 1))
                free(ac.activation(sig[q][:, :, j * P:(j + 1) * P],
                                   full(ac, name)[:, :].rearrange("p (t c) -> p t c", t=NT), ACT.Copy), name)

            for t in range(NT + 1):
                if t < NT:
                    ac.wait_ge(ld_x[t], 16)
                    square_x(0, t)
                if t >= 1:
                    normed(0, t - 1)
                if t == 1:
                    sine(0)
            sine(1)
            sine(2)
            for n in range(8, 12):
                conv_bias(n)
            for q in range(2):
                for c in range(2):
                    for f in range(NT):
                        name = ("K", q, c, f)
                        free(ac.activation(spec[q][c][:, f, :], full(ac, name)[:, :], ACT.Copy, scale=1.0 / S), name)
            for lo, turned in ((12, 8), (16, 12), (0, 16)):
                for n in range(lo, lo + 4):
                    conv_bias(n)
                for n in range(turned, turned + 4):
                    take_turned(n)
            for n in range(4, 8):
                conv_bias(n)
            for n in range(8):
                taken(ac, ("cv", n))
                if n < 4:
                    full(ac, ("K", 1, 1, NT - 1))
                    ac.activation(qT[:, n, :], conv[n], ACT.Silu).then_inc(q_ready, 1)
                else:
                    ac.activation(kT[:, n - 4, :], conv[n], ACT.Silu).then_inc(k_silu, 1)
            ac.wait_ge(v1_ones, 1)
            for t in range(NT):
                name = ("mv", t)
                free(ac.activation(v1[:, t, :, 0:P], full(ac, name)[:, :].rearrange("p (h c) -> p h c", h=MH), ACT.Copy), name)
            ac.wait_ge(xn_ready, NT)
            for t in range(NT):
                name = ("mo", t)
                free(ac.activation(o_gate[:, t, :], full(ac, name)[:, :], ACT.Sigmoid), name)
            ac.wait_ge(gate_abs, 1)
            done(ac.activation(r_a, r_a, ACT.Exp, scale=-1.0))
            ac.activation(r_a, r_a, ACT.Ln, bias=one_col[0:ND2, :]).then_inc(softplus_ready, 1)
            ac.wait_ge(exp_args, 1)
            ac.activation(r_den, r_den, ACT.Exp, scale=-1.0).then_inc(exps_ready, 1)
            ac.activation(r_in, r_in, ACT.Exp).then_inc(exps_ready, 1)
            ac.activation(r_w, r_w, ACT.Exp).then_inc(exps_ready, 1)
            ac.activation(dec8[:, :], dec8[:, :], ACT.Exp).then_inc(exps_ready, 1)
            for h in range(MH):
                name = ("kt", h)
                free(ac.activation(ktok[:, h, :, :], full(ac, name)[:, :].rearrange("p (c d) -> p c d", c=NT), ACT.Copy), name)
                for d in range(2):
                    taken(ac, ("bc", h, d))
                    ac.activation(wts[d], wts[d], ACT.Exp).then_inc(wts_ready, 1)
                for d in range(2):
                    name = ("in", h, d)
                    o = full(ac, name)
                    if d or h:
                        for m in range(2):
                            taken(ac, ("nd", h, 0, m) if d else ("nd", h - 1, 1, m))
                    for c in range(1, NT):
                        n = c if d == 0 else NT - 1 - c
                        i = ac.activation(inter[:, n, :], o[:, (c - 1) * (P + 1):c * (P + 1)], ACT.Copy,
                                          scale=gcol[:, 2, n, d * MH + h:d * MH + h + 1])
                    free(i, name)
            for part, row in ((1, ROW_HYENA_W), (0, ROW_MLSTM_W)):
                for j in range(MH):
                    name = ("yT", j + MH * part)
                    free(ac.activation(xT[:, j + MH * part, :], full(ac, name)[:, :], ACT.Copy, scale=scol(row + j)), name)
            for t in range(NT):
                taken(ac, ("mx00", t))
                square(1, 0, t, mixed[:, t, 0:512])
            renew(1, lambda t: [(1, ("mx01", t))])
            first = [BANK[("ff1", f)] for f in range(8)]
            with ac.Fori(0, NFF // 8) as i:
                for j in range(8):
                    b, k = first[j]
                    ac.wait_ge(bank_full[b], i + (k + 1))
                    ac.wait_ge(act_ready, 8 * i + (j + 1))
                    ac.activation(relu[j % 4], ps[b][:, :], ACT.Relu).then_inc(bank_free[b], 1)
            renew(2, lambda t: [(half, ("ff2", 2 * t + half)) for half in range(2)])
            for j in range(2):
                name = ("iq", j)
                free(ac.activation(iqT[:, j, :], full(ac, name)[:, :], ACT.Copy), name)
            name = ("ik", 0)
            free(ac.activation(ikT, full(ac, name)[:, :], ACT.Copy), name)
            n = 0
            for i in range(1, NT):
                for h in range(IH):
                    name = ("ix", i, h)
                    o = full(ac, name)
                    if n >= 2:
                        ac.wait_ge(rdot_used, n - 1)
                    free(ac.activation(rdot[n % 2][:, 0:(i + 1) * P], o[:, 0:(i + 1) * P], ACT.Relu), name)
                    n += 1

            def take(g):
                for name, kind, _, _ in GROUPS[g][3]:
                    o = full(ac, name)
                    what, j = name
                    if what in ("fq", "dq"):
                        i = ac.activation(qkT[what][:, j, :], o[:, :], ACT.Copy, scale=HD ** -0.5)
                    elif what in ("fk", "dk"):
                        i = ac.activation(qkT[what][:, j, :], o[:, :], ACT.Copy)
                    elif what in ("fv", "dv"):
                        i = ac.activation(vtok[what[0]][:, j, :], o[:, 0:AW], ACT.Copy)
                    elif what in ("fg", "dg"):
                        i = ac.activation(gtok[what[0]][:, j, :], o[:, 0:AW], ACT.Silu)
                    elif what == "pv":
                        i = ac.activation(pvT[:, j, :], o[:, :], ACT.Copy)
                    elif what == "pg":
                        i = ac.activation(pgT[:, j, :], o[:, :], ACT.Silu)
                    else:
                        continue
                    free(i, name)

            take("fq")
            take("fk")
            take("fg")
            ac.wait_ge(fgate_abs, 1)
            done(ac.activation(f_a, f_a, ACT.Exp, scale=-1.0))
            ac.activation(f_a, f_a, ACT.Ln, bias=one_col[0:AH, :]).then_inc(fsoft_ready, 1)
            take("fv")

            def forget_rows(n, h):
                name = ("nF", h)
                if n >= 2:
                    ac.wait_ge(smax_ready, n - 1)
                free(ac.activation(nf_bc[n % 2], full(ac, name)[:, :], ACT.Copy), name)

            def exps(n, kind, h):
                ac.wait_ge(smax_ready, n + 1)
                at0 = 0
                for i in range(NT):
                    w = (i + 1) * P
                    p = prob[n % 3][:, at0 * P:at0 * P + w]
                    ac.activation(p, p, ACT.Exp, bias=smax[:, n % 3, i:i + 1], accum_out=ssum[:, n % 3, i:i + 1])\
                      .then_inc(prob_ready, 1)
                    at0 += i + 1

            def take_probs(n, kind, h):
                at0 = 0
                for i in range(NT):
                    name = (kind + "T", h, i)
                    o = full(ac, name)
                    if n >= 2:
                        k2, h2 = HEADS[n - 2]
                        full(ac, (k2 + "o", h2))
                    free(ac.activation(probT[n % 2][:, at0:at0 + i + 1, :],
                                       o[:, 0:(i + 1) * P].rearrange("p (s c) -> p s c", s=i + 1), ACT.Copy), name)
                    at0 += i + 1

            for n, (kind, h) in enumerate(HEADS):
                if kind == "f":
                    forget_rows(n, h)
                if n >= LAG:
                    take_probs(n - LAG, *HEADS[n - LAG])
                exps(n, kind, h)
                if n in BETWEEN:
                    take(BETWEEN[n])
            for n in range(len(HEADS) - LAG, len(HEADS)):
                take_probs(n, *HEADS[n])
            for j in (3, 4, 5, 0, 1, 2):
                name = ("mT", j)
                free(ac.activation(xT[:, 2 + j, :], full(ac, name)[:, :], ACT.Copy), name)
            for half in range(2):
                for t in range(NT):
                    taken(ac, (f"fx{half}", t))
                    square(5, half, t, x[:, t, half * 512:(half + 1) * 512])

        @block.vector
        def _(ve):
            done = stepper(ve, dve_step)

            def take_norm(s, t):
                row = NORMS[s][0]
                for half in range(2):
                    name = ("nT", s, t, half)
                    weight = scol(row + 4 * half, 4).rearrange("p (d o) -> p d o", o=1).broadcast_to([P, 4, P])
                    free(ve.tensor_tensor(xT[:, 4 * half:4 * half + 4, t * P:(t + 1) * P],
                                          full(ve, name)[:, :].rearrange("p (d n) -> p d n", d=4), weight, ALU.mult), name)

            def sine_arg(n):
                name = ("f", n)
                free(ve.tensor_scalar(sin_arg, full(ve, name)[0:FHID, :], fcol[:, n:n + 1], fcol[:, 3 + n:4 + n],
                                      ALU.add, ALU.mult), name)
                taken(ve, name)
                done(ve.tensor_scalar(sin_turn, sin_arg, 1.0 / (2 * np.pi), MAGIC, ALU.mult, ALU.add))
                done(ve.tensor_scalar(sin_turn, sin_turn, MAGIC, None, ALU.subtract))
                for part in (TWO_PI_HI, TWO_PI_LO):
                    done(ve.scalar_tensor_tensor(out=sin_arg, in0=sin_turn, scalar=-part, in1=sin_arg,
                                                 op0=ALU.mult, op1=ALU.add))
                ve.tensor_scalar(sin_arg, sin_arg, PI, -PI, ALU.min, ALU.max).then_inc(sin_arg_ready, 1)

            free(ve.tensor_copy(colv[:, :], full(ve, ("cols",))[:, 0:N_ROWS]), ("cols",))
            free(ve.tensor_copy(fcol[:, :], full(ve, ("fcols",))[0:FHID, 0:6]), ("fcols",))
            taken(ve, ("cols",))
            taken(ve, ("fcols",))
            sine_arg(0)
            for n in (1, 2):
                take_norm(0, 2 * n - 2)
                take_norm(0, 2 * n - 1)
                if n == 2:
                    ve.wait_ge(ld_rows, 16 * 6)
                    ve.wait_ge(xn_ready, NT)
                    o = full(ve, ("gate",))
                    ve.tensor_scalar(r_i, o[0:ND2, :], gbias[:, 0:1], None, ALU.add)
                    free(ve.tensor_scalar(r_f, o[GF:GF + ND2, :], gbias[:, 1:2], None, ALU.add), ("gate",))
                sine_arg(n)
            conv_count = [0]

            def short_conv(lo):
                for n in range(lo, lo + 4):
                    conv_count[0] += 1
                    u, c = full(ve, ("cv", n)), conv[n]
                    ve.wait_ge(conv_bias_ready, conv_count[0])
                    done(ve.scalar_tensor_tensor(out=c[:, 1:S], in0=u[:, 0:S - 1], scalar=scol(ROW_CONV_W + n),
                                                 in1=c[:, 1:S], op0=ALU.mult, op1=ALU.add))
                    free(ve.scalar_tensor_tensor(out=c[:, 0:S - 1], in0=u[:, 1:S], scalar=scol(ROW_CONV_W + 2 * NCT + n),
                                                 in1=c[:, 0:S - 1], op0=ALU.mult, op1=ALU.add), ("cv", n))

            short_conv(8)
            ve.wait_ge(ld_window, 32)
            n = 0
            for q in range(2):
                for t in range(NT):
                    name = ("ft", q, t, 0)
                    free(ve.tensor_tensor(tap_sum[q][:, t, :], full(ve, name)[:, :], window[:, t, :], ALU.mult), name)
                    name = ("ft", q, t, 1)
                    if n >= 2:
                        ve.wait_ge(taps_ready, n - 1)
                    w = window_b if t == 0 else window[:, t, :]
                    free(ve.tensor_tensor(taps_b[n % 2], full(ve, name)[:, :], w, ALU.mult), name)
                    n += 1
            for lo in (12, 16, 0, 4):
                short_conv(lo)

            def products(q, f):
                n = NT * q + f
                if n >= 2:
                    ve.wait_ge(spec_ready, n - 1)
                k0, k1 = spec[q][0][:, f, :], spec[q][1][:, f, :]
                name = ("U", q, f)
                u = full(ve, name)
                taken(ve, ("K", q, 0, f))
                taken(ve, ("K", q, 1, f))
                ve.tensor_tensor(prod[n % 2][0], u[:, :], k0, ALU.mult).then_inc(prod_ready, 1)
                free(ve.tensor_tensor(prod[n % 2][1], u[:, :], k1, ALU.mult), name)
                name = ("S", q, f)
                u = full(ve, name)
                ve.tensor_tensor(k0, u[:, :], k0, ALU.mult).then_inc(prod_ready, 1)
                free(ve.tensor_tensor(k1, u[:, :], k1, ALU.mult), name)

            def long_conv(q, t):
                ve.wait_ge(skip_ready, NT * q + t + 1)
                name = ("y", q, t)
                g = sig[q + 1][:, t, :]
                z = sig[q][:, t, :]
                for n in range(12, 20):
                    taken(ve, ("cvT", n))
                free(ve.tensor_tensor(z, full(ve, name)[:, :], z, ALU.add), name)
                taken(ve, name)
                ve.tensor_tensor(g, z, g, ALU.mult).then_inc(long_ready, 1)

            for f in range(NT):
                products(0, f)
            for t in range(NT):
                long_conv(0, t)

            def unflip(o, i):
                done(ve.tensor_scalar(o, i, is_f, None, ALU.mult))
                return ve.scalar_tensor_tensor(out=o, in0=i[:, ::-1], scalar=is_b, in1=o, op0=ALU.mult, op1=ALU.add)

            def chunks(r):
                return r.rearrange("k (c l) -> k c l", c=NT)

            taken(ve, ("gate",))
            full(ve, ("y", 0, NT - 1))
            done(unflip(r_e, r_i))
            done(unflip(r_lf, r_f))
            ve.scalar_tensor_tensor(out=r_a, in0=r_lf, scalar=-1.0, in1=r_lf, op0=ALU.mult, op1=ALU.max).then_inc(gate_abs, 1)
            done(ve.tensor_scalar(r_lf, r_lf, 0.0, None, ALU.min))
            ve.wait_ge(softplus_ready, 1)
            done(ve.tensor_tensor(r_lf, r_lf, r_a, ALU.subtract))
            done(ve.tensor_tensor_scan(r_b, chunk_reset, r_lf, 0.0, ALU.mult, ALU.add))
            done(ve.tensor_tensor(r_e, r_e, r_b, ALU.subtract))
            done(ve.memset(m_start[:, :], 0.0))
            for c in range(NT):
                cs = slice(c * P, (c + 1) * P)
                done(ve.tensor_tensor_scan(r_m[:, cs], r_e[:, cs], r_e[:, cs], m_start[:, c:c + 1], ALU.max, ALU.max))
                last = slice((c + 1) * P - 1, (c + 1) * P)
                done(ve.tensor_tensor(m_start[:, c + 1:c + 2], r_m[:, last], r_b[:, last], ALU.add))
            m_last = chunks(r_m)[:, :, P - 1:P]
            ve.tensor_tensor(r_den, r_m, r_b, ALU.add)
            ve.tensor_tensor(chunks(r_in), m_start[:, 0:NT].rearrange("k (c o) -> k c o", o=1).broadcast_to([ND2, NT, P]),
                             chunks(r_m), ALU.subtract)
            ve.tensor_tensor(chunks(r_w), chunks(r_e), m_last.broadcast_to([ND2, NT, P]), ALU.subtract)
            ve.tensor_tensor(dec8[:, :].rearrange("k (c o) -> k c o", o=1),
                             m_start[:, 0:NT].rearrange("k (c o) -> k c o", o=1), m_last, ALU.subtract).then_inc(exp_args, 1)
            ve.wait_ge(exp_args, 1)
            done(ve.tensor_scalar(r_m, r_m, -1.0, None, ALU.mult))
            ve.wait_ge(exps_ready, 4)
            done(unflip(r_i, r_e))
            done(unflip(r_f, r_m))
            done(unflip(r_a, r_den))
            done(unflip(r_b, r_in))
            unflip(r_lf, r_w).then_inc(rows_ready, 1)
            ve.tensor_tensor(dblk[:, :, :], dec8[:, :].rearrange("k (o c) -> k o c", o=1).broadcast_to([ND2, ND2, NT]),
                             ident8.rearrange("k (r o) -> k r o", o=1).broadcast_to([ND2, ND2, NT]), ALU.mult)\
              .then_inc(dblk_ready, 1)
            name = ("gcol",)
            free(ve.tensor_copy(gcol[:, :, :, :].rearrange("p a c r -> p (a c r)"),
                                full(ve, name)[:, 0:4 * NT * ND2]), name)
            name = ("decay",)
            free(ve.tensor_copy(decay[:, :, :].rearrange("p r c -> p (r c)"), full(ve, name)[:, 0:ND2 * NT]), name)
            taken(ve, ("gcol",))
            taken(ve, name)

            def head_begin(h):
                name = ("s", h)
                o = full(ve, name)[:, :].rearrange("p (c l) -> p c l", c=NT)
                sm = s_mask[h % 2]
                for d, keep in enumerate((keep_f, keep_b)):
                    i = ve.tensor_tensor(sm[d], o, keep.rearrange("p (o l) -> p o l", o=1).broadcast_to([P, NT, P]), ALU.mult)
                free(i, name)
                for d in range(2):
                    r = d * MH + h
                    name = ("bc", h, d)
                    o = full(ve, name)
                    if h:
                        full(ve, ("nd", h - 1, d, 1))
                    for c in range(NT):
                        i = ve.tensor_scalar(wts[d][:, c, :], o[:, c * P:(c + 1) * P], gcol[:, 0, c, r:r + 1], 0.0,
                                             ALU.add, ALU.min)
                    free(i, name)
                    name = ("up", h, d)
                    o = full(ve, name)
                    if h:
                        full(ve, ("in", h - 1, d))
                    done(ve.tensor_copy(state[d][:, 0, :], o[:, 0:P + 1]))
                    done(ve.scalar_tensor_tensor(out=state[d][:, 1, :], in0=state[d][:, 0, :], scalar=decay[:, r, 1:2],
                                                 in1=o[:, P + 1:2 * (P + 1)], op0=ALU.mult, op1=ALU.add))
                    free(ve.scalar_tensor_tensor(out=state[d][:, 2, :], in0=state[d][:, 1, :], scalar=decay[:, r, 2:3],
                                                 in1=o[:, 2 * (P + 1):3 * (P + 1)], op0=ALU.mult, op1=ALU.add), name)
                taken(ve, ("s", h))
                for d in range(2):
                    ve.wait_ge(wts_ready, 2 * h + d + 1)
                    ve.tensor_tensor(wts[d], wts[d], sm[d], ALU.mult).then_inc(p_ready, 1)

            def head_end(h):
                for d in range(2):
                    r = d * MH + h
                    first_n = 0 if d == 0 else NT - 1
                    taken(ve, ("in", h, d))
                    for m in range(2):
                        name = ("nd", h, d, m)
                        o = full(ve, name)
                        for j in range(2):
                            n = 2 * m + j
                            src = o[:, j * (P + 1):(j + 1) * (P + 1)]
                            if n == first_n:
                                i = ve.tensor_copy(nd[:, n, :], src)
                            else:
                                i = ve.tensor_tensor(nd[:, n, :], src, inter[:, n, :], ALU.add)
                        free(i, name)
                    taken(ve, ("nd", h, d, 0))
                    taken(ve, ("nd", h, d, 1))
                    dn = nd[:, :, P:P + 1]
                    q = den[:, 0, :].rearrange("p (c o) -> p c o", o=1)
                    done(ve.scalar_tensor_tensor(out=q, in0=dn, scalar=-1.0, in1=dn, op0=ALU.mult, op1=ALU.max))
                    done(ve.tensor_tensor(q, q, gcol[:, 1, :, r:r + 1], ALU.max))
                    done(ve.reciprocal(den[:, 1, :], den[:, 0, :]))
                    rec = den[:, 1, :].rearrange("p (c o) -> p c o", o=1).broadcast_to([P, NT, P])
                    hs = hm[:, :, h * P:(h + 1) * P]
                    if d == 0:
                        done(ve.tensor_tensor(hs, nd[:, :, 0:P], rec, ALU.mult))
                    else:
                        done(ve.tensor_tensor(nd[:, :, 0:P], nd[:, :, 0:P], rec, ALU.mult))
                        ve.tensor_tensor(hs, hs, nd[:, :, 0:P], ALU.add).then_inc(h_ready, 1)

            for h in range(MH):
                head_begin(h)
                for name in conv2_chunk(h):
                    if name[0] == "U":
                        products(1, name[2])
                    elif name[0] == "y":
                        long_conv(1, name[2])
                head_end(h)
            for m, (sq, groups, ss, rs, y, root_ready) in enumerate(((sq_h, HG, sumsq_h, rstd_h, sig[2], rstd_h_ready),
                                                              (sq_m, MH, sumsq_m, rstd_m, hm, rstd_m_ready))):
                ve.wait_ge(sq_ready, NT * (m + 1))
                ve.tensor_reduce(ss[:, 0:NT * groups], sq.rearrange("p t (g c) -> p (t g) c", g=groups), AX_X, ALU.add)\
                  .then_inc(gsum_ready, 1)
                ve.wait_ge(root_ready, 1)
                for t in range(NT):
                    yt = y[:, t, :].rearrange("p (g c) -> p g c", g=groups)
                    rt = rs[:, t * groups:(t + 1) * groups].rearrange("p (g o) -> p g o", o=1)
                    ve.tensor_tensor(yt, yt, rt.broadcast_to([P, groups, HALF // groups]), ALU.mult).then_inc(yn_ready, 1)

            def scale_rows(s, sources, loaded):
                ve.wait_ge(loaded, 16)
                for t in range(NT):
                    ve.wait_ge(rstd_ready[s], t + 1)
                    for half, (source, name) in enumerate(sources(t)):
                        cols = slice(half * 512, (half + 1) * 512)
                        i = ve.scalar_tensor_tensor(out=mixed[:, t, cols], in0=source, scalar=rstd[:, s, t:t + 1],
                                                    in1=row_bc[:, cols], op0=ALU.mult, op1=ALU.mult)
                        if name:
                            free(i, name)
                        else:
                            i.then_inc(mix_ready, 1)

            for t in range(NT):
                name = ("mx00", t)
                free(ve.tensor_copy(mixed[:, t, 0:512], full(ve, name)[:, :]), name)
            scale_rows(1, lambda t: ((mixed[:, t, 0:512], None), (full(ve, ("mx01", t))[:, :], ("mx01", t))), ld_mix_post)
            for t in range(NT):
                take_norm(1, t)
            scale_rows(3, lambda t: [(full(ve, ("ff2", 2 * t + half))[:, :], ("ff2", 2 * t + half)) for half in range(2)],
                       ld_mlp_post)
            for t in range(NT):
                take_norm(2, t)
            for t in range(NT):
                name = ("iw", t)
                free(ve.tensor_scalar(iw[:, t, :], full(ve, name)[:, 0:IH], IH ** -0.5, None, ALU.mult), name)
            for t in range(NT):
                taken(ve, ("iw", t))
            n = 0
            for i in range(1, NT):
                w = (i + 1) * P
                sc = score[:, i - 1, 0:w]
                for h in range(IH):
                    n += 1
                    taken(ve, ("ix", i, h))
                    r = rdot[(n - 1) % 2][:, 0:w]
                    if h == 0:
                        ins = ve.tensor_scalar(sc, r, iw[:, i, h:h + 1], None, ALU.mult)
                    else:
                        ins = ve.scalar_tensor_tensor(out=sc, in0=r, scalar=iw[:, i, h:h + 1], in1=sc, op0=ALU.mult, op1=ALU.add)
                    ins.then_inc(rdot_used, 1)
                    ve.wait_ge(rdot_used, n)
                done(ve.memset(score[0:HD, i - 1, w - HD:w], LOWEST))

            for i in range(1, NT):
                w = (i + 1) * P
                sc, wk = score[:, i - 1, 0:w], work[:, i - 1, 0:w]
                for n in range(TOPK // 8):
                    src = sc if n == 0 else wk
                    done(ve.max(top8[:, :], src))
                    done(ve.match_replace(wk, top8[:, :], src, TAKEN))
                done(ve.tensor_tensor(sc, wk, sc, ALU.is_equal))
                ve.tensor_scalar(sc, sc, NEG, None, ALU.mult).then_inc(sel_ready, 1)

            name = ("ff", 0)
            free(ve.tensor_scalar(f_f, full(ve, name)[0:AH, :], fbias[:, :], None, ALU.add), name)
            taken(ve, name)
            ve.scalar_tensor_tensor(out=f_a, in0=f_f, scalar=-1.0, in1=f_f, op0=ALU.mult, op1=ALU.max).then_inc(fgate_abs, 1)
            done(ve.tensor_scalar(f_f, f_f, 0.0, None, ALU.min))
            ve.wait_ge(fsoft_ready, 1)
            done(ve.tensor_tensor(f_f, f_a, f_f, ALU.subtract))
            ve.tensor_tensor_scan(f_n, one_col[0:AH, :].broadcast_to([AH, S]), f_f, 0.0, ALU.mult, ALU.add).then_inc(nf_ready, 1)

            def maxima(n, kind, h):
                at0 = 0
                if n >= 3:
                    ve.wait_ge(prob_ready, NT * (n - 2))
                    k2, h2 = HEADS[n - 3]
                    for i in range(NT):
                        full(ve, (k2 + "T", h2, i))
                if kind == "f":
                    taken(ve, ("nF", h))
                for i in range(NT):
                    w = (i + 1) * P
                    name = (kind + "s", h, i)
                    if kind == "f":
                        bias = nf_bc[n % 2][:, 0:w]
                    else:
                        bias = chunk_bias if i == 0 else score[:, i - 1, 0:w]
                        if i and h == 0:
                            ve.wait_ge(sel_ready, i)
                    free(ve.tensor_tensor_reduce(prob[n % 3][:, at0 * P:at0 * P + w], full(ve, name)[:, 0:w], bias, 1.0,
                                                 LOWEST, ALU.add, ALU.max, smax[:, n % 3, i:i + 1]), name)
                    at0 += i + 1
                for i in range(NT):
                    taken(ve, (kind + "s", h, i))
                ve.tensor_scalar(smax[:, n % 3, :], smax[:, n % 3, :], -1.0, None, ALU.mult).then_inc(smax_ready, 1)

            def outputs(n, kind, h):
                ve.wait_ge(prob_ready, NT * (n + 1))
                done(ve.reciprocal(ssum[:, n % 3, :], ssum[:, n % 3, :]))
                name = (kind + "o", h)
                o = full(ve, name)[:, 0:NT * HD].rearrange("p (t c) -> p t c", t=NT)
                rec = ssum[:, n % 3, :].rearrange("p (t o) -> p t o", o=1).broadcast_to([P, NT, HD])
                free(ve.tensor_tensor(otok[kind][:, :, h * HD:(h + 1) * HD], o, rec, ALU.mult), name)

            for n, (kind, h) in enumerate(HEADS):
                maxima(n, kind, h)
                if n >= LAG:
                    outputs(n - LAG, *HEADS[n - LAG])
            for n in range(len(HEADS) - LAG, len(HEADS)):
                outputs(n, *HEADS[n])
            for j in range(PW // P):
                name = ("mix_pool", j)
                o = full(ve, name)
                taken(ve, ("pg", j))
                free(ve.scalar_tensor_tensor(out=xT[:, j, :], in0=o[:, :], scalar=scol(ROW_POOL + j), in1=pgT[:, j, :],
                                             op0=ALU.mult, op1=ALU.mult), name)
            for half in range(2):
                for t in range(NT):
                    name = (f"fx{half}", t)
                    xs = x[:, t, half * 512:(half + 1) * 512]
                    free(ve.tensor_tensor(xs, xs, full(ve, name)[:, :], ALU.add), name)
            ve.wait_ge(ld_final, 16)
            for t in range(NT):
                ve.wait_ge(rstd_ready[5], t + 1)
                ve.scalar_tensor_tensor(out=mixed[:, t, :], in0=x[:, t, :], scalar=rstd[:, 5, t:t + 1], in1=row_bc[:, :],
                                        op0=ALU.mult, op1=ALU.mult).then_inc(out_ready, 1)

        @block.gpsimd
        def _(po):
            done = stepper(po, pool_step)

            def root(o, i, n, ready):
                done(po.tensor_scalar(o, i, 1.0 / n, EPS, ALU.mult, ALU.add))
                po.tensor_tensor(o, o, minus_half[:, 0:o.shape[1]], ALU.pow).then_inc(ready, 1)

            def norm_root(s, t, count):
                po.wait_ge(sumsq_ready[s], count)
                r = rstd[:, s, t:t + 1]
                done(po.tensor_scalar(r, sumsq[:, s, 0, t:t + 1], sumsq[:, s, 1, t:t + 1], EPS, ALU.add, ALU.add))
                po.tensor_tensor(r, r, minus_half[:, 0:1], ALU.pow).then_inc(rstd_ready[s], 1)

            def add_rows(s, count, scaled):
                for t in range(NT + 1):
                    if t < NT:
                        norm_root(2 * s - 1, t, count(t))
                        po.wait_ge(ld_x[t], 32)
                        for half in range(2):
                            cols = slice(half * 512, (half + 1) * 512)
                            scaled(t, half)
                            po.tensor_tensor(x[:, t, cols], x[:, t, cols], mixed[:, t, cols], ALU.add).then_inc(x_ready, 1)
                    if t:
                        norm_root(2 * s, t - 1, 2 * t)

            for tile, value in ((minus_half, -0.5), (one_col, 1.0), (ones8, 1.0)):
                po.memset(tile[:, :], value).then_inc(consts_set, 1)
            po.memset(pool_w[:, :, :], 0.0).then_inc(pool_w_ready, 1)
            po.wait_ge(consts_set, 3)
            po.memset(gate_w2[:, :, ND2:GF], 0.0).then_inc(gate_w_ready, 1)
            po.wait_ge(ld_gate, 16)
            for kind in range(2):
                src = gate_w[:, :, :].rearrange("p k (d j c) -> p k d j c", d=2, j=2)[:, :, :, kind, :]
                dst = gate_w2[:, :, GF * kind:GF * kind + ND2].rearrange("p k (d c) -> p k d c", d=2)
                po.tensor_copy(dst, src).then_inc(gate_w_ready, 1)
            for t in range(NT):
                norm_root(0, t, 2 * t + 2)
            n = 0
            for q in range(2):
                for t in range(NT):
                    taken(po, ("ft", q, t, 0))
                    taken(po, ("ft", q, t, 1))
                    f, b = tap_sum[q][:, t, :], taps_b[n % 2]
                    po.tensor_tensor(tap_dif[q][:, t, :], b, f, ALU.subtract)
                    po.tensor_tensor(f, f, b, ALU.add).then_inc(taps_ready, 1)
                    n += 1
            po.memset(v1[:, :, :, P:P + 1], 1.0).then_inc(v1_ones, 1)
            for h in range(MH):
                po.wait_ge(k_silu, h + 1)
                po.tensor_scalar(kT[:, h, :], kT[:, h, :], P ** -0.5, None, ALU.mult).then_inc(k_ready, 1)

            def combine(q, f):
                n = NT * q + f
                taken(po, ("S", q, f))
                taken(po, ("U", q, f))
                k0, k1 = spec[q][0][:, f, :], spec[q][1][:, f, :]
                po.wait_ge(prod_ready, 2 * n + 2)
                po.tensor_tensor(k0, k0, prod[n % 2][1], ALU.subtract)
                po.tensor_tensor(k1, k1, prod[n % 2][0], ALU.add).then_inc(spec_ready, 1)

            def skip(q):
                full(po, ("S", q, NT - 1))
                po.wait_ge(ld_fb, 16)
                for t in range(NT):
                    z = sig[q][:, t, :]
                    po.tensor_tensor(z, z, row_bc[:, q * HALF:(q + 1) * HALF], ALU.mult).then_inc(skip_ready, 1)

            for f in range(NT):
                combine(0, f)
            skip(0)

            def state_keys(h):
                taken(po, ("kt", h))
                taken(po, ("gcol",))
                for d in range(2):
                    if h:
                        full(po, ("up", h - 1, d))
                    for c in range(3):
                        n = c if d == 0 else NT - 1 - c
                        i = po.tensor_scalar(kw[d][c], ktok[:, h, n, :], gcol[:, 3, n, d * MH + h:d * MH + h + 1], None, ALU.mult)
                    i.then_inc(kw_ready, 1)

            for h in range(MH):
                state_keys(h)
                for name in conv2_chunk(h):
                    if name[0] == "U":
                        combine(1, name[2])
                if h == 1:
                    skip(1)
            po.wait_ge(long_ready, 2 * NT)
            full(po, ("y", 1, NT - 1))
            for t in range(NT):
                po.tensor_tensor(sq_h[:, t, :], sig[2][:, t, :], sig[2][:, t, :], ALU.mult).then_inc(sq_ready, 1)
            po.wait_ge(gsum_ready, 1)
            root(rstd_h[:, :], sumsq_h[:, :], HALF // HG, rstd_h_ready)
            po.wait_ge(h_ready, MH)
            for t in range(NT):
                taken(po, ("mo", t))
                po.tensor_tensor(hm[:, t, :], hm[:, t, :], o_gate[:, t, :], ALU.mult).then_inc(gated, 1)
                po.wait_ge(gated, t + 1)
                po.tensor_tensor(sq_m[:, t, :], hm[:, t, :], hm[:, t, :], ALU.mult).then_inc(sq_ready, 1)
            po.wait_ge(gsum_ready, 2)
            root(rstd_m[:, :], sumsq_m[:, :], HALF // MH, rstd_m_ready)
            add_rows(1, lambda t: NT + t + 1, lambda t, half: taken(po, ("mx01", t)) if half else po.wait_ge(mix_ready, t + 1))
            first = [BANK[("ff1", f)] for f in range(8)]
            for n in range(4):
                po.engine_nop().then_inc(act_ready, 1)
            with po.Fori(0, NFF // 8) as i:
                for j in range(8):
                    b, k = first[j]
                    po.wait_ge(bank_free[b], i + (k + 1))
                    r = relu[j % 4]
                    ins = po.tensor_tensor(act[:, bass.ds(8 * i + j, 1), :], r, r, ALU.mult)
                    ins.then_inc(act_ready, 1)
            add_rows(2, lambda t: 2 * t + 2, lambda t, half: taken(po, ("ff2", 2 * t + half)))
            for half in range(2):
                use = 2 * group_at["index"] + half
                po.wait_ge(slot_loaded[use % NSLOT], 16 * (use // NSLOT + 1))
                src = slots[:, use % NSLOT, :, 256:256 + ID].rearrange("p k (o c) -> p k o c", o=1)
                po.tensor_copy(wik[:, 4 * half:4 * half + 4, :].rearrange("p k (r c) -> p k r c", r=4),
                               src.broadcast_to([P, 4, 4, ID])).then_inc(wik_ready, 1)

            def gate(kind):
                for n in range(AH):
                    taken(po, (kind + "o", n))
                    for t in range(NT):
                        taken(po, (kind + "g", t))
                    o = otok[kind][:, :, n * HD:(n + 1) * HD]
                    po.tensor_tensor(o, o, gtok[kind][:, :, n * HD:(n + 1) * HD], ALU.mult).then_inc(og_ready, 1)

            def add_back(o, i, by):
                done(po.tensor_copy(o[:, 0:by], i[:, 0:by]))
                done(po.tensor_tensor(o[:, by:S], i[:, by:S], i[:, 0:S - by], ALU.add))

            po.wait_ge(ld_count, 16)
            for j in range(2):
                taken(po, ("pv", j))
                v, (s2, s4, w) = pvT[:, j, :], (win[0], win[1], win[3 + j])
                add_back(s2, v, 1)
                if j == 1:
                    add_back(s4, s2, 2)
                    add_back(s2, s4, 4)
                done(po.tensor_copy(w[0:HD, :], s2[0:HD, :]))
                add_back(w[HD:P, :], s2[HD:P, :], 2 if j == 0 else 8)
                done(po.tensor_tensor(w, w, inv_count[:, j, :], ALU.mult))
                po.tensor_tensor(w, w, v, ALU.subtract).then_inc(win_ready, 1)
            gate("f")
            gate("d")
            for t in range(NT):
                norm_root(5, t, NT + t + 1)


def kernel(**inputs):
    import concourse.bacc as bacc
    from concourse.bass_utils import run_bass_kernel_spmd

    nc = bacc.Bacc("TRN2", target_bir_lowering=False, num_devices=1)
    arrays, aps = {}, {}
    for name, value in {**inputs, **constants()}.items():
        arr = np.ascontiguousarray(value)
        arrays["in_" + name] = arr
        aps[name] = nc.dram_tensor("in_" + name, arr.shape, mybir.dt.from_np(arr.dtype), kind="ExternalInput").ap()
    out = nc.dram_tensor("out", (1, S, D), F32, kind="ExternalOutput").ap()
    build_program(nc, aps, out)
    result = run_bass_kernel_spmd(nc, [arrays], core_ids=[0])
    return np.asarray(result.results[0]["out"])
```

```python
from contextlib import ExitStack

import numpy as np

import concourse.bass as bass
from concourse import mybir

F32 = mybir.dt.float32
F32R = mybir.dt.float32r
ALU = mybir.AluOpType
ACT = mybir.ActivationFunctionType
AX_X = mybir.AxisListType.X

P = 128
S = 512
NT = S // P
D = 1024
ND = D // P
HALF = D // 2
MH = 4
ND2 = 2 * MH
NCONV = 5 * HALF
NCT = NCONV // P
OFF_MV, OFF_MO, OFF_GATE = NCONV, NCONV + HALF, NCONV + 2 * HALF
HG = 8
NF = NT // 2
EMB, FHID = 33, 64
DFF = 4 * D
NFF = DFF // P
EPS = 1e-6
HD = 64
AW = 384
AH = AW // HD
PW = 256
IH, ID = 8, 32
TOPK = 128
OFF_DQ, OFF_DK, OFF_DV, OFF_DG = 512, 896, 1280, 1664
OFF_IQ = 2048
OFF_FQ, OFF_FK, OFF_FV, OFF_FG = 2344, 2728, 3112, 3496
NIN2 = 3886
GF = 32
NEG = -1e30
LOWEST = -3e38
TAKEN = -3.3e38
MAGIC = 12582912.0
TWO_PI_HI = 6.28125
TWO_PI_LO = 2 * np.pi - 6.28125
PI = float(np.nextafter(np.float32(np.pi), np.float32(0)))

ROW_CONV_W, ROW_CONV_B = 0, 3 * NCT
ROW_MIX_PRE = ROW_CONV_B + NCT
ROW_MLP_PRE = ROW_MIX_PRE + ND
ROW_MLSTM_W = ROW_MLP_PRE + ND
ROW_HYENA_W = ROW_MLSTM_W + MH
ROW_NORM2 = ROW_HYENA_W + MH
ROW_POOL = ROW_NORM2 + ND
N_ROWS = ROW_POOL + PW // P



def weight_groups():
    def ch(n0, cols):
        return [(("cv", n0 + j), "ch", P * j, P) for j in range(cols // P)]

    def tok(name, c0, n):
        return [((name, t), f"tok{t}", c0, n) for t in range(NT)]

    def many(name, cols, c0=0):
        return [((name, j), "ch", c0 + P * j, P) for j in range(cols // P)]

    return {
        "hv": ("w_in", 1024, 512, ch(8, 512)),
        "hx1": ("w_in", 1536, 512, ch(12, 512)),
        "hx2": ("w_in", 2048, 512, ch(16, 512)),
        "mq": ("w_in", 0, 512, ch(0, 512)),
        "mk": ("w_in", 512, 512, ch(4, 512)),
        "mv": ("w_in", OFF_MV, 512, tok("mv", 0, 512)),
        "mo": ("w_in", OFF_MO, 512, tok("mo", 0, 512)),
        "out0": ("w_out", 0, 512, tok("mx00", 0, 512)),
        "out1": ("w_out", 512, 512, tok("mx01", 0, 512)),
        "index": ("w_in_2", OFF_IQ, 296, many("iq", IH * ID) + [(("ik", 0), "ch", 256, ID)] + tok("iw", 288, IH)),
        "fq": ("w_in_2", OFF_FQ, AW, many("fq", AW)),
        "fk": ("w_in_2", OFF_FK, AW, many("fk", AW)),
        "fg": ("w_in_2", OFF_FG, AW + AH, [(("ff", 0), "ch", AW, AH)] + tok("fg", 0, AW)),
        "fv": ("w_in_2", OFF_FV, AW, tok("fv", 0, AW)),
        "dq": ("w_in_2", OFF_DQ, AW, many("dq", AW)),
        "dk": ("w_in_2", OFF_DK, AW, many("dk", AW)),
        "dv": ("w_in_2", OFF_DV, AW, tok("dv", 0, AW)),
        "dg": ("w_in_2", OFF_DG, AW, tok("dg", 0, AW)),
        "pool": ("w_in_2", 0, 512, many("pv", PW) + many("pg", PW, PW)),
        "fin0": ("w_out_2", 0, 512, tok("fx0", 0, 512)),
        "fin1": ("w_out_2", 512, 512, tok("fx1", 0, 512)),
    }


GROUPS = weight_groups()
GROUP_ORDER = ["hv", "hx1", "hx2", "mq", "mk", "mv", "mo", "out0", "out1", "index", "fq", "fk", "fg", "fv",
               "dq", "dk", "dv", "pool", "dg", "fin0", "fin1"]
K_ORDER = {"out0": (4, 5, 6, 7, 0, 1, 2, 3), "fin0": (0, 1, 6, 7, 4, 5, 2, 3)}
EARLY = {"out0": 3, "fin0": 2}
N_BEFORE = 9
UP = 4 * N_BEFORE
DOWN = UP + NFF
PIECE = {g: 4 * n + (2 * NFF if n >= N_BEFORE else 0) for n, g in enumerate(GROUP_ORDER)}
CHANNELS = {"out0": [("yT", j) for j in range(ND)],
            "fin0": [("mix_pool", j) for j in range(PW // P)] + [("mT", j) for j in range(6)]}
BETWEEN = {0: "dq", 1: "dk", 3: "dv", 5: "pool", 8: "dg"}
CHOICE = [0, 16, 28, 31, 44, 48, 48]
LAG = 2
HEADS = [("f", h) for h in range(AH)] + [("d", h) for h in range(AH)]


def psum_order():
    def group(g):
        return [name for name, *_ in GROUPS[g][3]]

    def turned(lo, hi):
        return [("cvT", n) for n in range(lo, hi)]

    def norm(s):
        return [("nT", s, t, half) for t in range(NT) for half in range(2)]

    def spectrum(q):
        return [(c, q, f, odd) for f in range(NF) for c in "US" for odd in range(2)]

    def begin(h):
        return [("s", h)] + [(what, h, d) for d in range(2) for what in ("bc", "up")]

    def end(h):
        return [(what, h, d) + m for d in range(2) for what, m in (("in", ()), ("nd", (0,)), ("nd", (1,)))]

    o = [("cols",)] + norm(0)[:4] + [("fcols",), ("f", 0)] + norm(0)[4:] + [("f", 1), ("gate",), ("f", 2)] + group("hv")
    o += [("ft", q, t, d) for q in range(2) for t in range(NT) for d in range(2)]
    o += [("K", q, c, f, odd) for q in range(2) for c in range(2) for f in range(NF) for odd in range(2)]
    o += group("hx1") + turned(8, 12) + group("hx2") + turned(12, 16) + group("mq") + turned(16, 20)
    o += spectrum(0) + group("mk") + [("y", 0, t) for t in range(NT)] + [("gcol",), ("decay",), ("kt", 0)] + group("mv")
    o += begin(0) + spectrum(1) + [("kt", 1)] + group("mo") + [("y", 1, t) for t in range(NT)]
    o += begin(1) + [("kt", 2)] + end(0) + begin(2) + [("kt", 3)] + end(1)
    o += begin(3) + end(2) + [("yT", j) for j in range(MH, ND)] + [("yT", 0)] + end(3) + [("yT", 1)]
    o += group("out0") + [("yT", 2), ("yT", 3)] + group("out1") + norm(1)
    o += [("ff1", f) for f in range(NFF)] + [("ff2", n) for n in range(2 * NT)]
    o += norm(2) + group("index")
    for i, g in enumerate(("fq", "fk", "fg"), 1):
        o += [("ix", i, h) for h in range(IH)] + group(g)
    o += group("fv")
    for n, (kind, h) in enumerate(HEADS):
        o += scores_of(kind, h)
        if n >= LAG:
            o += values_of(*HEADS[n - LAG])
        if n in BETWEEN:
            o += group(BETWEEN[n])
    for head in HEADS[-LAG:]:
        o += values_of(*head)
    o += [("mix_pool", j) for j in range(PW // P)] + [("mT", j) for j in (3, 4, 5)]
    o += group("fin0") + [("mT", j) for j in (0, 1, 2)] + group("fin1")
    return o


def scores_of(kind, h):
    return ([("nF", h)] if kind == "f" else []) + [(kind + "s", h, i) for i in range(NT)]


def values_of(kind, h):
    return [(kind + "T", h, i) for i in range(NT)] + [(kind + "o", h)]


def bank_table():
    order = psum_order()
    assert len(set(order)) == len(order)
    return {name: (n % 8, n // 8) for n, name in enumerate(order)}


def constants():
    f32 = np.float32
    n = np.concatenate([np.arange(0, S, 2), np.arange(1, S, 2)])
    ang = np.pi * (((2 * np.arange(S // 2)[None, :] + 1) * n[:, None]) % (4 * S)) / (2 * S)
    dft = np.stack([np.cos(ang), np.sin(ang)]).astype(f32)
    bands = (EMB - 1) // 2
    t = np.linspace(0.0, 1.0, S, dtype=f32)[:, None]
    turn = (f32(2.0 * np.pi) * np.arange(S, dtype=f32)[:, None] / f32(S)).astype(f32)
    fr = np.linspace(1e-4, bands - 1, bands, dtype=f32)[None, :]
    z = np.concatenate([t, np.cos(fr * turn), -np.sin(fr * turn)], axis=-1).astype(f32)
    lo, hi = np.log(1e-2) / 1.5, np.log(1e-2) / 0.3
    deltas = np.abs(np.linspace(lo, hi, HALF, dtype=f32))
    window = (np.exp(-t * deltas[None, :]) / S).astype(f32)[n]
    window_b = window[:P].copy()
    window_b[0] = 0
    i, j = np.arange(P)[:, None], np.arange(P)[None, :]
    masks = np.stack([np.eye(P), np.where(i <= j, 0.0, NEG), np.where(i >= j, 0.0, NEG),
                      np.where((i < HD) & (j >= HD), NEG, 0.0)]).astype(f32)
    count = np.minimum(np.arange(S) + 1, np.array([2, 4, 8, 16])[:, None])
    inv_count = (1.0 / np.repeat(count, HD, axis=0)).astype(f32)
    rows = np.zeros((ND2, S + ND2 + 2), f32)
    rows[:, 0:S] = np.arange(S) % P != 0
    rows[:, S:S + ND2] = np.eye(ND2)
    rows[:MH, -2] = 1
    rows[MH:, -1] = 1
    return {
        "c_dft_in": dft, "c_dft_out": np.ascontiguousarray(dft.transpose(0, 2, 1)),
        "c_z": np.ascontiguousarray(z[n].T), "c_window": window, "c_window_b": window_b,
        "c_masks": masks, "c_inv_count": inv_count, "c_rows": rows,
    }


def build_program(nc, a, out):
    BANK = bank_table()
    with ExitStack() as ctx:
        def sb(name, shape, dtype=F32):
            return ctx.enter_context(nc.sbuf_tensor(name, shape, dtype))

        def sem(name):
            return ctx.enter_context(nc.semaphore(name))

        raw = sb("raw_weights", [P, 2, 2048])
        wh, wl = sb("weight_high", [P, 2, 1024], F32R), sb("weight_low", [P, 2, 1024], F32R)
        xh, xl = sb("x_high", [P, ND, S], F32R), sb("x_low", [P, ND, S], F32R)
        x = sb("x", [P, NT, D])
        masks = sb("masks", [P, 4, P])
        ident, cut_after, causal, chunk_bias = (masks[:, n, :] for n in range(4))
        colv = sb("colv", [P, N_ROWS])
        fcol = sb("fcol", [FHID, 6])
        row_bc = sb("row_bc", [P, D])
        rows_c = sb("rows_c", [ND2, S + ND2 + 2])
        chunk_reset = rows_c[:, 0:S]
        ident8 = rows_c[:, S:S + ND2]
        is_f, is_b = rows_c[:, S + ND2:S + ND2 + 1], rows_c[:, S + ND2 + 1:]
        gbias = sb("gbias", [ND2, 2])
        fbias = sb("fbias", [AH, 1])
        ones8 = sb("ones8", [ND2, P])
        one_col = sb("one_col", [P, 1])
        minus_half = sb("minus_half", [P, NT * HG])
        sumsq = sb("sumsq", [P, 6, 2, NT])
        rstd = sb("rstd", [P, 6, NT])
        sumsq_h, rstd_h = sb("sumsq_h", [P, NT * HG]), sb("rstd_h", [P, NT * HG])
        sumsq_m, rstd_m = sb("sumsq_m", [P, MH, NT]), sb("rstd_m", [P, MH, NT])
        gcol = sb("gcol", [P, 4, NT, ND2])
        decay = sb("decay", [P, ND2, NT])
        m_start = sb("m_start", [ND2, NT + 1])
        dec8 = sb("dec8", [ND2, NT])
        dblk = sb("dblk", [ND2, ND2, NT])
        den = sb("den", [P, 2, NT])
        gate_w = sb("gate_w", [P, ND, 16])
        gate_wh, gate_wl = sb("gate_high", [P, ND, GF + ND2], F32R), sb("gate_low", [P, ND, GF + ND2], F32R)
        iw = sb("iw", [P, NT, IH])
        top8 = sb("top8", [P, 8])
        smax = sb("smax", [P, 3, NT])
        ssum = sb("ssum", [P, 3, NT])
        pool_w = sb("pool_w", [P, 2, P])
        main_kb = 108
        main = sb("main", [P, int(main_kb * 256)])

        def at(kb, *shape, parts=P):
            n = int(np.prod(shape))
            o = int(round(kb * 256))
            assert o + n <= main_kb * 256, (kb, shape)
            v = main[0:parts, o:o + n]
            if len(shape) == 2:
                v = v.rearrange("p (a b) -> p a b", b=shape[1])
            if len(shape) == 3:
                v = v.rearrange("p (a b c) -> p a b c", b=shape[1], c=shape[2])
            return v

        spec = [[at(16 * q + 8 * c, NT, S) for c in range(2)] for q in range(2)]
        dft_out = at(32, 2, NF, S)
        dft_in = at(40, 2, NT, S // 2)
        tap_sum = [at(48, NT, S), at(64, NT, S)]
        tap_dif = [at(56, NT, S), at(72, NT, S)]
        sig = [at(48, NT, S), at(56, NT, S), at(64, NT, S)]
        r_e, r_lf = (at(72 + 2 * n, S, parts=ND2) for n in range(2))
        wave_tmp = [at(76 + 2 * n, S) for n in range(2)]
        conv_buf = [at(80 + 2 * n, S) for n in range(8)]
        conv = {n: conv_buf[n % 8 if n >= 8 else (n + 4) % 8] for n in range(NCT)}
        proj = x[:, 0:2, :].rearrange("p a b -> p (a b)").rearrange("p (n c) -> p n c", n=4)
        kT, qT = at(80, MH, S), at(88, MH, S)
        r_den, r_in, r_w, r_m = (at(96 + 2 * n, S, parts=ND2) for n in range(4))
        wave = [at(96 + 2 * n, S) for n in range(4)]
        filt_w4, window, window_b = at(0, 2 * S * 2, parts=FHID), at(16, NT, S), at(24, S)
        hidden = at(26, S, parts=FHID)
        taps_b = [at(28 + 2 * n, S) for n in range(2)]
        sin_arg, sin_turn = at(48, S, parts=FHID), at(50, S, parts=FHID)
        zT = at(52, S, parts=EMB)
        filt_w = [at(54, FHID, parts=EMB), at(54.25, FHID, parts=FHID), at(54.5, FHID, parts=FHID)]
        colrows, frows = at(55, P, parts=N_ROWS), at(55.5, FHID, parts=6)
        xn_first = at(80, NT, D)
        turned = [at(96 + 2 * n, S) for n in range(4)]
        v1 = at(0, NT, MH * (P + 1)).rearrange("p t (h c) -> p t h c", h=MH)
        ktok = [at(52 + 2 * n, NT, P) for n in range(2)]
        kw = [[[at(kb + 1.5 * d + 0.5 * c, P) for c in range(3)] for d in range(2)] for kb in (104, 48)]
        wts = [[at(kb + 2 * d, NT, P) for d in range(2)] for kb in (8.25, 32)]
        state = [[at(kb + 1.75 * d, 3, P + 1) for d in range(2)] for kb in (12.25, 36)]
        inter = [at(kb, NT, P + 1) for kb in (16, 39.5)]
        nd = [at(kb, NT, P + 1) for kb in (18.25, 41.75)]
        hm = at(24, NT, HALF)
        o_gate = x[:, 0:2, :].rearrange("p a b -> p (a b)").rearrange("p (t c) -> p t c", t=NT)
        x_rows = x[0:ND2, 2:4, :].rearrange("p a b -> p (a b)").rearrange("p (t c) -> p t c", c=S)
        r_a, r_b, r_i, r_f = (x_rows[:, n, :] for n in range(4))
        sq_h, sq_m = at(96, NT, HALF), at(72, NT, HALF)
        act = at(0, NFF, S)
        xn_mlp = at(0, NT, D)
        mixed = at(80, NT, D)
        relu = [at(96 + 2 * n, S) for n in range(4)]
        junk = [at(kb, 4, 512) for kb in (56, 48, 48, 64, 64, 64)]
        iqT, ikT = at(0, 2, S), at(4, S)
        score, work = at(6, 3, S), at(12, 3, S)
        rdot = [at(18 + 2 * n, S) for n in range(2)]
        qkT = {"fq": at(22, 3, S), "fk": at(28, 3, S), "dq": at(34, 3, S), "dk": at(40, 3, S)}
        vtok = {"f": at(46, NT, AW), "d": at(52, NT, AW)}
        gtok = {"f": at(58, NT, AW), "d": at(22, NT, AW)}
        otok = {"f": at(64, NT, AW), "d": at(46, NT, AW)}
        prob = [at(70 + 5 * n, 10 * P) for n in range(3)]
        probT = [at(85 + 5 * n, 10, P) for n in range(2)]
        nf_bc = [at(95 + 2 * n, S) for n in range(2)]
        f_f, f_a, f_n = (at(99 + 2 * n, S, parts=AH) for n in range(3))
        pvT, pgT = at(12, 2, S), at(16, 2, S)
        win = [at(28 + 2 * n, S) for n in range(3)] + [at(0, S)]
        inv_count = at(2, 2, S)
        pooled = [at(99 + 2 * n, S) for n in range(2)]

        ps = [ctx.enter_context(nc.psum_tensor(f"bank{n}", [P, 512], F32)) for n in range(8)]

        bank_full = [sem(f"bank_full{n}") for n in range(8)]
        bank_free = [sem(f"bank_free{n}") for n in range(8)]
        raw_loaded = [sem(f"raw_loaded{n}") for n in range(2)]
        high_ready, split_ready = sem("high_ready"), sem("split_ready")
        piece_used = sem("piece_used")
        xh_ready, xl_ready = sem("xh_ready"), sem("xl_ready")
        act_high, act_split = sem("act_high"), sem("act_split")
        (ld_cols, ld_masks, ld_fcols, ld_filter, ld_filt_w4, ld_window, ld_dft, ld_rows, ld_gate, ld_fb, ld_mix_post,
         ld_mlp_post, ld_final, ld_pool, ld_count, stored) = (sem("ld_" + n) for n in (
             "cols masks fcols filter filt_w4 window dft rows gate fb mix_post mlp_post final pool count stored").split())
        dve_step, act_step, pool_step = sem("dve_step"), sem("act_step"), sem("pool_step")
        consts_set, v1_ones = sem("consts_set"), sem("v1_ones")
        ld_x = [sem(f"ld_x{t}") for t in range(NT)]
        sumsq_ready = [sem(f"sumsq_ready{s}") for s in range(6)]
        rstd_ready = [sem(f"rstd_ready{s}") for s in range(6)]
        rstd_h_ready, rstd_m_ready = sem("rstd_h_ready"), sem("rstd_m_ready")
        x_ready, xn_ready = sem("x_ready"), sem("xn_ready")
        sin_arg_ready, hidden_ready, taps_ready = (sem(n) for n in "sin_arg_ready hidden_ready taps_ready".split())
        conv_ready, q_ready, k_silu, k_ready = (sem(n) for n in "conv_ready q_ready k_silu k_ready".split())
        minus_ready, mirror_ready, spec_ready, skip_ready, long_ready = (
            sem(n) for n in "minus_ready mirror_ready spec_ready skip_ready long_ready".split())
        gate_w_ready, gate_abs, softplus_ready, exp_args, exps_ready, rows_ready, dblk_ready = (
            sem(n) for n in "gate_w_ready gate_abs softplus_ready exp_args exps_ready rows_ready dblk_ready".split())
        kw_ready, first_state, p_ready, h_ready = (sem(n) for n in "kw_ready first_state p_ready h_ready".split())
        sq_h_ready, gsum_h_ready, yn_h_ready = (sem(n) for n in "sq_h_ready gsum_h_ready yn_h_ready".split())
        gated, sumsq_m_ready, yn_m_ready = sem("gated"), sem("sumsq_m_ready"), sem("yn_m_ready")
        act_ready = sem("act_ready")
        rdot_used = sem("rdot_used")
        sel_ready = sem("sel_ready")
        fgate_abs, fsoft_ready, nf_ready = sem("fgate_abs"), sem("fsoft_ready"), sem("nf_ready")
        smax_ready, prob_ready, og_ready = (sem(n) for n in "smax_ready prob_ready og_ready".split())
        win_ready, pool_w_ready = sem("win_ready"), sem("pool_w_ready")
        out_ready = sem("out_ready")

        def full(eng, name):
            b, k = BANK[name]
            eng.wait_ge(bank_full[b], k + 1)
            return ps[b]

        def free(ins, name):
            return ins.then_inc(bank_free[BANK[name][0]], 1)

        def taken(eng, name):
            b, k = BANK[name]
            eng.wait_ge(bank_free[b], k + 1)

        CONV = {n: (n - 8) % NCT + 1 for n in range(NCT)}
        counted = np.cumsum([n % 4 < 3 if not UP <= n < DOWN + NFF else DOWN <= n < DOWN + NFF - 2
                             for n in range(4 * len(GROUP_ORDER) + 2 * NFF)]).tolist()

        def used(eng, n):
            if UP <= n < DOWN:
                full(eng, ("ff1", n - UP))
            elif DOWN + NFF - 2 <= n < DOWN + NFF:
                full(eng, ("ff2", 2 * NT - 1))
            elif DOWN <= n < DOWN + NFF or n % 4 < 3:
                eng.wait_ge(piece_used, counted[n])
            else:
                g = [g for g in GROUP_ORDER if PIECE[g] == n - 3][0]
                full(eng, GROUPS[g][3][-1][0])

        def piece_shape(n):
            if UP <= n < DOWN + NFF:
                return raw[:, n // 2 % 2, n % 2 * D:(n % 2 + 1) * D], [w[:, n % 2, :] for w in (wh, wl)]
            cols = [GROUPS[g][2] for g in GROUP_ORDER if PIECE[g] <= n < PIECE[g] + 4][0]
            return (raw[:, n // 2 % 2, 0:4 * cols].rearrange("p (k c) -> p k c", k=4)[:, n % 2 * 2:n % 2 * 2 + 2, :],
                    [w[:, n % 2, 0:2 * cols].rearrange("p (k c) -> p k c", k=2) for w in (wh, wl)])

        def low_part(eng, n):
            src, (hi, lo) = piece_shape(n)
            eng.wait_ge(high_ready, n + 1)
            eng.tensor_tensor(lo, src, hi.bitcast(F32), ALU.subtract).then_inc(split_ready, 1)

        XT_ORDER = [("nT", 0, t, half) for t in range(NT) for half in range(2)]
        XT_ORDER += [("yT", j) for j in (4, 5, 6, 7, 0, 1, 2, 3)]
        XT_ORDER += [("nT", s, t, half) for s in (1, 2) for t in range(NT) for half in range(2)]
        XT_ORDER += [("mix_pool", j) for j in range(PW // P)] + [("mT", j) for j in (3, 4, 5, 0, 1, 2)]
        XH = {name: n + 1 for n, name in enumerate(XT_ORDER)}
        XL = {name: n + 1 for n, name in enumerate(nm for nm in XT_ORDER if nm[0] in ("nT", "mix_pool"))}

        def stepper(eng, step):
            count = [0]

            def done(ins):
                count[0] += 1
                ins.then_inc(step, 1)
                eng.wait_ge(step, count[0])
            return done

        def scol(row, n=1):
            return colv[:, row:row + n]

        NORMS = {0: (ROW_MIX_PRE, 0, xn_first), 1: (ROW_MLP_PRE, 2, xn_mlp), 2: (ROW_NORM2, 4, mixed)}
        x_tok = a["x"].rearrange("b (t p) d -> p (b t) d", p=P)
        out_tok = out.rearrange("b (t p) d -> p (b t) d", p=P)

        def vec(name, n):
            return a[name].rearrange("(r p) -> r p", p=P) if n else a[name]

        group_at = {g: n for n, g in enumerate(GROUP_ORDER)}
        block = ctx.enter_context(nc.Block())

        @block.sync
        def _(sp):
            def load_unit(u, parts):
                if u >= 2:
                    sp.wait_ge(split_ready, 2 * u - 2)
                for to, source in parts:
                    sp.dma_start(to, source).then_inc(raw_loaded[u % 2], 16)

            def weights(g):
                weight, c0, n, tiles = GROUPS[g]
                src = a[weight] if weight[-2:] != "_2" else a[weight].rearrange("l k n -> (l k) n")
                src = src.rearrange("(k p) n -> p k n", p=P)[:, :, c0:c0 + n]
                ks = K_ORDER.get(g, range(ND))
                for half in range(2):
                    u = PIECE[g] // 2 + half
                    to = raw[:, u % 2, 0:4 * n].rearrange("p (k c) -> p k c", k=4)
                    load_unit(u, [(to[:, 2 * i:2 * i + 2, :], src[:, ks[4 * half + 2 * i]:ks[4 * half + 2 * i] + 2, :])
                                  for i in range(2)])

            sp.dma_start(masks[:, :, :], a["c_masks"].rearrange("m p n -> p m n")).then_inc(ld_masks, 16)
            for t in range(NT):
                sp.dma_start(x[:, t, :], x_tok[:, t, :]).then_inc(ld_x[t], 16)
            for name, row in (("norm_mix_pre", ROW_MIX_PRE), ("conv_b", ROW_CONV_B), ("norm_mlp_pre", ROW_MLP_PRE),
                              ("mlstm_norm_w", ROW_MLSTM_W), ("hyena_norm_w", ROW_HYENA_W), ("norm_g_2", ROW_NORM2),
                              ("pool_scale_2", ROW_POOL)):
                src = a[name] if name[-2:] != "_2" else a[name].rearrange("l n -> (l n)")
                src = src.rearrange("(r p) -> r p", p=P)
                sp.dma_start(colrows[row:row + src.shape[0], :], src).then_inc(ld_cols, 16)
            sp.dma_start(colrows[0:3 * NCT, :], a["conv_w"].rearrange("w (r p) -> (w r) p", p=P)).then_inc(ld_cols, 16)
            for n in range(3):
                sp.dma_start(frows[n:n + 1, :], a[f"filt_b{n + 1}"].rearrange("(a n) -> a n", a=1)).then_inc(ld_fcols, 16)
            sp.dma_start(frows[3:6, :], a["filt_freq"]).then_inc(ld_fcols, 16)
            sp.dma_start(zT, a["c_z"]).then_inc(ld_filter, 16)
            for n in range(3):
                sp.dma_start(filt_w[n], a[f"filt_w{n + 1}"]).then_inc(ld_filter, 16)
            sp.dma_start(gate_w[:, :, :], a["w_in"].rearrange("(k p) n -> p k n", p=P)[:, :, OFF_GATE:OFF_GATE + 16])\
              .then_inc(ld_gate, 16)
            weights("hv")
            sp.dma_start(filt_w4, a["filt_w4"]).then_inc(ld_filt_w4, 16)
            sp.dma_start(window, a["c_window"].rearrange("(t p) c -> p t c", p=P)).then_inc(ld_window, 16)
            sp.dma_start(window_b, a["c_window_b"]).then_inc(ld_window, 16)
            for c in range(2):
                sp.dma_start(dft_in[:, c], a["c_dft_in"][c].rearrange("(t p) f -> p t f", p=P)).then_inc(ld_dft, 16)
            sp.dma_start(rows_c[:, :], a["c_rows"]).then_inc(ld_rows, 16)
            for kind in range(2):
                for d in range(2):
                    o = (2 * d + kind) * MH
                    sp.dma_start(gbias[d * MH:(d + 1) * MH, kind:kind + 1],
                                 a["b_gates"][o:o + MH].rearrange("(r o) -> r o", o=1)).then_inc(ld_rows, 16)
            sp.dma_start(fbias[:, :], a["fox_bf_2"].rearrange("l (r o) -> (l r) o", o=1)).then_inc(ld_rows, 16)
            for c in range(2):
                sp.dma_start(dft_out[:, c], a["c_dft_out"][c].rearrange("(f p) t -> p f t", p=P)).then_inc(ld_dft, 16)
            sp.dma_start(row_bc[:, :], a["filt_bias"].rearrange("o c -> (o c)").partition_broadcast(P)).then_inc(ld_fb, 16)

            for g in GROUP_ORDER[1:7]:
                weights(g)
            weights("out0")
            sp.wait_ge(long_ready, 2 * NT)
            sp.wait_ge(skip_ready, 2 * NT)
            sp.dma_start(row_bc[:, :], a["norm_mix_post"].partition_broadcast(P)).then_inc(ld_mix_post, 16)
            sp.wait_ge(gated, MH)
            full(sp, ("bc", MH - 1, 1))
            for t in range(NT):
                sp.dma_start(x[:, t, :], x_tok[:, t, :]).then_inc(ld_x[t], 16)
            weights("out1")
            w_up = a["w_mlp_in"].rearrange("(k p) n -> p k n", p=P)
            with sp.Fori(0, NFF // 4) as i:
                for j in range(2):
                    sp.wait_ge(split_ready, 4 * i + (UP + 2 * j - 2))
                    for c in range(2):
                        sp.dma_start(raw[:, j, c * D:(c + 1) * D].rearrange("p (k n) -> p k n", k=ND),
                                     w_up[:, :, bass.ds(i * 512 + (2 * j + c) * P, P)]).then_inc(raw_loaded[j], 16)
            w_down = a["w_mlp_out"].rearrange("(f p) n -> f p n", p=P)
            for f in range(0, NFF, 2):
                u = (DOWN + f) // 2
                load_unit(u, [(raw[:, u % 2, i * D:(i + 1) * D], w_down[f + i]) for i in range(2)])
            sp.wait_ge(x_ready, 2 * NT)
            sp.dma_start(row_bc[:, :], a["norm_mlp_post"].partition_broadcast(P)).then_inc(ld_mlp_post, 16)
            weights("index")
            weights("fq")
            sp.wait_ge(x_ready, 4 * NT)
            sp.dma_start(row_bc[:, :], a["final_g_2"].partition_broadcast(P)).then_inc(ld_final, 16)
            sp.wait_ge(pool_w_ready, 1)
            for j in range(PW // P):
                for n in range(2):
                    sp.dma_start(pool_w[n * HD:(n + 1) * HD, j, n * HD:(n + 1) * HD], a["pool_w_2"][0, 2 * j + n])\
                      .then_inc(ld_pool, 16)
            for g in ("fk", "fg", "fv"):
                weights(g)
            full(sp, ("ix", NT - 1, IH - 1))
            sp.dma_start(inv_count, a["c_inv_count"].rearrange("(j p) s -> p j s", p=P)).then_inc(ld_count, 16)
            for g in GROUP_ORDER[group_at["dq"]:]:
                weights(g)
            for t in range(NT):
                sp.wait_ge(out_ready, t + 1)
                sp.dma_start(out_tok[:, t, :], mixed[:, t, :]).then_inc(stored, 16)
            sp.wait_ge(stored, 16 * NT)

        @block.tensor
        def _(pe):
            order = psum_order()
            at_tile = [0]

            def tile(name):
                assert order[at_tile[0]] == name, (order[at_tile[0]], name)
                at_tile[0] += 1
                b, k = BANK[name]
                if k:
                    pe.wait_ge(bank_free[b], k)
                return ps[b]

            def made(ins, name):
                ins.then_inc(bank_full[BANK[name][0]], 1)

            def product(o, left, right, start, stop):
                (lh, ll), (rh, rl) = left, right
                pe.matmul(o, lh, rh, start=start, stop=False)
                pe.matmul(o, lh, rl, start=False, stop=False)
                return pe.matmul(o, ll, rh, start=False, stop=stop)

            def project(g, pieces=range(4)):
                ks = K_ORDER.get(g, range(ND))
                for i in pieces:
                    n = PIECE[g] + i
                    pe.wait_ge(split_ready, n + 1)
                    w = piece_shape(n)[1]
                    for name, kind, c0, cols in GROUPS[g][3]:
                        if i == 0:
                            tile(name)
                        bank = ps[BANK[name][0]]
                        for kk in range(2):
                            k = ks[2 * i + kk]
                            part = [v[:, kk, c0:c0 + cols] for v in w]
                            if kind == "ch":
                                o, left, right = bank[0:cols, :], part, (xh[:, k, :], xl[:, k, :])
                            else:
                                tok = slice(int(kind[3:]) * P, (int(kind[3:]) + 1) * P)
                                o, left, right = bank[:, 0:cols], (xh[:, k, tok], xl[:, k, tok]), part
                            mm = product(o, left, right, i + kk == 0, i == 3 and kk == 1)
                        if i == 3:
                            made(mm, name)
                    if i < 3:
                        mm.then_inc(piece_used, 1)

            def project_first(g):
                for tokens in (range(NT - 1), range(NT - 1, NT)):
                    cols = slice(tokens[0] * P, (tokens[-1] + 1) * P)
                    wait_x([("nT", 2, t, half) for t in tokens for half in range(2)])
                    for i in range(2):
                        n = PIECE[g] + i
                        pe.wait_ge(split_ready, n + 1)
                        w = piece_shape(n)[1]
                        for name, kind, c0, width in GROUPS[g][3]:
                            if i == 0 and tokens[0] == 0:
                                tile(name)
                            bank = ps[BANK[name][0]]
                            for kk in range(2):
                                k = 2 * i + kk
                                part = [v[:, kk, c0:c0 + width] for v in w]
                                if kind == "ch":
                                    mm = product(bank[0:width, cols], part, (xh[:, k, cols], xl[:, k, cols]), k + tokens[0] == 0, False)
                                elif int(kind[3:]) in tokens:
                                    tok = slice(int(kind[3:]) * P, (int(kind[3:]) + 1) * P)
                                    mm = product(bank[:, 0:width], (xh[:, k, tok], xl[:, k, tok]), part, k == 0, False)
                        if tokens[0]:
                            mm.then_inc(piece_used, 1)
                project(g, (2, 3))

            def wait_x(names):
                for name in names:
                    if name in XL:
                        pe.wait_ge(xl_ready, XL[name])
                    else:
                        taken(pe, name)

            def early(g):
                wait_x([CHANNELS[g][k] for k in K_ORDER[g][:2 * EARLY[g]]])
                project(g, range(EARLY[g]))

            def late(g):
                wait_x([CHANNELS[g][k] for k in K_ORDER[g][2 * EARLY[g]:]])
                project(g, range(EARLY[g], 4))

            def turn_norm(s, t):
                pe.wait_ge(xn_ready, NT * s + t + 1)
                xn = NORMS[s][2]
                for half in range(2):
                    o = tile(("nT", s, t, half))
                    for d in range(4):
                        mm = pe.transpose(o[:, d * P:(d + 1) * P], xn[:, t, (4 * half + d) * P:(4 * half + d + 1) * P], ident)
                    made(mm, ("nT", s, t, half))

            def wait_norm(s):
                wait_x([("nT", s, t, half) for t in range(NT) for half in range(2)])

            pe.wait_ge(ld_masks, 16)
            pe.wait_ge(ld_cols, 16 * 8)
            made(pe.transpose(tile(("cols",))[:, 0:N_ROWS], colrows, ident[0:N_ROWS, 0:N_ROWS]), ("cols",))
            turn_norm(0, 0)
            turn_norm(0, 1)
            pe.wait_ge(ld_fcols, 16 * 4)
            made(pe.transpose(tile(("fcols",))[0:FHID, 0:6], frows, ident[0:6, 0:6]), ("fcols",))
            pe.wait_ge(ld_filter, 16 * 4)
            made(pe.matmul(tile(("f", 0))[0:FHID, :], filt_w[0], zT, start=True, stop=True), ("f", 0))
            turn_norm(0, 2)
            turn_norm(0, 3)
            pe.wait_ge(hidden_ready, 1)
            made(pe.matmul(tile(("f", 1))[0:FHID, :], filt_w[1], hidden, start=True, stop=True), ("f", 1))
            wait_norm(0)
            pe.wait_ge(gate_w_ready, 4)
            o = tile(("gate",))
            for k in range(ND):
                mm = product(o[0:GF + ND2, :], (gate_wh[:, k, :], gate_wl[:, k, :]), (xh[:, k, :], xl[:, k, :]),
                             k == 0, k == ND - 1)
            made(mm, ("gate",))
            pe.wait_ge(hidden_ready, 2)
            made(pe.matmul(tile(("f", 2))[0:FHID, :], filt_w[2], hidden, start=True, stop=True), ("f", 2))
            project("hv")
            pe.wait_ge(hidden_ready, 3)
            pe.wait_ge(ld_filt_w4, 16)
            for q in range(2):
                for t in range(NT):
                    for d in range(2):
                        j = 2 * d + q
                        made(pe.matmul(tile(("ft", q, t, d))[:, :], hidden[:, t * P:(t + 1) * P],
                                       filt_w4[:, j * HALF:(j + 1) * HALF], start=True, stop=True), ("ft", q, t, d))
            def transform(name, c, f, odd, source):
                o = tile(name)
                for t in (2 * odd, 2 * odd + 1):
                    mm = pe.matmul(o[:, :], dft_in[:, c, t, f * P:(f + 1) * P], source[:, t, :],
                                   start=(t == 2 * odd), stop=(t == 2 * odd + 1))
                made(mm, name)

            pe.wait_ge(ld_dft, 64)
            for q in range(2):
                pe.wait_ge(taps_ready, NT * (q + 1))
                for c in range(2):
                    for f in range(NF):
                        for odd in range(2):
                            transform(("K", q, c, f, odd), c, f, odd, (tap_sum, tap_dif)[c][q])
            def turn_conv(lo):
                for n in range(lo, lo + 4):
                    pe.wait_ge(conv_ready, CONV[n])
                    o = tile(("cvT", n))
                    for t in range(NT):
                        src = conv[n].rearrange("p (m two) -> p two m", two=2)[:, t // NF, (t % NF) * P:(t % NF + 1) * P]
                        mm = pe.transpose(o[:, t * P:(t + 1) * P], src, ident)
                    made(mm, ("cvT", n))

            project("hx1")
            turn_conv(8)
            project("hx2")
            turn_conv(12)
            project("mq")
            turn_conv(16)

            def spectrum(q):
                for n in range(8 + 4 * q, 12 + 4 * q):
                    taken(pe, ("cvT", n))
                if q:
                    pe.wait_ge(long_ready, NT)
                for f in range(NF):
                    for c in range(2):
                        for odd in range(2):
                            transform(("US"[c], q, f, odd), c, f, odd, sig[q])

            def back(q):
                pe.wait_ge(spec_ready, NF * (q + 1))
                for t in range(NT):
                    o = tile(("y", q, t))
                    for c in range(2):
                        for f in range(NF):
                            k = f + NF * ((t // NF + c) % 2)
                            mm = pe.matmul(o[:, :], dft_out[:, c, f, t * P:(t + 1) * P], spec[q][1 - c][:, k, :],
                                           start=(c + f == 0), stop=(c == 1 and f == NF - 1))
                    made(mm, ("y", q, t))

            spectrum(0)
            project("mk")
            back(0)

            pe.wait_ge(rows_ready, 1)
            o = tile(("gcol",))
            for n, row in enumerate((r_i, r_a, r_b, r_lf)):
                for c in range(NT):
                    k = (n * NT + c) * ND2
                    mm = pe.transpose(o[:, k:k + ND2], row[:, c * P:(c + 1) * P], ident8)
            made(mm, ("gcol",))
            pe.wait_ge(dblk_ready, 1)
            made(pe.matmul(tile(("decay",))[:, 0:ND2 * NT], ones8[:, :], dblk[:, :, :].rearrange("k r c -> k (r c)"),
                           start=True, stop=True), ("decay",))

            def turn_keys(h):
                o = tile(("kt", h))
                pe.wait_ge(k_ready, h + 1)
                for c in range(NT):
                    mm = pe.transpose(o[:, c * P:(c + 1) * P], kT[:, h, c * P:(c + 1) * P], ident)
                made(mm, ("kt", h))

            def head_begin(h):
                o = tile(("s", h))
                pe.wait_ge(q_ready, h + 1)
                for c in range(NT):
                    cs = slice(c * P, (c + 1) * P)
                    mm = pe.matmul(o[:, cs], kT[:, h, cs], qT[:, h, cs], start=True, stop=True)
                made(mm, ("s", h))
                for d in range(2):
                    r = d * MH + h
                    o = tile(("bc", h, d))
                    pe.matmul(o[:, :], ident8[:, r:r + 1].broadcast_to([ND2, P]), r_f, start=True, stop=False)
                    cut = (cut_after, causal)[d].rearrange("p (o l) -> p o l", o=1).broadcast_to([P, NT, P])
                    made(pe.matmul(o[:, :], ident, cut, start=False, stop=True), ("bc", h, d))
                    o = tile(("up", h, d))
                    pe.wait_ge(kw_ready, 2 * h + d + 1)
                    for t in range(NT):
                        taken(pe, ("mv", t))
                    for c in range(3):
                        n = c if d == 0 else NT - 1 - c
                        mm = pe.matmul(o[:, c * (P + 1):(c + 1) * (P + 1)], kw[h % 2][d][c], v1[:, n, h, :], start=True, stop=True)
                    made(mm, ("up", h, d))

            def head_end(h):
                for d in range(2):
                    o = tile(("in", h, d))
                    taken(pe, ("up", h, d))
                    for c in range(1, NT):
                        n = c if d == 0 else NT - 1 - c
                        mm = pe.matmul(o[:, (c - 1) * (P + 1):c * (P + 1)], qT[:, h, n * P:(n + 1) * P], state[h % 2][d][:, c - 1, :],
                                       start=True, stop=True)
                    made(mm, ("in", h, d))
                    if d == 0:
                        pe.wait_ge(p_ready, h + 1)
                    else:
                        taken(pe, ("s", h))
                    for m in range(2):
                        o = tile(("nd", h, d, m))
                        for j in range(2):
                            n = 2 * m + j
                            mm = pe.matmul(o[:, j * (P + 1):(j + 1) * (P + 1)], wts[h % 2][d][:, n, :], v1[:, n, h, :],
                                           start=True, stop=True)
                        made(mm, ("nd", h, d, m))

            def turn_out(j):
                if j < MH:
                    pe.wait_ge(yn_m_ready, j + 1)
                else:
                    pe.wait_ge(yn_h_ready, NT)
                source = hm if j < MH else sig[2]
                o = tile(("yT", j))
                for t in range(NT):
                    to = o[:, t * P:(t + 1) * P]
                    if j >= MH:
                        to = o[:, :].rearrange("p (m two) -> p two m", two=2)[:, t // NF, t % NF * P:(t % NF + 1) * P]
                    mm = pe.transpose(to, source[:, t, (j % MH) * P:(j % MH + 1) * P], ident)
                made(mm, ("yT", j))

            turn_keys(0)
            project("mv")
            head_begin(0)
            spectrum(1)
            turn_keys(1)
            project("mo")
            back(1)
            head_begin(1)
            turn_keys(2)
            head_end(0)
            head_begin(2)
            turn_keys(3)
            head_end(1)
            head_begin(3)
            head_end(2)
            for j in range(MH, ND):
                turn_out(j)
            turn_out(0)
            head_end(3)
            turn_out(1)
            early("out0")
            for j in (2, 3):
                turn_out(j)
            late("out0")
            project("out1")

            for t in range(NT):
                turn_norm(1, t)
            first = [BANK[("ff1", f)] for f in range(8)]
            at_tile[0] += NFF


            def up_part(j, cols):
                b = first[j][0]
                w = [v.rearrange("p (k n) -> p k n", k=ND) for v in piece_shape(UP + j)[1]]
                for k in range(ND):
                    mm = product(ps[b][:, cols], [v[:, k, :] for v in w], (xh[:, k, cols], xl[:, k, cols]), k == 0, k == ND - 1)
                return mm

            for tokens in (range(NT - 1), range(NT - 1, NT)):
                wait_x([("nT", 1, t, half) for t in tokens for half in range(2)])
                for j in range(2):
                    b, k = first[j]
                    pe.wait_ge(split_ready, UP + j + 1)
                    pe.wait_ge(bank_free[b], k)
                    mm = up_part(j, slice(tokens[0] * P, (tokens[-1] + 1) * P))
                    if tokens[0]:
                        mm.then_inc(bank_full[b], 1)
            for j in range(2, 8):
                b, k = first[j]
                pe.wait_ge(split_ready, UP + j + 1)
                pe.wait_ge(bank_free[b], k)
                up_part(j, slice(0, S)).then_inc(bank_full[b], 1)
            with pe.Fori(1, NFF // 8) as i:
                for j in range(8):
                    b, k = first[j]
                    pe.wait_ge(split_ready, 8 * i + (UP + j + 1))
                    pe.wait_ge(bank_free[b], k + i)
                    up_part(j, slice(0, S)).then_inc(bank_full[b], 1)
            down = [tile(("ff2", n)) for n in range(2 * NT)]

            def down_part(f, n):
                t, half = n // 2, n % 2
                w = piece_shape(DOWN + f)[1]
                tok = slice(t * P, (t + 1) * P)
                return product(down[n][:, :], (xh[:, f % 8, tok], xl[:, f % 8, tok]), [v[:, half * 512:(half + 1) * 512] for v in w],
                               f == 0, f == NFF - 1)

            for f in range(NFF):
                pe.wait_ge(split_ready, DOWN + f + 1)
                pe.wait_ge(act_split, f + 1)
                if f < NFF - 2:
                    for n in range(2 * NT):
                        mm = down_part(f, n)
                    mm.then_inc(piece_used, 1)
            for n in range(2 * NT):
                for f in (NFF - 2, NFF - 1):
                    mm = down_part(f, n)
                made(mm, ("ff2", n))

            for t in range(NT):
                turn_norm(2, t)
            project_first("index")
            for n in (("iq", 0), ("iq", 1), ("ik", 0)):
                taken(pe, n)
            for i, g in enumerate(("fq", "fk", "fg"), 1):
                for h in range(IH):
                    o = tile(("ix", i, h))
                    r = ID * (h % 4)
                    made(pe.matmul(o[:, 0:(i + 1) * P], iqT[r:r + ID, h // 4, i * P:(i + 1) * P],
                                   ikT[r:r + ID, 0:(i + 1) * P], start=True, stop=True), ("ix", i, h))
                project(g)
            project("fv")

            def scores(kind, h):
                if kind == "f":
                    pe.wait_ge(nf_ready, 1)
                    made(pe.matmul(tile(("nF", h))[:, :], ident8[0:AH, h:h + 1].broadcast_to([AH, P]), f_n, start=True, stop=True), ("nF", h))
                if h % 2 == 0:
                    taken(pe, (kind + "q", h // 2))
                    taken(pe, (kind + "k", h // 2))
                r = HD * (h % 2)
                q, k = qkT[kind + "q"], qkT[kind + "k"]
                for i in range(NT):
                    o = tile((kind + "s", h, i))
                    mm = pe.matmul(o[:, 0:(i + 1) * P], q[r:r + HD, h // 2, i * P:(i + 1) * P],
                                   k[r:r + HD, h // 2, 0:(i + 1) * P], start=True, stop=(kind == "d"))
                    if kind == "f":
                        mm = pe.matmul(o[:, i * P:(i + 1) * P], ident, causal, start=False, stop=True)
                    made(mm, (kind + "s", h, i))

            def values(n, kind, h):
                pr, pt = prob[n % 3], probT[n % 2]
                at0 = 0
                for i in range(NT):
                    o = tile((kind + "T", h, i))
                    pe.wait_ge(prob_ready, NT * n + i + 1)
                    for s in range(i + 1):
                        mm = pe.transpose(o[:, s * P:(s + 1) * P], pr[:, (at0 + s) * P:(at0 + s + 1) * P], ident)
                    made(mm, (kind + "T", h, i))
                    at0 += i + 1
                if h == 0:
                    for t in range(NT):
                        taken(pe, (kind + "v", t))
                o = tile((kind + "o", h))
                at0 = 0
                for i in range(NT):
                    taken(pe, (kind + "T", h, i))
                    for s in range(i + 1):
                        mm = pe.matmul(o[:, i * HD:(i + 1) * HD], pt[:, at0 + s, :], vtok[kind][:, s, h * HD:(h + 1) * HD],
                                       start=(s == 0), stop=(s == i))
                    at0 += i + 1
                made(mm, (kind + "o", h))

            for n, (kind, h) in enumerate(HEADS):
                scores(kind, h)
                if n >= LAG:
                    values(n - LAG, *HEADS[n - LAG])
                if n in BETWEEN:
                    project(BETWEEN[n])
            for n in range(len(HEADS) - LAG, len(HEADS)):
                values(n, *HEADS[n])
            pe.wait_ge(ld_pool, 16 * 4)
            for j in range(PW // P):
                pe.wait_ge(win_ready, j + 1)
                made(pe.matmul(tile(("mix_pool", j))[:, :], pool_w[:, j, :], win[2 + j], start=True, stop=True),
                     ("mix_pool", j))

            def turn_heads(kind, count, lo):
                pe.wait_ge(og_ready, count)
                for j in range(lo, lo + 3):
                    o = tile(("mT", j))
                    for t in range(NT):
                        mm = pe.transpose(o[:, t * P:(t + 1) * P], otok[kind][:, t, (j - lo) * P:(j - lo + 1) * P], ident)
                    made(mm, ("mT", j))

            turn_heads("f", AH, 3)
            early("fin0")
            turn_heads("d", 2 * AH, 0)
            late("fin0")
            project("fin1")
            assert at_tile[0] == len(order)

        @block.scalar
        def _(ac):
            done = stepper(ac, act_step)

            done_squares = []

            def square(s, half, t, source):
                m = len(done_squares)
                if m >= 4:
                    ac.wait_ge(*done_squares[m - 4])
                ac.activation(junk[s][:, m % 4, :], source, ACT.Square, scale=D ** -0.5, accum_out=sumsq[:, s, half, t:t + 1])\
                  .then_inc(sumsq_ready[s], 1)
                done_squares.append((sumsq_ready[s], 1 + sum(d[0] is sumsq_ready[s] for d in done_squares)))

            def square_x(s, t):
                for half in range(2):
                    if s:
                        ac.wait_ge(x_ready, 2 * NT * (s // 2 - 1) + 2 * t + half + 1)
                    square(s, half, t, x[:, t, half * 512:(half + 1) * 512])

            def normed(s, t):
                _, n, xn = NORMS[s]
                ac.wait_ge(rstd_ready[n], t + 1)
                ac.activation(xn[:, t, :], x[:, t, :], ACT.Copy, scale=rstd[:, n, t:t + 1]).then_inc(xn_ready, 1)

            def take_norm(s, t):
                for half in range(2):
                    name = ("nT", s, t, half)
                    taken(ac, name)
                    v = turned[(XL[name] - 1) % 4].rearrange("p (d n) -> p d n", d=4)
                    ac.activation(xh[:, 4 * half:4 * half + 4, t * P:(t + 1) * P], v, ACT.Copy).then_inc(xh_ready, 1)

            def high(n):
                src, (hi, _) = piece_shape(n)
                ac.wait_ge(raw_loaded[n // 2 % 2], 32 * (n // 4 + 1))
                if n >= 2:
                    used(ac, n - 2)
                ac.activation(hi, src, ACT.Copy).then_inc(high_ready, 1)

            def highs(g, *pieces):
                for i in pieces:
                    high(PIECE[g] + i)

            def renew(s, halves, after=None):
                for step in range(NT + 4):
                    if step < NT:
                        for half, name in halves(step):
                            square(2 * s - 1, half, step, full(ac, name)[:, :])
                    if 1 <= step <= NT:
                        square_x(2 * s, step - 1)
                    if 2 <= step <= NT + 1:
                        normed(s, step - 2)
                    if step == 2 and after:
                        high(after)
                    if step >= 4:
                        take_norm(s, step - 4)

            def sine(n):
                ac.wait_ge(sin_arg_ready, n + 1)
                ac.activation(hidden, sin_arg, ACT.Sin).then_inc(hidden_ready, 1)

            def conv_bias(n):
                if n >= 16:
                    full(ac, ("cvT", n - 8))
                if n < 8:
                    full(ac, ("cvT", n + 12))
                name = ("cv", n)
                o = full(ac, name)[:, :]
                ac.activation(conv[n], o, ACT.Identity, bias=scol(ROW_CONV_B + n), scale=scol(ROW_CONV_W + NCT + n))
                if CONV[n] > 4:
                    ac.wait_ge(conv_ready, CONV[n] - 4)
                else:
                    ac.wait_ge(xn_ready, NT)
                free(ac.activation(proj[:, n % 4, :], o, ACT.Copy), name)

            def take_turned(n):
                name = ("cvT", n)
                q, j = (n - 8) // 4, n % 4
                full(ac, ("K", q if n < 12 else 1, 1, NF - 1, 1))
                free(ac.activation(sig[q][:, :, j * P:(j + 1) * P],
                                   full(ac, name)[:, :].rearrange("p (t c) -> p t c", t=NT), ACT.Copy), name)

            for t in range(NT + 1):
                if t < NT:
                    ac.wait_ge(ld_x[t], 16)
                    square_x(0, t)
                if t >= 1:
                    normed(0, t - 1)
            take_norm(0, 0)
            take_norm(0, 1)
            sine(0)
            take_norm(0, 2)
            take_norm(0, 3)
            sine(1)
            highs("hv", 0, 1)
            sine(2)
            highs("hv", 2, 3)
            highs("hx1", 0, 1)
            for n in range(8, 12):
                conv_bias(n)
            def take_even(o, name):
                free(ac.activation(o, full(ac, name)[:, :], ACT.Copy), name)

            def take_spectrum(q):
                for f in range(NF):
                    if q or f:
                        ac.wait_ge(spec_ready, NF * q + f)
                    for c in range(2):
                        take_even(wave[2 * c], ("US"[c], q, f, 0))

            for q in range(2):
                for c in range(2):
                    for f in range(NF):
                        take_even(spec[q][c][:, f, :], ("K", q, c, f, 0))
            highs("hx1", 2, 3)
            highs("hx2", 0, 1)
            for n in range(12, 16):
                conv_bias(n)
            for n in range(8, 12):
                take_turned(n)
            ac.wait_ge(gate_abs, 1)
            done(ac.activation(r_a, r_a, ACT.Exp, scale=-1.0))
            ac.activation(r_a, r_a, ACT.Ln, bias=one_col[0:ND2, :]).then_inc(softplus_ready, 1)
            highs("hx2", 2, 3)
            highs("mq", 0, 1)
            for n in range(16, 20):
                conv_bias(n)
            for n in range(12, 16):
                take_turned(n)
            ac.wait_ge(exp_args, 1)
            ac.activation(r_den, r_den, ACT.Exp, scale=-1.0).then_inc(exps_ready, 1)
            ac.activation(r_in, r_in, ACT.Exp).then_inc(exps_ready, 1)
            ac.activation(r_w, r_w, ACT.Exp).then_inc(exps_ready, 1)
            ac.activation(dec8[:, :], dec8[:, :], ACT.Exp).then_inc(exps_ready, 1)
            highs("mq", 2, 3)
            highs("mk", 0, 1)
            for n in range(4):
                conv_bias(n)
            for n in range(16, 20):
                take_turned(n)
            take_spectrum(0)
            highs("mk", 2, 3)
            highs("mv", 0, 1)
            for n in range(4, 8):
                conv_bias(n)
            for n in range(8):
                ac.wait_ge(conv_ready, CONV[n])
                if n < 4:
                    ac.activation(qT[:, n, :], conv[n], ACT.Silu).then_inc(q_ready, 1)
                else:
                    ac.activation(kT[:, n - 4, :], conv[n], ACT.Silu).then_inc(k_silu, 1)

            def take_keys(h):
                name = ("kt", h)
                if h < 2:
                    ac.wait_ge(long_ready, NT)
                else:
                    ac.wait_ge(kw_ready, 2 * h - 2)
                free(ac.activation(ktok[h % 2], full(ac, name)[:, :].rearrange("p (c d) -> p c d", c=NT), ACT.Copy), name)

            def head_begin(h):
                taken(ac, ("gcol",))
                for d in range(2):
                    r = d * MH + h
                    name = ("bc", h, d)
                    o = full(ac, name)
                    if h >= 2:
                        full(ac, ("nd", h - 2, d, 1))
                    for c in range(NT):
                        i = ac.activation(wts[h % 2][d][:, c, :], o[:, c * P:(c + 1) * P], ACT.Exp, bias=gcol[:, 0, c, r:r + 1])
                    free(i, name)
                    o = full(ac, ("up", h, d))
                    if h >= 2:
                        full(ac, ("in", h - 2, d))
                    ac.activation(state[h % 2][d][:, 0, :], o[:, 0:P + 1], ACT.Copy).then_inc(first_state, 1)

            def square_head(h):
                ac.wait_ge(gated, h + 1)
                for t in range(NT):
                    ac.activation(sq_m[:, t, h * P:(h + 1) * P], hm[:, t, h * P:(h + 1) * P], ACT.Square, scale=P ** -0.5,
                                  accum_out=sumsq_m[:, h, t:t + 1]).then_inc(sumsq_m_ready, 1)

            def head_end(h):
                for d in range(2):
                    name = ("in", h, d)
                    o = full(ac, name)
                    if d or h >= 2:
                        for m in range(2):
                            taken(ac, ("nd", h, 0, m) if d else ("nd", h - 2, 1, m))
                    for c in range(1, NT):
                        n = c if d == 0 else NT - 1 - c
                        i = ac.activation(inter[h % 2][:, n, :], o[:, (c - 1) * (P + 1):c * (P + 1)], ACT.Copy,
                                          scale=gcol[:, 2, n, d * MH + h:d * MH + h + 1])
                    free(i, name)

            def take_out(j):
                name = ("yT", j)
                row = ROW_MLSTM_W + j if j < MH else ROW_HYENA_W + j - MH
                ac.activation(xh[:, j, :], full(ac, name)[:, :], ACT.Copy, scale=scol(row)).then_inc(xh_ready, 1)

            take_keys(0)
            highs("mv", 2, 3)
            highs("mo", 0, 1)
            ac.wait_ge(v1_ones, 1)
            for t in range(NT):
                name = ("mv", t)
                free(ac.activation(v1[:, t, :, 0:P], full(ac, name)[:, :].rearrange("p (h c) -> p h c", h=MH), ACT.Copy), name)
            head_begin(0)
            take_spectrum(1)
            take_keys(1)
            highs("mo", 2, 3)
            highs("out0", 0, 1)
            ac.wait_ge(xn_ready, NT)
            for t in range(NT):
                name = ("mo", t)
                free(ac.activation(o_gate[:, t, :], full(ac, name)[:, :], ACT.Sigmoid), name)
            head_begin(1)
            take_keys(2)
            head_end(0)
            head_begin(2)
            take_keys(3)
            head_end(1)
            square_head(0)
            head_begin(3)
            head_end(2)
            square_head(1)
            for j in range(MH, ND):
                take_out(j)
            take_out(0)
            head_end(3)
            take_out(1)
            square_head(2)
            highs("out0", 2)
            square_head(3)
            highs("out0", 3)
            take_out(2)
            take_out(3)
            highs("out1", 0, 1)
            for t in range(NT):
                square(1, 0, t, full(ac, ("mx00", t))[:, :])
            highs("out1", 2, 3)
            high(UP)
            renew(1, lambda t: [(1, ("mx01", t))], UP + 1)
            first = [BANK[("ff1", f)] for f in range(8)]
            with ac.Fori(0, NFF // 8) as i:
                for j in range(8):
                    b, k = first[j]
                    ac.wait_ge(bank_full[b], i + (k + 1))
                    ac.wait_ge(act_ready, 8 * i + (j + 1))
                    ac.activation(relu[j % 4], ps[b][:, :], ACT.Relu).then_inc(bank_free[b], 1)
                    src, (hi, _) = piece_shape(UP + j + 2)
                    ac.wait_ge(raw_loaded[(j + 2) // 2 % 2], 64 * i + 32 * ((UP + j + 2) // 4 + 1))
                    ac.activation(hi, src, ACT.Copy).then_inc(high_ready, 1)

            def act_part(f):
                ac.wait_ge(act_ready, 4 + f + 1)
                if f < 8:
                    full(ac, ("ff1", NFF - 1))
                else:
                    used(ac, DOWN + f - 8)
                ac.activation(xh[:, f % 8, :], act[:, f, :], ACT.Copy).then_inc(act_high, 1)

            for f in range(4):
                act_part(f)
            for f in range(NFF):
                if f + 4 < NFF:
                    act_part(f + 4)
                if f + 2 < NFF:
                    high(DOWN + f + 2)
            renew(2, lambda t: [(half, ("ff2", 2 * t + half)) for half in range(2)], PIECE["index"])
            highs("index", 1)
            highs("index", 2, 3)
            highs("fq", 0)
            for j in range(2):
                name = ("iq", j)
                free(ac.activation(iqT[:, j, :], full(ac, name)[:, :], ACT.Copy), name)
            name = ("ik", 0)
            o = full(ac, name)
            for r in range(4):
                i = ac.activation(ikT[r * ID:(r + 1) * ID, :], o[0:ID, :], ACT.Copy)
            free(i, name)

            def relus(i):
                for h in range(IH):
                    n = (i - 1) * IH + h
                    name = ("ix", i, h)
                    o = full(ac, name)
                    if n >= 2:
                        ac.wait_ge(rdot_used, n - 1)
                    free(ac.activation(rdot[n % 2][:, 0:(i + 1) * P], o[:, 0:(i + 1) * P], ACT.Relu), name)

            def take(g):
                for name, kind, _, _ in GROUPS[g][3]:
                    o = full(ac, name)
                    what, j = name
                    if what in ("fq", "dq"):
                        i = ac.activation(qkT[what][:, j, :], o[:, :], ACT.Copy, scale=HD ** -0.5)
                    elif what in ("fk", "dk"):
                        i = ac.activation(qkT[what][:, j, :], o[:, :], ACT.Copy)
                    elif what in ("fv", "dv"):
                        i = ac.activation(vtok[what[0]][:, j, :], o[:, 0:AW], ACT.Copy)
                    elif what in ("fg", "dg"):
                        i = ac.activation(gtok[what[0]][:, j, :], o[:, 0:AW], ACT.Silu)
                    elif what == "pv":
                        ac.wait_ge(sel_ready, NT - 1)
                        i = ac.activation(pvT[:, j, :], o[:, :], ACT.Copy)
                    elif what == "pg":
                        i = ac.activation(pgT[:, j, :], o[:, :], ACT.Silu)
                    else:
                        continue
                    free(i, name)

            highs("fq", 1)
            relus(1)
            highs("fq", 2, 3)
            highs("fk", 0, 1)
            take("fq")
            relus(2)
            highs("fk", 2, 3)
            highs("fg", 0, 1)
            take("fk")
            relus(3)
            highs("fg", 2, 3)
            highs("fv", 0, 1)
            take("fg")
            ac.wait_ge(fgate_abs, 1)
            done(ac.activation(f_a, f_a, ACT.Exp, scale=-1.0))
            ac.activation(f_a, f_a, ACT.Ln, bias=one_col[0:AH, :]).then_inc(fsoft_ready, 1)
            highs("fv", 2, 3)
            highs("dq", 0, 1)
            take("fv")

            def forget_rows(n, h):
                name = ("nF", h)
                if n >= 2:
                    ac.wait_ge(smax_ready, n - 1)
                free(ac.activation(nf_bc[n % 2], full(ac, name)[:, :], ACT.Copy), name)

            def exps(n, kind, h):
                ac.wait_ge(smax_ready, n + 1)
                at0 = 0
                for i in range(NT):
                    w = (i + 1) * P
                    p = prob[n % 3][:, at0 * P:at0 * P + w]
                    ac.activation(p, p, ACT.Exp, bias=smax[:, n % 3, i:i + 1], accum_out=ssum[:, n % 3, i:i + 1])\
                      .then_inc(prob_ready, 1)
                    at0 += i + 1

            def take_probs(n, kind, h):
                at0 = 0
                for i in range(NT):
                    name = (kind + "T", h, i)
                    o = full(ac, name)
                    if n >= 2:
                        k2, h2 = HEADS[n - 2]
                        full(ac, (k2 + "o", h2))
                    free(ac.activation(probT[n % 2][:, at0:at0 + i + 1, :],
                                       o[:, 0:(i + 1) * P].rearrange("p (s c) -> p s c", s=i + 1), ACT.Copy), name)
                    at0 += i + 1

            for n, (kind, h) in enumerate(HEADS):
                if kind == "f":
                    forget_rows(n, h)
                if n >= LAG:
                    take_probs(n - LAG, *HEADS[n - LAG])
                exps(n, kind, h)
                if n in BETWEEN:
                    g = BETWEEN[n]
                    highs(g, 2, 3)
                    highs(GROUP_ORDER[group_at[g] + 1], 0, 1)
                    take(g)
            for n in range(len(HEADS) - LAG, len(HEADS)):
                take_probs(n, *HEADS[n])
            for j in range(PW // P):
                taken(ac, ("mix_pool", j))
                ac.activation(xh[:, j, :], pooled[j], ACT.Copy).then_inc(xh_ready, 1)

            def take_heads(lo):
                for j in range(lo, lo + 3):
                    ac.activation(xh[:, 2 + j, :], full(ac, ("mT", j))[:, :], ACT.Copy).then_inc(xh_ready, 1)

            take_heads(3)
            highs("fin0", 2, 3)
            take_heads(0)
            highs("fin1", 0, 1, 2, 3)
            for half in range(2):
                for t in range(NT):
                    taken(ac, (f"fx{half}", t))
                    square(5, half, t, x[:, t, half * 512:(half + 1) * 512])

        @block.vector
        def _(ve):
            done = stepper(ve, dve_step)

            def take_norm(s, t):
                row = NORMS[s][0]
                for half in range(2):
                    name = ("nT", s, t, half)
                    n = XL[name] - 1
                    weight = scol(row + 4 * half, 4).rearrange("p (d o) -> p d o", o=1).broadcast_to([P, 4, P])
                    if n >= 4:
                        ve.wait_ge(xl_ready, n - 3)
                    free(ve.tensor_tensor(turned[n % 4].rearrange("p (d n) -> p d n", d=4),
                                          full(ve, name)[:, :].rearrange("p (d n) -> p d n", d=4), weight, ALU.mult), name)

            def split_norm(s, t):
                for half in range(2):
                    name = ("nT", s, t, half)
                    v = turned[(XL[name] - 1) % 4].rearrange("p (d n) -> p d n", d=4)
                    at_x = (slice(None), slice(4 * half, 4 * half + 4), slice(t * P, (t + 1) * P))
                    ve.wait_ge(xh_ready, XH[name])
                    ve.tensor_tensor(xl[at_x], v, xh[at_x].bitcast(F32), ALU.subtract).then_inc(xl_ready, 1)

            def lows(g, *pieces):
                for i in pieces:
                    low_part(ve, PIECE[g] + i)

            def split_out(j):
                name = ("yT", j)
                row = ROW_MLSTM_W + j if j < MH else ROW_HYENA_W + j - MH
                o = full(ve, name)
                ve.wait_ge(xh_ready, XH[name])
                free(ve.scalar_tensor_tensor(out=xl[:, j, :], in0=o[:, :], scalar=scol(row), in1=xh[:, j, :].bitcast(F32),
                                             op0=ALU.mult, op1=ALU.subtract), name)

            def sine_arg(n):
                name = ("f", n)
                free(ve.tensor_scalar(sin_arg, full(ve, name)[0:FHID, :], fcol[:, n:n + 1], fcol[:, 3 + n:4 + n],
                                      ALU.add, ALU.mult), name)
                taken(ve, name)
                done(ve.tensor_scalar(sin_turn, sin_arg, 1.0 / (2 * np.pi), MAGIC, ALU.mult, ALU.add))
                done(ve.tensor_scalar(sin_turn, sin_turn, MAGIC, None, ALU.subtract))
                for part in (TWO_PI_HI, TWO_PI_LO):
                    done(ve.scalar_tensor_tensor(out=sin_arg, in0=sin_turn, scalar=-part, in1=sin_arg,
                                                 op0=ALU.mult, op1=ALU.add))
                ve.tensor_scalar(sin_arg, sin_arg, PI, -PI, ALU.min, ALU.max).then_inc(sin_arg_ready, 1)

            free(ve.tensor_copy(colv[:, :], full(ve, ("cols",))[:, 0:N_ROWS]), ("cols",))
            taken(ve, ("cols",))
            take_norm(0, 0)
            take_norm(0, 1)
            split_norm(0, 0)
            split_norm(0, 1)
            free(ve.tensor_copy(fcol[:, :], full(ve, ("fcols",))[0:FHID, 0:6]), ("fcols",))
            taken(ve, ("fcols",))
            sine_arg(0)
            take_norm(0, 2)
            take_norm(0, 3)
            split_norm(0, 2)
            split_norm(0, 3)
            sine_arg(1)
            lows("hv", 0, 1)
            ve.wait_ge(ld_rows, 16 * 6)
            ve.wait_ge(xn_ready, NT)
            o = full(ve, ("gate",))
            ve.tensor_scalar(r_i, o[0:ND2, :], gbias[:, 0:1], None, ALU.add)
            free(ve.tensor_scalar(r_f, o[GF:GF + ND2, :], gbias[:, 1:2], None, ALU.add), ("gate",))
            sine_arg(2)
            lows("hv", 2, 3)
            lows("hx1", 0, 1)

            def short_conv(lo):
                for n in range(lo, lo + 4):
                    taken(ve, ("cv", n))
                    u, c = proj[:, n % 4, :], conv[n]
                    done(ve.scalar_tensor_tensor(out=c[:, 1:S], in0=u[:, 0:S - 1], scalar=scol(ROW_CONV_W + n),
                                                 in1=c[:, 1:S], op0=ALU.mult, op1=ALU.add))
                    ve.scalar_tensor_tensor(out=c[:, 0:S - 1], in0=u[:, 1:S], scalar=scol(ROW_CONV_W + 2 * NCT + n),
                                            in1=c[:, 0:S - 1], op0=ALU.mult, op1=ALU.add).then_inc(conv_ready, 1)

            short_conv(8)
            ve.wait_ge(ld_window, 32)
            n = 0
            for q in range(2):
                for t in range(NT):
                    name = ("ft", q, t, 0)
                    free(ve.tensor_tensor(tap_sum[q][:, t, :], full(ve, name)[:, :], window[:, t, :], ALU.mult), name)
                    name = ("ft", q, t, 1)
                    if n >= 2:
                        ve.wait_ge(taps_ready, n - 1)
                    w = window_b if t == 0 else window[:, t, :]
                    free(ve.tensor_tensor(taps_b[n % 2], full(ve, name)[:, :], w, ALU.mult), name)
                    n += 1
            def add_odd(even, odd, plus, minus, sign):
                taken(ve, even)
                o = full(ve, odd)[:, :]
                a, b = (plus, o) if sign > 0 else (o, plus)
                done(ve.tensor_tensor(minus, a, b, ALU.subtract))
                free(ve.tensor_tensor(plus, plus, o, ALU.add), odd)

            for q in range(2):
                for c in range(2):
                    for f in range(NF):
                        add_odd(("K", q, c, f, 0), ("K", q, c, f, 1), spec[q][c][:, f, :], spec[q][c][:, NF + f, :], 1 - 2 * c)

            def products(q, f):
                n = NF * q + f
                up, um, sp, sm = wave
                for c, (plus, minus) in enumerate(((up, um), (sp, sm))):
                    even, odd = ("US"[c], q, f, 0), ("US"[c], q, f, 1)
                    taken(ve, even)
                    o = full(ve, odd)[:, :]
                    if n:
                        ve.wait_ge(spec_ready, n)
                    a, b = (plus, o) if c == 0 else (o, plus)
                    ve.tensor_tensor(minus, a, b, ALU.subtract).then_inc(minus_ready, 1)
                    ve.wait_ge(minus_ready, 2 * n + c + 1)
                    free(ve.tensor_tensor(plus, plus, o, ALU.add), odd)
                for c in range(2):
                    taken(ve, ("US"[c], q, f, 1))
                k0, k1, k0m, k1m = (spec[q][c][:, i, :] for i in (f, NF + f) for c in range(2))
                for c in range(2):
                    taken(ve, ("K", q, c, f, 1))
                done(ve.tensor_tensor(wave_tmp[0], up, k1, ALU.mult))
                ve.tensor_tensor(k1, sp, k1, ALU.mult)
                done(ve.tensor_tensor(up, up, k0, ALU.mult))
                ve.tensor_tensor(k0, sp, k0, ALU.mult)
                done(ve.tensor_tensor(k1, k1, up, ALU.add))
                done(ve.tensor_tensor(k0, k0, wave_tmp[0], ALU.subtract))
                ve.wait_ge(mirror_ready, n + 1)
                for a, b in ((k1, k1m), (k0, k0m)):
                    done(ve.tensor_tensor(b, a, b, ALU.subtract))
                for a, b in ((k1, k1m), (k0, k0m)):
                    i = ve.scalar_tensor_tensor(out=a, in0=a, scalar=2.0, in1=b, op0=ALU.mult, op1=ALU.subtract)
                i.then_inc(spec_ready, 1)

            def long_conv(q, t):
                ve.wait_ge(skip_ready, NT * q + t + 1)
                name = ("y", q, t)
                g = sig[q + 1][:, t, :]
                z = sig[q][:, t, :]
                for n in range(12, 20):
                    taken(ve, ("cvT", n))
                free(ve.tensor_tensor(z, full(ve, name)[:, :], z, ALU.add), name)
                taken(ve, name)
                ve.tensor_tensor(g, z, g, ALU.mult).then_inc(long_ready, 1)

            lows("hx1", 2, 3)
            lows("hx2", 0)

            def unflip(o, i):
                done(ve.tensor_scalar(o, i, is_f, None, ALU.mult))
                return ve.scalar_tensor_tensor(out=o, in0=i[:, ::-1], scalar=is_b, in1=o, op0=ALU.mult, op1=ALU.add)

            def chunks(r):
                return r.rearrange("k (c l) -> k c l", c=NT)

            taken(ve, ("gate",))
            full(ve, ("K", 1, 1, NF - 1, 1))
            done(unflip(r_e, r_i))
            done(unflip(r_lf, r_f))
            ve.scalar_tensor_tensor(out=r_a, in0=r_lf, scalar=-1.0, in1=r_lf, op0=ALU.mult, op1=ALU.max).then_inc(gate_abs, 1)
            done(ve.tensor_scalar(r_lf, r_lf, 0.0, None, ALU.min))
            lows("hx2", 1)
            short_conv(12)
            lows("hx2", 2)
            ve.wait_ge(softplus_ready, 1)
            done(ve.tensor_tensor(r_lf, r_lf, r_a, ALU.subtract))
            done(ve.tensor_tensor_scan(r_b, chunk_reset, r_lf, 0.0, ALU.mult, ALU.add))
            done(ve.tensor_tensor(r_e, r_e, r_b, ALU.subtract))
            done(ve.memset(m_start[:, :], 0.0))
            for c in range(NT):
                cs = slice(c * P, (c + 1) * P)
                done(ve.tensor_tensor_scan(r_m[:, cs], r_e[:, cs], r_e[:, cs], m_start[:, c:c + 1], ALU.max, ALU.max))
                last = slice((c + 1) * P - 1, (c + 1) * P)
                done(ve.tensor_tensor(m_start[:, c + 1:c + 2], r_m[:, last], r_b[:, last], ALU.add))
            lows("hx2", 3)
            lows("mq", 0, 1)
            short_conv(16)
            m_last = chunks(r_m)[:, :, P - 1:P]
            ve.tensor_tensor(r_den, r_m, r_b, ALU.add)
            ve.tensor_tensor(chunks(r_in), m_start[:, 0:NT].rearrange("k (c o) -> k c o", o=1).broadcast_to([ND2, NT, P]),
                             chunks(r_m), ALU.subtract)
            ve.tensor_tensor(chunks(r_w), chunks(r_e), m_last.broadcast_to([ND2, NT, P]), ALU.subtract)
            ve.tensor_tensor(dec8[:, :].rearrange("k (c o) -> k c o", o=1),
                             m_start[:, 0:NT].rearrange("k (c o) -> k c o", o=1), m_last, ALU.subtract).then_inc(exp_args, 1)
            ve.wait_ge(exp_args, 1)
            done(ve.tensor_scalar(r_m, r_m, -1.0, None, ALU.mult))
            lows("mq", 2)
            ve.wait_ge(exps_ready, 4)
            done(unflip(r_i, r_e))
            done(unflip(r_f, r_m))
            done(unflip(r_a, r_den))
            done(unflip(r_b, r_in))
            unflip(r_lf, r_w).then_inc(rows_ready, 1)
            ve.tensor_tensor(dblk[:, :, :], dec8[:, :].rearrange("k (o c) -> k o c", o=1).broadcast_to([ND2, ND2, NT]),
                             ident8.rearrange("k (r o) -> k r o", o=1).broadcast_to([ND2, ND2, NT]), ALU.mult)\
              .then_inc(dblk_ready, 1)
            lows("mq", 3)
            lows("mk", 0, 1)
            short_conv(0)
            products(0, 0)
            lows("mk", 2)
            products(0, 1)
            lows("mk", 3)
            lows("mv", 0, 1)
            short_conv(4)
            for t in range(NT):
                long_conv(0, t)
            lows("mv", 2, 3)
            lows("mo", 0, 1)
            name = ("gcol",)
            free(ve.tensor_copy(gcol[:, :, :, :].rearrange("p a c r -> p (a c r)"),
                                full(ve, name)[:, 0:4 * NT * ND2]), name)
            name = ("decay",)
            free(ve.tensor_copy(decay[:, :, :].rearrange("p r c -> p (r c)"), full(ve, name)[:, 0:ND2 * NT]), name)
            taken(ve, ("gcol",))
            taken(ve, name)

            def head_begin(h):
                o = full(ve, ("s", h))[:, :].rearrange("p (c l) -> p c l", c=NT)
                for d in range(2):
                    r = d * MH + h
                    taken(ve, ("bc", h, d))
                    w = wts[h % 2][d]
                    i = ve.tensor_tensor(w, o, w, ALU.mult)
                    if d == 0:
                        i.then_inc(p_ready, 1)
                    else:
                        free(i, ("s", h))
                    name = ("up", h, d)
                    o_up = full(ve, name)
                    st = state[h % 2][d]
                    ve.wait_ge(first_state, 2 * h + d + 1)
                    done(ve.scalar_tensor_tensor(out=st[:, 1, :], in0=st[:, 0, :], scalar=decay[:, r, 1:2],
                                                 in1=o_up[:, P + 1:2 * (P + 1)], op0=ALU.mult, op1=ALU.add))
                    free(ve.scalar_tensor_tensor(out=st[:, 2, :], in0=st[:, 1, :], scalar=decay[:, r, 2:3],
                                                 in1=o_up[:, 2 * (P + 1):3 * (P + 1)], op0=ALU.mult, op1=ALU.add), name)

            def head_end(h):
                nd_h, inter_h = nd[h % 2], inter[h % 2]
                for d in range(2):
                    r = d * MH + h
                    first_n = 0 if d == 0 else NT - 1
                    taken(ve, ("in", h, d))
                    for m in range(2):
                        name = ("nd", h, d, m)
                        o = full(ve, name)
                        for j in range(2):
                            n = 2 * m + j
                            src = o[:, j * (P + 1):(j + 1) * (P + 1)]
                            if n == first_n:
                                i = ve.tensor_copy(nd_h[:, n, :], src)
                            else:
                                i = ve.tensor_tensor(nd_h[:, n, :], src, inter_h[:, n, :], ALU.add)
                        free(i, name)
                    taken(ve, ("nd", h, d, 0))
                    taken(ve, ("nd", h, d, 1))
                    dn = nd_h[:, :, P:P + 1]
                    q = den[:, 0, :].rearrange("p (c o) -> p c o", o=1)
                    done(ve.scalar_tensor_tensor(out=q, in0=dn, scalar=-1.0, in1=dn, op0=ALU.mult, op1=ALU.max))
                    done(ve.tensor_tensor(q, q, gcol[:, 1, :, r:r + 1], ALU.max))
                    done(ve.reciprocal(den[:, 1, :], den[:, 0, :]))
                    rec = den[:, 1, :].rearrange("p (c o) -> p c o", o=1).broadcast_to([P, NT, P])
                    hs = hm[:, :, h * P:(h + 1) * P]
                    if d == 0:
                        done(ve.tensor_tensor(hs, nd_h[:, :, 0:P], rec, ALU.mult))
                    else:
                        done(ve.tensor_tensor(nd_h[:, :, 0:P], nd_h[:, :, 0:P], rec, ALU.mult))
                        ve.tensor_tensor(hs, hs, nd_h[:, :, 0:P], ALU.add).then_inc(h_ready, 1)

            def hyena_sums():
                ve.wait_ge(sq_h_ready, NT)
                ve.tensor_reduce(sumsq_h[:, :], sq_h.rearrange("p t (g c) -> p (t g) c", g=HG), AX_X, ALU.add)\
                  .then_inc(gsum_h_ready, 1)

            def hyena_norm():
                ve.wait_ge(rstd_h_ready, 1)
                for t in range(NT):
                    y = sig[2][:, t, :].rearrange("p (g c) -> p g c", g=HG)
                    r = rstd_h[:, t * HG:(t + 1) * HG].rearrange("p (g o) -> p g o", o=1)
                    ve.tensor_tensor(y, y, r.broadcast_to([P, HG, HALF // HG]), ALU.mult).then_inc(yn_h_ready, 1)

            def mlstm_norm(h):
                ve.wait_ge(rstd_m_ready, h + 1)
                y = hm[:, :, h * P:(h + 1) * P]
                r = rstd_m[:, h, :].rearrange("p (t o) -> p t o", o=1)
                ve.tensor_tensor(y, y, r.broadcast_to([P, NT, P]), ALU.mult).then_inc(yn_m_ready, 1)

            head_begin(0)
            products(1, 0)
            products(1, 1)
            lows("mo", 2, 3)
            lows("out0", 0, 1)
            for t in range(NT):
                long_conv(1, t)
            head_begin(1)
            head_end(0)
            hyena_sums()
            head_begin(2)
            head_end(1)
            head_begin(3)
            hyena_norm()
            mlstm_norm(0)
            head_end(2)
            mlstm_norm(1)
            for j in range(MH, ND):
                split_out(j)
            split_out(0)
            head_end(3)
            split_out(1)
            mlstm_norm(2)
            lows("out0", 2)
            mlstm_norm(3)
            lows("out0", 3)
            split_out(2)
            split_out(3)
            lows("out1", 0, 1)

            def weigh(s, t, half, name, count):
                cols = slice(half * 512, (half + 1) * 512)
                ve.wait_ge(sumsq_ready[2 * s - 1], count)
                free(ve.tensor_tensor(mixed[:, t, cols], full(ve, name)[:, :], row_bc[:, cols], ALU.mult), name)

            def renew(s, halves, after):
                for step in range(NT + 3):
                    if step < NT:
                        for args in halves(step):
                            weigh(s, step, *args)
                    if 1 <= step <= NT:
                        t = step - 1
                        for half, (_, name, _) in enumerate(products_of(s, t)):
                            taken(ve, name)
                        ve.wait_ge(rstd_ready[2 * s - 1], t + 1)
                        ve.wait_ge(ld_x[t], 32)
                        for half in range(2):
                            cols = slice(half * 512, (half + 1) * 512)
                            ve.scalar_tensor_tensor(out=x[:, t, cols], in0=mixed[:, t, cols], scalar=rstd[:, 2 * s - 1, t:t + 1],
                                                    in1=x[:, t, cols], op0=ALU.mult, op1=ALU.add).then_inc(x_ready, 1)
                    if step == 2:
                        low_part(ve, after)
                    if step >= 3:
                        take_norm(s, step - 3)
                    if step >= 4:
                        split_norm(s, step - 4)
                split_norm(s, NT - 1)

            def products_of(s, t):
                if s == 1:
                    return [(half, (f"mx0{half}", t), NT * half + t + 1) for half in range(2)]
                return [(half, ("ff2", 2 * t + half), 2 * t + half + 1) for half in range(2)]

            ve.wait_ge(ld_mix_post, 16)
            for t in range(NT):
                weigh(1, t, *products_of(1, t)[0])
            lows("out1", 2, 3)
            low_part(ve, UP)
            renew(1, lambda t: products_of(1, t)[1:], UP + 1)
            with ve.Fori(0, NFF // 8) as i:
                for j in range(8):
                    src, (hi, lo) = piece_shape(UP + j + 2)
                    ve.wait_ge(high_ready, 8 * i + (UP + j + 3))
                    ve.tensor_tensor(lo, src, hi.bitcast(F32), ALU.subtract).then_inc(split_ready, 1)

            def act_part(f):
                ve.wait_ge(act_high, f + 1)
                ve.tensor_tensor(xl[:, f % 8, :], act[:, f, :], xh[:, f % 8, :].bitcast(F32), ALU.subtract).then_inc(act_split, 1)

            for f in range(4):
                act_part(f)
            for f in range(NFF):
                if f + 4 < NFF:
                    act_part(f + 4)
                if f + 2 < NFF:
                    low_part(ve, DOWN + f + 2)
            ve.wait_ge(ld_mlp_post, 16)
            renew(2, lambda t: products_of(2, t), PIECE["index"])
            lows("index", 1)
            for t in range(NT):
                name = ("iw", t)
                free(ve.tensor_scalar(iw[:, t, :], full(ve, name)[:, 0:IH], IH ** -0.5, None, ALU.mult), name)
            for t in range(NT):
                taken(ve, ("iw", t))
            n = 0
            for i in range(1, NT):
                w = (i + 1) * P
                sc = score[:, i - 1, 0:w]
                for h in range(IH):
                    n += 1
                    taken(ve, ("ix", i, h))
                    r = rdot[(n - 1) % 2][:, 0:w]
                    if h == 0:
                        ins = ve.tensor_scalar(sc, r, iw[:, i, h:h + 1], None, ALU.mult)
                    else:
                        ins = ve.scalar_tensor_tensor(out=sc, in0=r, scalar=iw[:, i, h:h + 1], in1=sc, op0=ALU.mult, op1=ALU.add)
                    ins.then_inc(rdot_used, 1)
                    ve.wait_ge(rdot_used, n)
                done(ve.memset(score[0:HD, i - 1, w - HD:w], LOWEST))

            def choose(lo, hi):
                rounds = TOPK // 8
                for m in range(lo, hi):
                    i, n = 1 + m // rounds, m % rounds
                    w = (i + 1) * P
                    sc, wk = score[:, i - 1, 0:w], work[:, i - 1, 0:w]
                    src = sc if n == 0 else wk
                    done(ve.max(top8[:, :], src))
                    done(ve.match_replace(wk, top8[:, :], src, TAKEN))
                    if n == rounds - 1:
                        done(ve.tensor_tensor(sc, wk, sc, ALU.is_equal))
                        ve.tensor_scalar(sc, sc, NEG, None, ALU.mult).then_inc(sel_ready, 1)

            name = ("ff", 0)
            free(ve.tensor_scalar(f_f, full(ve, name)[0:AH, :], fbias[:, :], None, ALU.add), name)
            taken(ve, name)
            ve.scalar_tensor_tensor(out=f_a, in0=f_f, scalar=-1.0, in1=f_f, op0=ALU.mult, op1=ALU.max).then_inc(fgate_abs, 1)
            done(ve.tensor_scalar(f_f, f_f, 0.0, None, ALU.min))
            ve.wait_ge(fsoft_ready, 1)
            done(ve.tensor_tensor(f_f, f_a, f_f, ALU.subtract))
            ve.tensor_tensor_scan(f_n, one_col[0:AH, :].broadcast_to([AH, S]), f_f, 0.0, ALU.mult, ALU.add).then_inc(nf_ready, 1)

            def maxima(n, kind, h):
                at0 = 0
                if n >= 3:
                    ve.wait_ge(prob_ready, NT * (n - 2))
                    k2, h2 = HEADS[n - 3]
                    for i in range(NT):
                        full(ve, (k2 + "T", h2, i))
                if kind == "f":
                    taken(ve, ("nF", h))
                for i in range(NT):
                    w = (i + 1) * P
                    name = (kind + "s", h, i)
                    if kind == "f":
                        bias = nf_bc[n % 2][:, 0:w]
                    else:
                        bias = chunk_bias if i == 0 else score[:, i - 1, 0:w]
                        if i and h == 0:
                            ve.wait_ge(sel_ready, i)
                    free(ve.tensor_tensor_reduce(prob[n % 3][:, at0 * P:at0 * P + w], full(ve, name)[:, 0:w], bias, 1.0,
                                                 LOWEST, ALU.add, ALU.max, smax[:, n % 3, i:i + 1]), name)
                    at0 += i + 1
                for i in range(NT):
                    taken(ve, (kind + "s", h, i))
                ve.tensor_scalar(smax[:, n % 3, :], smax[:, n % 3, :], -1.0, None, ALU.mult).then_inc(smax_ready, 1)

            def outputs(n, kind, h):
                ve.wait_ge(prob_ready, NT * (n + 1))
                done(ve.reciprocal(ssum[:, n % 3, :], ssum[:, n % 3, :]))
                name = (kind + "o", h)
                o = full(ve, name)[:, 0:NT * HD].rearrange("p (t c) -> p t c", t=NT)
                rec = ssum[:, n % 3, :].rearrange("p (t o) -> p t o", o=1).broadcast_to([P, NT, HD])
                free(ve.tensor_tensor(otok[kind][:, :, h * HD:(h + 1) * HD], o, rec, ALU.mult), name)

            for n, (kind, h) in enumerate(HEADS):
                maxima(n, kind, h)
                if n >= LAG:
                    outputs(n - LAG, *HEADS[n - LAG])
                if n < AH:
                    choose(CHOICE[n], CHOICE[n + 1])
            for n in range(len(HEADS) - LAG, len(HEADS)):
                outputs(n, *HEADS[n])
            for j in range(PW // P):
                name = ("mix_pool", j)
                o = full(ve, name)
                taken(ve, ("pg", j))
                free(ve.scalar_tensor_tensor(out=pooled[j], in0=o[:, :], scalar=scol(ROW_POOL + j), in1=pgT[:, j, :],
                                             op0=ALU.mult, op1=ALU.mult), name)
            for j in range(PW // P):
                ve.wait_ge(xh_ready, XH["mix_pool", j])
                ve.tensor_tensor(xl[:, j, :], pooled[j], xh[:, j, :].bitcast(F32), ALU.subtract).then_inc(xl_ready, 1)
            for j in (3, 4, 5, 0, 1, 2):
                name = ("mT", j)
                o = full(ve, name)
                ve.wait_ge(xh_ready, XH[name])
                free(ve.tensor_tensor(xl[:, 2 + j, :], o[:, :], xh[:, 2 + j, :].bitcast(F32), ALU.subtract), name)
            for half in range(2):
                for t in range(NT):
                    name = (f"fx{half}", t)
                    xs = x[:, t, half * 512:(half + 1) * 512]
                    free(ve.tensor_tensor(xs, xs, full(ve, name)[:, :], ALU.add), name)
            ve.wait_ge(ld_final, 16)
            for t in range(NT):
                ve.wait_ge(rstd_ready[5], t + 1)
                ve.scalar_tensor_tensor(out=mixed[:, t, :], in0=x[:, t, :], scalar=rstd[:, 5, t:t + 1], in1=row_bc[:, :],
                                        op0=ALU.mult, op1=ALU.mult).then_inc(out_ready, 1)

        @block.gpsimd
        def _(po):
            done = stepper(po, pool_step)

            def root(o, i, n, ready):
                done(po.tensor_scalar(o, i, 1.0 / n, EPS, ALU.mult, ALU.add))
                po.tensor_tensor(o, o, minus_half[:, 0:o.shape[1]], ALU.pow).then_inc(ready, 1)

            def norm_root(s, t, count):
                po.wait_ge(sumsq_ready[s], count)
                r = rstd[:, s, t:t + 1]
                done(po.tensor_scalar(r, sumsq[:, s, 0, t:t + 1], sumsq[:, s, 1, t:t + 1], EPS, ALU.add, ALU.add))
                po.tensor_tensor(r, r, minus_half[:, 0:1], ALU.pow).then_inc(rstd_ready[s], 1)

            def renew_roots(s, count):
                for step in range(NT + 2):
                    if step < NT:
                        norm_root(2 * s - 1, step, count(step))
                    if step >= 2:
                        norm_root(2 * s, step - 2, 2 * (step - 1))

            for tile, value in ((minus_half, -0.5), (one_col, 1.0), (ones8, 1.0)):
                po.memset(tile[:, :], value).then_inc(consts_set, 1)
            po.memset(pool_w[:, :, :], 0.0).then_inc(pool_w_ready, 1)
            po.wait_ge(consts_set, 3)
            for t in range(NT):
                norm_root(0, t, 2 * t + 2)
            for w in (gate_wh, gate_wl):
                po.memset(w[:, :, ND2:GF].bitcast(F32), 0.0).then_inc(gate_w_ready, 1)
            po.wait_ge(ld_gate, 16)
            for kind in range(2):
                src = gate_w[:, :, :].rearrange("p k (d j c) -> p k d j c", d=2, j=2)[:, :, :, kind, :]
                hi, lo = (w[:, :, GF * kind:GF * kind + ND2].rearrange("p k (d c) -> p k d c", d=2) for w in (gate_wh, gate_wl))
                done(po.tensor_copy(hi, src))
                po.tensor_tensor(lo, src, hi.bitcast(F32), ALU.subtract).then_inc(gate_w_ready, 1)
            n = 0
            for q in range(2):
                for t in range(NT):
                    taken(po, ("ft", q, t, 0))
                    taken(po, ("ft", q, t, 1))
                    f, b = tap_sum[q][:, t, :], taps_b[n % 2]
                    po.tensor_tensor(tap_dif[q][:, t, :], b, f, ALU.subtract)
                    po.tensor_tensor(f, f, b, ALU.add).then_inc(taps_ready, 1)
                    n += 1
            def mirror(q, f):
                n = NF * q + f
                _, um, _, sm = wave
                k0, k1 = spec[q][0][:, NF + f, :], spec[q][1][:, NF + f, :]
                po.wait_ge(minus_ready, 2 * n + 2)
                for c in range(2):
                    taken(po, ("K", q, c, f, 1))
                done(po.tensor_tensor(wave_tmp[1], um, k1, ALU.mult))
                po.tensor_tensor(k1, sm, k1, ALU.mult)
                done(po.tensor_tensor(um, um, k0, ALU.mult))
                po.tensor_tensor(k0, sm, k0, ALU.mult)
                done(po.tensor_tensor(k1, k1, um, ALU.add))
                po.tensor_tensor(k0, k0, wave_tmp[1], ALU.subtract).then_inc(mirror_ready, 1)

            def skip(q):
                full(po, ("S", q, NF - 1, 1))
                po.wait_ge(ld_fb, 16)
                for t in range(NT):
                    z = sig[q][:, t, :]
                    po.tensor_tensor(z, z, row_bc[:, q * HALF:(q + 1) * HALF], ALU.mult).then_inc(skip_ready, 1)

            def state_keys(h):
                taken(po, ("kt", h))
                taken(po, ("gcol",))
                for d in range(2):
                    if h >= 2:
                        full(po, ("up", h - 2, d))
                    for c in range(3):
                        n = c if d == 0 else NT - 1 - c
                        i = po.tensor_scalar(kw[h % 2][d][c], ktok[h % 2][:, n, :], gcol[:, 3, n, d * MH + h:d * MH + h + 1],
                                             None, ALU.mult)
                    i.then_inc(kw_ready, 1)

            def gate_head(h):
                y = hm[:, :, h * P:(h + 1) * P]
                po.wait_ge(h_ready, h + 1)
                for t in range(NT):
                    taken(po, ("mo", t))
                po.tensor_tensor(y, y, o_gate[:, :, h * P:(h + 1) * P], ALU.mult).then_inc(gated, 1)

            def head_root(h):
                po.wait_ge(sumsq_m_ready, NT * (h + 1))
                root(rstd_m[:, h, :], sumsq_m[:, h, :], 1, rstd_m_ready)

            for f in range(NF):
                mirror(0, f)
            skip(0)
            for h in range(MH):
                po.wait_ge(k_silu, h + 1)
                po.tensor_scalar(kT[:, h, :], kT[:, h, :], P ** -0.5, None, ALU.mult).then_inc(k_ready, 1)
            full(po, ("y", 0, NT - 1))
            po.memset(v1[:, :, :, P:P + 1], 1.0).then_inc(v1_ones, 1)
            state_keys(0)
            for f in range(NF):
                mirror(1, f)
            skip(1)
            state_keys(1)
            po.wait_ge(long_ready, 2 * NT)
            for t in range(NT):
                po.tensor_tensor(sq_h[:, t, :], sig[2][:, t, :], sig[2][:, t, :], ALU.mult).then_inc(sq_h_ready, 1)
            state_keys(2)
            state_keys(3)
            gate_head(0)
            po.wait_ge(gsum_h_ready, 1)
            root(rstd_h[:, :], sumsq_h[:, :], HALF // HG, rstd_h_ready)
            head_root(0)
            for h in range(1, MH):
                gate_head(h)
                head_root(h)
            renew_roots(1, lambda t: NT + t + 1)
            first = [BANK[("ff1", f)] for f in range(8)]
            for n in range(4):
                po.engine_nop().then_inc(act_ready, 1)
            with po.Fori(0, NFF // 8) as i:
                for j in range(8):
                    b, k = first[j]
                    po.wait_ge(bank_free[b], i + (k + 1))
                    r = relu[j % 4]
                    ins = po.tensor_tensor(act[:, bass.ds(8 * i + j, 1), :], r, r, ALU.mult)
                    ins.then_inc(act_ready, 1)
            renew_roots(2, lambda t: 2 * t + 2)
            def lows(g, *pieces):
                for i in pieces:
                    low_part(po, PIECE[g] + i)

            lows("index", 2, 3)
            for g in ("fq", "fk", "fg", "fv", "dq", "dk", "dv", "pool"):
                lows(g, 0, 1, 2, 3)
            lows("dg", 0, 1)

            def gate(kind):
                for n in range(AH):
                    taken(po, (kind + "o", n))
                    for t in range(NT):
                        taken(po, (kind + "g", t))
                    o = otok[kind][:, :, n * HD:(n + 1) * HD]
                    po.tensor_tensor(o, o, gtok[kind][:, :, n * HD:(n + 1) * HD], ALU.mult).then_inc(og_ready, 1)

            def add_back(o, i, by):
                done(po.tensor_copy(o[:, 0:by], i[:, 0:by]))
                done(po.tensor_tensor(o[:, by:S], i[:, by:S], i[:, 0:S - by], ALU.add))

            po.wait_ge(ld_count, 16)
            for j in range(2):
                taken(po, ("pv", j))
                v, (s2, s4, w) = pvT[:, j, :], (win[0], win[1], win[2 + j])
                add_back(s2, v, 1)
                if j == 1:
                    add_back(s4, s2, 2)
                    add_back(s2, s4, 4)
                done(po.tensor_copy(w[0:HD, :], s2[0:HD, :]))
                add_back(w[HD:P, :], s2[HD:P, :], 2 if j == 0 else 8)
                done(po.tensor_tensor(w, w, inv_count[:, j, :], ALU.mult))
                po.tensor_tensor(w, w, v, ALU.subtract).then_inc(win_ready, 1)
            lows("dg", 2, 3)
            lows("fin0", 0, 1)
            gate("f")
            gate("d")
            lows("fin0", 2, 3)
            lows("fin1", 0, 1, 2, 3)
            for t in range(NT):
                norm_root(5, t, NT + t + 1)


def kernel(**inputs):
    import concourse.bacc as bacc
    from concourse.bass_utils import run_bass_kernel_spmd

    nc = bacc.Bacc("TRN2", target_bir_lowering=False, num_devices=1)
    arrays, aps = {}, {}
    for name, value in {**inputs, **constants()}.items():
        arr = np.ascontiguousarray(value)
        arrays["in_" + name] = arr
        aps[name] = nc.dram_tensor("in_" + name, arr.shape, mybir.dt.from_np(arr.dtype), kind="ExternalInput").ap()
    out = nc.dram_tensor("out", (1, S, D), F32, kind="ExternalOutput").ap()
    build_program(nc, aps, out)
    result = run_bass_kernel_spmd(nc, [arrays], core_ids=[0])
    return np.asarray(result.results[0]["out"])
```

```python
from contextlib import ExitStack

import numpy as np

import concourse.bass as bass
from concourse import mybir

F32 = mybir.dt.float32
F32R = mybir.dt.float32r
ALU = mybir.AluOpType
ACT = mybir.ActivationFunctionType
AX_X = mybir.AxisListType.X

P = 128
S = 512
NT = S // P
D = 1024
ND = D // P
HALF = D // 2
MH = 4
ND2 = 2 * MH
NCONV = 5 * HALF
NCT = NCONV // P
OFF_MV, OFF_MO, OFF_GATE = NCONV, NCONV + HALF, NCONV + 2 * HALF
HG = 8
NF = NT // 2
EMB, FHID = 33, 64
DFF = 4 * D
NFF = DFF // P
EPS = 1e-6
HD = 64
AW = 384
AH = AW // HD
PW = 256
IH, ID = 8, 32
TOPK = 128
OFF_DQ, OFF_DK, OFF_DV, OFF_DG = 512, 896, 1280, 1664
OFF_IQ = 2048
OFF_FQ, OFF_FK, OFF_FV, OFF_FG = 2344, 2728, 3112, 3496
GF = 32
NEG = -1e30
LOWEST = -3e38
TAKEN = -3.3e38
MAGIC = 12582912.0
TWO_PI_HI = 6.28125
TWO_PI_LO = 2 * np.pi - 6.28125
PI = float(np.nextafter(np.float32(np.pi), np.float32(0)))

ROW_CONV_W, ROW_CONV_B = 0, 3 * NCT
ROW_MIX_PRE = ROW_CONV_B + NCT
ROW_MLP_PRE = ROW_MIX_PRE + ND
ROW_MLSTM_W = ROW_MLP_PRE + ND
ROW_HYENA_W = ROW_MLSTM_W + MH
ROW_NORM2 = ROW_HYENA_W + MH
ROW_POOL = ROW_NORM2 + ND
N_ROWS = ROW_POOL + PW // P



def weight_groups():
    def ch(n0, cols):
        return [(("cv", n0 + j), "ch", P * j, P) for j in range(cols // P)]

    def tok(name, c0, n):
        return [((name, t), f"tok{t}", c0, n) for t in range(NT)]

    def many(name, cols, c0=0):
        return [((name, j), "ch", c0 + P * j, P) for j in range(cols // P)]

    return {
        "hv": ("w_in", 1024, 512, ch(8, 512)),
        "hx1": ("w_in", 1536, 512, ch(12, 512)),
        "hx2": ("w_in", 2048, 512, ch(16, 512)),
        "mq": ("w_in", 0, 512, ch(0, 512)),
        "mk": ("w_in", 512, 512, ch(4, 512)),
        "mv": ("w_in", OFF_MV, 512, tok("mv", 0, 512)),
        "mo": ("w_in", OFF_MO, 512, tok("mo", 0, 512)),
        "out0": ("w_out", 0, 512, tok("mx00", 0, 512)),
        "out1": ("w_out", 512, 512, tok("mx01", 0, 512)),
        "index": ("w_in_2", OFF_IQ, 296, many("iq", IH * ID) + [(("ik", 0), "ch", 256, ID + IH)]),
        "fq": ("w_in_2", OFF_FQ, AW, many("fq", AW)),
        "fk": ("w_in_2", OFF_FK, AW, many("fk", AW)),
        "fg": ("w_in_2", OFF_FG, AW + AH, tok("fg", 0, AW + AH)),
        "fv": ("w_in_2", OFF_FV, AW, tok("fv", 0, AW)),
        "dq": ("w_in_2", OFF_DQ, AW, many("dq", AW)),
        "dk": ("w_in_2", OFF_DK, AW, many("dk", AW)),
        "dv": ("w_in_2", OFF_DV, AW, tok("dv", 0, AW)),
        "dg": ("w_in_2", OFF_DG, AW, tok("dg", 0, AW)),
        "pool": ("w_in_2", 0, 512, many("pv", PW) + many("pg", PW, PW)),
        "fin0": ("w_out_2", 0, 512, tok("fx0", 0, 512)),
        "fin1": ("w_out_2", 512, 512, tok("fx1", 0, 512)),
    }


GROUPS = weight_groups()
GROUP_ORDER = ["hv", "hx1", "hx2", "mq", "mk", "mv", "mo", "out0", "out1", "index", "fq", "fk", "fg", "fv",
               "dq", "dk", "dv", "pool", "dg", "fin0", "fin1"]
K_ORDER = {"out0": (4, 5, 6, 7, 0, 1, 2, 3), "fin0": (0, 1, 6, 7, 2, 5, 3, 4)}
N_BEFORE = 9
UP = 4 * N_BEFORE
DOWN = UP + NFF
PIECE = {g: 4 * n + (2 * NFF if n >= N_BEFORE else 0) for n, g in enumerate(GROUP_ORDER)}
CHANNELS = {"out0": [("yT", j) for j in range(ND)],
            "fin0": [("mix_pool", j) for j in range(PW // P)] + [("mT", j) for j in range(6)]}
HEADS = [("f", h) for h in range(AH)] + [("d", h) for h in range(AH)]
LAG = 2
BETWEEN = {0: "dq", 1: "dk", 2: "dv", 5: "pool", 8: "dg"}
CHOICE_TILE, CHOICE_HEAD = [16, 30, 40], [43, 46, 48]


def psum_order():
    def group(g):
        return [name for name, *_ in GROUPS[g][3]]

    def turned(lo, hi):
        return [("cvT", n) for n in range(lo, hi)]

    def norm(s):
        return [("nT", s, t, half) for t in range(NT) for half in range(2)]

    def spectrum(q):
        return [(c, q, f, odd) for f in range(NF) for c in "US" for odd in range(2)]

    def begin(h):
        return [("s", h)] + [(what, h, d) for d in range(2) for what in ("bc", "up")]

    def end(h):
        return [(what, h, d) + m for d in range(2) for what, m in (("in", ()), ("nd", (0,)), ("nd", (1,)))]

    o = [("cols",)] + norm(0) + group("hv") + [("fcols",), ("f", 0), ("f", 1), ("f", 2), ("gate",)]
    o += [("ft", q, t, d) for q in range(2) for t in range(NT) for d in range(2)]
    o += [("K", q, c, f, odd) for q in range(2) for c in range(2) for f in range(NF) for odd in range(2)]
    o += group("hx1") + turned(8, 12) + group("hx2") + turned(12, 16) + group("mq") + turned(16, 20)
    o += spectrum(0) + group("mk") + [("y", 0, t) for t in range(NT)] + [("gcol",), ("decay",), ("kt", 0)] + group("mv")
    o += begin(0) + spectrum(1) + [("kt", 1)] + group("mo") + [("y", 1, t) for t in range(NT)]
    o += begin(1) + [("kt", 2)] + end(0) + begin(2) + [("kt", 3)] + end(1)
    o += begin(3) + end(2) + [("yT", j) for j in range(MH, ND)] + end(3)
    o += group("out0") + [("yT", j) for j in range(MH)] + group("out1") + norm(1)
    o += [("ff1", f) for f in range(NFF)] + [("ff2", n) for n in range(2 * NT)]
    o += norm(2) + group("index") + group("fq") + [("iw", 0)]
    for i, g in enumerate(("fk", "fg", None), 1):
        o += [("ix", i, h) for h in range(IH)] + (group(g) if g else [])
    o += [("ff", 0)] + group("fv")
    for n, (kind, h) in enumerate(HEADS):
        o += scores_of(kind, h)
        if n >= LAG:
            o += values_of(*HEADS[n - LAG])
        if n in BETWEEN:
            o += group(BETWEEN[n])
    o += [("mix_pool", j) for j in range(PW // P)] + [("mT", j) for j in (3, 4, 5)] + group("fin0")
    o += [("mT", j) for j in (0, 1)]
    for head in HEADS[-LAG:]:
        o += values_of(*head)
    o += [("mT", 2)] + group("fin1")
    return o


def scores_of(kind, h):
    return ([("nF", h)] if kind == "f" else []) + [(kind + "s", h, i) for i in range(NT)]


def values_of(kind, h):
    return [(kind + "T", h, i) for i in range(NT)] + [(kind + "o", h)]


def bank_table():
    order = psum_order()
    assert len(set(order)) == len(order)
    table, tiles_in = {}, [0] * 8
    last = order.index(GROUPS["fin0"][3][0][0])
    held = [n % 8 for n in range(last, last + NT)]
    others = [b for b in range(8) if b not in held]
    for n, name in enumerate(order):
        b = n % 8 if n < last + NT else others[n % 4]
        table[name] = (b, tiles_in[b])
        tiles_in[b] += 1
    return table


def constants():
    f32 = np.float32
    n = np.concatenate([np.arange(0, S, 2), np.arange(1, S, 2)])
    ang = np.pi * (((2 * np.arange(S // 2)[None, :] + 1) * n[:, None]) % (4 * S)) / (2 * S)
    dft = np.stack([np.cos(ang), np.sin(ang)]).astype(f32)
    bands = (EMB - 1) // 2
    t = np.linspace(0.0, 1.0, S, dtype=f32)[:, None]
    turn = (f32(2.0 * np.pi) * np.arange(S, dtype=f32)[:, None] / f32(S)).astype(f32)
    fr = np.linspace(1e-4, bands - 1, bands, dtype=f32)[None, :]
    z = np.concatenate([t, np.cos(fr * turn), -np.sin(fr * turn)], axis=-1).astype(f32)
    lo, hi = np.log(1e-2) / 1.5, np.log(1e-2) / 0.3
    deltas = np.abs(np.linspace(lo, hi, HALF, dtype=f32))
    window = (np.exp(-t * deltas[None, :]) / S).astype(f32)[n]
    window_b = window[:P].copy()
    window_b[0] = 0
    i, j = np.arange(P)[:, None], np.arange(P)[None, :]
    masks = np.stack([np.eye(P), np.where(i <= j, 0.0, NEG), np.where(i >= j, 0.0, NEG),
                      np.where((i < HD) & (j >= HD), NEG, 0.0)]).astype(f32)
    count = np.minimum(np.arange(S) + 1, np.array([2, 4, 8, 16])[:, None])
    inv_count = (1.0 / np.repeat(count, HD, axis=0)).astype(f32)
    rows = np.zeros((ND2, S + ND2 + 2), f32)
    rows[:, 0:S] = np.arange(S) % P != 0
    rows[:, S:S + ND2] = np.eye(ND2)
    rows[:MH, -2] = 1
    rows[MH:, -1] = 1
    return {
        "c_dft_in": dft, "c_dft_out": np.ascontiguousarray(dft.transpose(0, 2, 1)),
        "c_z": np.ascontiguousarray(z[n].T), "c_window": window, "c_window_b": window_b,
        "c_masks": masks, "c_inv_count": inv_count, "c_rows": rows,
    }


def build_program(nc, a, out):
    BANK = bank_table()
    with ExitStack() as ctx:
        def sb(name, shape, dtype=F32):
            return ctx.enter_context(nc.sbuf_tensor(name, shape, dtype))

        def sem(name):
            return ctx.enter_context(nc.semaphore(name))

        raw = sb("raw_weights", [P, 2, 2048])
        wh, wl = sb("weight_high", [P, 2, 1024], F32R), sb("weight_low", [P, 2, 1024], F32R)
        xh, xl = sb("x_high", [P, ND, S], F32R), sb("x_low", [P, ND, S], F32R)
        x = sb("x", [P, NT, D])
        masks = sb("masks", [P, 4, P])
        ident, cut_after, causal, chunk_bias = (masks[:, n, :] for n in range(4))
        masks_one = sb("masks_one_pass", [P, 3, P], F32R)
        ident_one, cut_after_one, causal_one = (masks_one[:, n, :] for n in range(3))
        colv = sb("colv", [P, N_ROWS])
        fcol = sb("fcol", [FHID, 6])
        row_bc = sb("row_bc", [P, D])
        rows_c = sb("rows_c", [ND2, S + ND2 + 2])
        chunk_reset = rows_c[:, 0:S]
        ident8 = rows_c[:, S:S + ND2]
        is_f, is_b = rows_c[:, S + ND2:S + ND2 + 1], rows_c[:, S + ND2 + 1:]
        gbias = sb("gbias", [ND2, 2])
        fbias = sb("fbias", [AH, 1])
        ones8 = sb("ones8", [ND2, P])
        one_col = sb("one_col", [P, 1])
        minus_half = sb("minus_half", [P, NT * HG])
        sumsq = sb("sumsq", [P, 6, 2, NT])
        rstd = sb("rstd", [P, 6, NT])
        sumsq_h, rstd_h = sb("sumsq_h", [P, NT * HG]), sb("rstd_h", [P, NT * HG])
        sumsq_m, rstd_m = sb("sumsq_m", [P, MH, NT]), sb("rstd_m", [P, MH, NT])
        gcol = sb("gcol", [P, 4, NT, ND2])
        decay = sb("decay", [P, ND2, NT])
        m_start = sb("m_start", [ND2, NT + 1])
        dec8 = sb("dec8", [ND2, NT])
        dblk = sb("dblk", [ND2, ND2, NT])
        den = sb("den", [P, 2, NT])
        gate_w = sb("gate_w", [P, ND, 16])
        gate_wh, gate_wl = sb("gate_high", [P, ND, GF + ND2], F32R), sb("gate_low", [P, ND, GF + ND2], F32R)
        iw = sb("iw", [P, NT, IH])
        fgate_tok = sb("fgate_tok", [P, NT, AH])
        top8 = sb("top8", [P, 8])
        smax = sb("smax", [P, 3, NT])
        ssum = sb("ssum", [P, 3, NT])
        pool_w = sb("pool_w", [P, 2, P])
        main_kb = 111
        with nc.sbuf_tensor("main_split", [P, 108 * 256], F32R) as main_split:
            pass
        main = sb("main", [P, int(main_kb * 256)])

        def at(kb, *shape, parts=P):
            n = int(np.prod(shape))
            o = int(round(kb * 256))
            assert o + n <= main_kb * 256, (kb, shape)
            v = main[0:parts, o:o + n]
            if len(shape) == 2:
                v = v.rearrange("p (a b) -> p a b", b=shape[1])
            if len(shape) == 3:
                v = v.rearrange("p (a b c) -> p a b c", b=shape[1], c=shape[2])
            return v

        spec = [[at(16 * q + 8 * c, NT, S) for c in range(2)] for q in range(2)]
        dft_out = at(32, 2, NF, S)
        dft_in = at(40, 2, NT, S // 2)
        tap_sum = [at(48, NT, S), at(64, NT, S)]
        tap_dif = [at(56, NT, S), at(72, NT, S)]
        sig = [at(48, NT, S), at(56, NT, S), at(64, NT, S)]
        r_e, r_lf = (at(72 + 2 * n, S, parts=ND2) for n in range(2))
        wave_tmp = [at(76 + 2 * n, S) for n in range(2)]
        conv_buf = [at(80 + 2 * n, S) for n in range(8)]
        conv = {n: conv_buf[n % 8 if n >= 8 else (n + 4) % 8] for n in range(NCT)}
        proj = x[:, 0:2, :].rearrange("p a b -> p (a b)").rearrange("p (n c) -> p n c", n=4)
        kT, qT = at(80, MH, S), at(88, MH, S)
        r_den, r_in, r_w, r_m = (at(96 + 2 * n, S, parts=ND2) for n in range(4))
        wave = [at(96 + 2 * n, S) for n in range(2)]
        wave_minus = [[at(kb + 2 * n, S) for n in range(2)] for kb in (100, 107)]
        filt_w4, window, window_b = at(0, 2 * S * 2, parts=FHID), at(16, NT, S), at(24, S)
        hidden = at(26, S, parts=FHID)
        taps_b = [at(28 + 2 * n, S) for n in range(2)]
        sin_arg, sin_turn = at(48, S, parts=FHID), at(50, S, parts=FHID)
        zT = at(52, S, parts=EMB)
        filt_w = [at(54, FHID, parts=EMB), at(54.25, FHID, parts=FHID), at(54.5, FHID, parts=FHID)]
        colrows, frows = at(55, P, parts=N_ROWS), at(55.5, FHID, parts=6)
        xn_first = at(80, NT, D)
        turned = [at(96 + 2 * n, S) for n in range(4)]
        v1 = at(0, NT, MH * (P + 1)).rearrange("p t (h c) -> p t h c", h=MH)
        ktok = [at(52 + 2 * n, NT, P) for n in range(2)]
        kw = [[[at(kb + 1.5 * d + 0.5 * c, P) for c in range(3)] for d in range(2)] for kb in (104, 48)]
        wts = [[at(kb + 2 * d, NT, P) for d in range(2)] for kb in (8.25, 32)]
        state = [[at(kb + 1.75 * d, 3, P + 1) for d in range(2)] for kb in (12.25, 36)]
        inter = [at(kb, NT, P + 1) for kb in (16, 39.5)]
        nd = [at(kb, NT, P + 1) for kb in (18.25, 41.75)]
        hm = at(24, NT, HALF)
        o_gate = x[:, 0:2, :].rearrange("p a b -> p (a b)").rearrange("p (t c) -> p t c", t=NT)
        x_rows = x[0:ND2, 2:4, :].rearrange("p a b -> p (a b)").rearrange("p (t c) -> p t c", c=S)
        r_a, r_b, r_i, r_f = (x_rows[:, n, :] for n in range(4))
        sq_h, sq_m = at(96, NT, HALF), at(72, NT, HALF)
        act = at(0, NFF, S)
        xn_mlp = at(0, NT, D)
        mixed = at(80, NT, D)
        relu = [at(96 + 2 * n, S) for n in range(4)]
        junk = [at(kb, 4, 512) for kb in (56, 48, 48, 64, 64, 72)]
        iqT, ikT = at(0, 2, S), at(4, S)
        iw_T = at(48, S)[ID:ID + IH, :]
        score, work = at(6, 3, S), at(12, 3, S)
        rdot = [at(18 + 2 * n, S) for n in range(2)]
        qkT = {"fq": at(22, 3, S), "fk": at(28, 3, S), "dq": at(34, 3, S), "dk": at(40, 3, S)}
        vtok = {"f": at(46, NT, AW), "d": at(52, NT, AW)}
        gtok = {"f": at(58, NT, AW), "d": at(22, NT, AW)}
        otok = {"f": at(64, NT, AW), "d": at(46, NT, AW)}
        prob = [at(70 + 5 * n, 10 * P) for n in range(3)]
        probT = [at(85 + 5 * n, 10, P) for n in range(2)]
        nf_bc = [at(95 + 2 * n, S) for n in range(2)]
        f_f, f_a, f_n = (at(99 + 2 * n, S, parts=AH) for n in range(3))
        pvT, pgT = at(12, 2, S), at(16, 2, S)
        win = [at(28 + 2 * n, S) for n in range(3)] + [at(0, S)]
        inv_count = at(2, 2, S)
        pooled = [at(99 + 2 * n, S) for n in range(2)]

        def beside(*kbs):
            return [main_split[:, kb * 256:kb * 256 + 1024] for kb in kbs]

        SIDE = {PIECE["hv"] + 2: beside(56, 60), PIECE["hv"] + 3: beside(64, 68),
                PIECE["out1"]: beside(32, 36), PIECE["out1"] + 1: beside(40, 44),
                UP: beside(64, 68), UP + 1: beside(72, 76),
                DOWN + NFF - 4: beside(0, 4), DOWN + NFF - 3: beside(8, 12),
                **{PIECE["index"] + i: beside(16 + 8 * i, 20 + 8 * i) for i in range(4)},
                PIECE["fin1"]: beside(95, 104), PIECE["fin1"] + 1: beside(58, 64)}

        AHEAD = 4
        act_ahead = [[main_split[:, kb * 256:kb * 256 + S] for kb in (80 + 4 * f, 82 + 4 * f)] for f in range(AHEAD)]

        def act_parts(f):
            return act_ahead[f] if f < AHEAD else [v[:, (f - AHEAD) % ND, :] for v in (xh, xl)]

        ps = [ctx.enter_context(nc.psum_tensor(f"bank{n}", [P, 512], F32)) for n in range(8)]

        bank_full = [sem(f"bank_full{n}") for n in range(8)]
        bank_free = [sem(f"bank_free{n}") for n in range(8)]
        raw_loaded = [sem(f"raw_loaded{n}") for n in range(2)]
        high_ready, split_ready = sem("high_ready"), sem("split_ready")
        piece_used = sem("piece_used")
        xh_ready, xl_ready = sem("xh_ready"), sem("xl_ready")
        act_high, act_split = sem("act_high"), sem("act_split")
        (ld_cols, ld_masks, ld_fcols, ld_filter, ld_filt_w4, ld_window, ld_dft, ld_rows, ld_gate, ld_fb, ld_mix_post,
         ld_mlp_post, ld_final, ld_pool, ld_count, stored) = (sem("ld_" + n) for n in (
             "cols masks fcols filter filt_w4 window dft rows gate fb mix_post mlp_post final pool count stored").split())
        dve_step, act_step, pool_step = sem("dve_step"), sem("act_step"), sem("pool_step")
        masks_ready = sem("masks_ready")
        consts_set, v1_ones = sem("consts_set"), sem("v1_ones")
        ld_x = [sem(f"ld_x{t}") for t in range(NT)]
        sumsq_ready = [sem(f"sumsq_ready{s}") for s in range(6)]
        rstd_ready = [sem(f"rstd_ready{s}") for s in range(6)]
        rstd_h_ready, rstd_m_ready = sem("rstd_h_ready"), sem("rstd_m_ready")
        x_ready, xn_ready = sem("x_ready"), sem("xn_ready")
        sin_arg_ready, hidden_ready, taps_ready = (sem(n) for n in "sin_arg_ready hidden_ready taps_ready".split())
        conv_ready, q_ready, k_silu, k_ready = (sem(n) for n in "conv_ready q_ready k_silu k_ready".split())
        wave_used, minus_ready, mirror_ready, spec_ready, skip_ready, long_ready = (
            sem(n) for n in "wave_used minus_ready mirror_ready spec_ready skip_ready long_ready".split())
        gate_w_ready, gate_abs, softplus_ready, exp_args, exps_ready, rows_ready, dblk_ready = (
            sem(n) for n in "gate_w_ready gate_abs softplus_ready exp_args exps_ready rows_ready dblk_ready".split())
        kw_ready, first_state, p_ready, h_ready = (sem(n) for n in "kw_ready first_state p_ready h_ready".split())
        sq_h_ready, gsum_h_ready, yn_h_ready = (sem(n) for n in "sq_h_ready gsum_h_ready yn_h_ready".split())
        gated, sumsq_m_ready, yn_m_ready = sem("gated"), sem("sumsq_m_ready"), sem("yn_m_ready")
        act_ready = sem("act_ready")
        rdot_used = sem("rdot_used")
        sel_ready = sem("sel_ready")
        fgate_abs, fsoft_ready, nf_ready = sem("fgate_abs"), sem("fsoft_ready"), sem("nf_ready")
        smax_ready, prob_ready, og_ready = (sem(n) for n in "smax_ready prob_ready og_ready".split())
        win_ready, pool_w_ready = sem("win_ready"), sem("pool_w_ready")
        out_ready = sem("out_ready")

        def full(eng, name):
            b, k = BANK[name]
            eng.wait_ge(bank_full[b], k + 1)
            return ps[b]

        def free(ins, name):
            return ins.then_inc(bank_free[BANK[name][0]], 1)

        def taken(eng, name):
            b, k = BANK[name]
            eng.wait_ge(bank_free[b], k + 1)

        CONV = {n: (n - 8) % NCT + 1 for n in range(NCT)}
        def counts(n):
            if PIECE["out1"] <= n < DOWN or n >= PIECE["fin1"]:
                return False
            return n < DOWN + NFF - 4 if DOWN <= n < DOWN + NFF else n % 4 < 3

        counted = np.cumsum([counts(n) for n in range(4 * len(GROUP_ORDER) + 2 * NFF)]).tolist()

        def used(eng, n):
            if counts(n):
                eng.wait_ge(piece_used, counted[n])
            elif UP <= n < DOWN:
                full(eng, ("ff1", n - UP))
            elif DOWN <= n < DOWN + NFF:
                full(eng, ("ff2", 2 * NT - 1))
            else:
                g = [g for g in GROUP_ORDER if PIECE[g] <= n < PIECE[g] + 4][0]
                full(eng, GROUPS[g][3][-1][0])

        def place_free(eng, n):
            before = [m for m in range(n % 2, n, 2) if m not in SIDE]
            if n not in SIDE and before:
                used(eng, before[-1])

        def piece_shape(n):
            split = SIDE[n] if n in SIDE else [w[:, n % 2, :] for w in (wh, wl)]
            if UP <= n < DOWN + NFF:
                return raw[:, n // 2 % 2, n % 2 * D:(n % 2 + 1) * D], split
            cols = [GROUPS[g][2] for g in GROUP_ORDER if PIECE[g] <= n < PIECE[g] + 4][0]
            return (raw[:, n // 2 % 2, 0:4 * cols].rearrange("p (k c) -> p k c", k=4)[:, n % 2 * 2:n % 2 * 2 + 2, :],
                    [w[:, 0:2 * cols].rearrange("p (k c) -> p k c", k=2) for w in split])

        def low_part(eng, n):
            src, (hi, lo) = piece_shape(n)
            eng.wait_ge(high_ready, n + 1)
            eng.tensor_tensor(lo, src, hi.bitcast(F32), ALU.subtract).then_inc(split_ready, 1)

        XT_ORDER = [("nT", 0, t, half) for t in range(NT) for half in range(2)]
        XT_ORDER += [("yT", j) for j in (4, 5, 6, 7, 0, 1, 2, 3)]
        XT_ORDER += [("nT", s, t, half) for s in (1, 2) for t in range(NT) for half in range(2)]
        XT_ORDER += [("mix_pool", j) for j in range(PW // P)] + [("mT", j) for j in (3, 4, 5, 0, 1, 2)]
        XH = {name: n + 1 for n, name in enumerate(XT_ORDER)}
        XL = {name: n + 1 for n, name in enumerate(nm for nm in XT_ORDER if nm[0] in ("nT", "mix_pool"))}

        def stepper(eng, step):
            count = [0]

            def done(ins):
                count[0] += 1
                ins.then_inc(step, 1)
                eng.wait_ge(step, count[0])
            return done

        def scol(row, n=1):
            return colv[:, row:row + n]

        NORMS = {0: (ROW_MIX_PRE, 0, xn_first), 1: (ROW_MLP_PRE, 2, xn_mlp), 2: (ROW_NORM2, 4, mixed)}
        x_tok = a["x"].rearrange("b (t p) d -> p (b t) d", p=P)
        out_tok = out.rearrange("b (t p) d -> p (b t) d", p=P)

        group_at = {g: n for n, g in enumerate(GROUP_ORDER)}
        block = ctx.enter_context(nc.Block())

        @block.sync
        def _(sp):
            def load_unit(u, parts):
                if u >= 2:
                    sp.wait_ge(split_ready, 2 * u - 2)
                for to, source in parts:
                    sp.dma_start(to, source).then_inc(raw_loaded[u % 2], 16)

            def weights(g, halves=range(2)):
                weight, c0, n, tiles = GROUPS[g]
                src = a[weight] if weight[-2:] != "_2" else a[weight].rearrange("l k n -> (l k) n")
                src = src.rearrange("(k p) n -> p k n", p=P)[:, :, c0:c0 + n]
                ks = K_ORDER.get(g, range(ND))
                for half in halves:
                    u = PIECE[g] // 2 + half
                    to = raw[:, u % 2, 0:4 * n].rearrange("p (k c) -> p k c", k=4)
                    parts = []
                    for i in range(2):
                        k0, k1 = ks[4 * half + 2 * i:4 * half + 2 * i + 2]
                        parts.append((to[:, 2 * i:2 * i + 2, :], src[:, k0:k1 + 1:k1 - k0, :]))
                    load_unit(u, parts)

            sp.dma_start(masks[:, :, :], a["c_masks"].rearrange("m p n -> p m n")).then_inc(ld_masks, 16)
            for t in range(NT):
                sp.dma_start(x[:, t, :], x_tok[:, t, :]).then_inc(ld_x[t], 16)
            for name, row in (("norm_mix_pre", ROW_MIX_PRE), ("conv_b", ROW_CONV_B), ("norm_mlp_pre", ROW_MLP_PRE),
                              ("mlstm_norm_w", ROW_MLSTM_W), ("hyena_norm_w", ROW_HYENA_W), ("norm_g_2", ROW_NORM2),
                              ("pool_scale_2", ROW_POOL)):
                src = a[name] if name[-2:] != "_2" else a[name].rearrange("l n -> (l n)")
                src = src.rearrange("(r p) -> r p", p=P)
                sp.dma_start(colrows[row:row + src.shape[0], :], src).then_inc(ld_cols, 16)
            sp.dma_start(colrows[0:3 * NCT, :], a["conv_w"].rearrange("w (r p) -> (w r) p", p=P)).then_inc(ld_cols, 16)
            weights("hv", [0])
            for n in range(3):
                sp.dma_start(frows[n:n + 1, :], a[f"filt_b{n + 1}"].rearrange("(a n) -> a n", a=1)).then_inc(ld_fcols, 16)
            sp.dma_start(frows[3:6, :], a["filt_freq"]).then_inc(ld_fcols, 16)
            sp.dma_start(zT, a["c_z"]).then_inc(ld_filter, 16)
            for n in range(3):
                sp.dma_start(filt_w[n], a[f"filt_w{n + 1}"]).then_inc(ld_filter, 16)
            sp.dma_start(gate_w[:, :, :], a["w_in"].rearrange("(k p) n -> p k n", p=P)[:, :, OFF_GATE:OFF_GATE + 16])\
              .then_inc(ld_gate, 16)
            weights("hv", [1])
            sp.dma_start(filt_w4, a["filt_w4"]).then_inc(ld_filt_w4, 16)
            sp.dma_start(window, a["c_window"].rearrange("(t p) c -> p t c", p=P)).then_inc(ld_window, 16)
            sp.dma_start(window_b, a["c_window_b"]).then_inc(ld_window, 16)
            for c in range(2):
                sp.dma_start(dft_in[:, c], a["c_dft_in"][c].rearrange("(t p) f -> p t f", p=P)).then_inc(ld_dft, 16)
            sp.dma_start(rows_c[:, :], a["c_rows"]).then_inc(ld_rows, 16)
            for kind in range(2):
                for d in range(2):
                    o = (2 * d + kind) * MH
                    sp.dma_start(gbias[d * MH:(d + 1) * MH, kind:kind + 1],
                                 a["b_gates"][o:o + MH].rearrange("(r o) -> r o", o=1)).then_inc(ld_rows, 16)
            sp.dma_start(fbias[:, :], a["fox_bf_2"].rearrange("l (r o) -> (l r) o", o=1)).then_inc(ld_rows, 16)
            for c in range(2):
                sp.dma_start(dft_out[:, c], a["c_dft_out"][c].rearrange("(f p) t -> p f t", p=P)).then_inc(ld_dft, 16)
            sp.dma_start(row_bc[:, :], a["filt_bias"].rearrange("o c -> (o c)").partition_broadcast(P)).then_inc(ld_fb, 16)

            for g in GROUP_ORDER[1:7]:
                weights(g)
            weights("out0")
            sp.wait_ge(long_ready, 2 * NT)
            sp.wait_ge(skip_ready, 2 * NT)
            sp.dma_start(row_bc[:, :], a["norm_mix_post"].partition_broadcast(P)).then_inc(ld_mix_post, 16)
            sp.wait_ge(gated, MH)
            full(sp, ("bc", MH - 1, 1))
            for t in range(NT):
                sp.dma_start(x[:, t, :], x_tok[:, t, :]).then_inc(ld_x[t], 16)
            weights("out1")
            w_up = a["w_mlp_in"].rearrange("(k p) n -> p k n", p=P)
            with sp.Fori(0, NFF // 4) as i:
                for j in range(2):
                    sp.wait_ge(split_ready, 4 * i + (UP + 2 * j - 2))
                    for c in range(2):
                        sp.dma_start(raw[:, j, c * D:(c + 1) * D].rearrange("p (k n) -> p k n", k=ND),
                                     w_up[:, :, bass.ds(i * 512 + (2 * j + c) * P, P)]).then_inc(raw_loaded[j], 16)
            w_down = a["w_mlp_out"].rearrange("(f p) n -> f p n", p=P)
            for f in range(0, NFF, 2):
                u = (DOWN + f) // 2
                load_unit(u, [(raw[:, u % 2, i * D:(i + 1) * D], w_down[f + i]) for i in range(2)])
            sp.wait_ge(x_ready, 2 * NT)
            sp.dma_start(row_bc[:, :], a["norm_mlp_post"].partition_broadcast(P)).then_inc(ld_mlp_post, 16)
            weights("index")
            weights("fq")
            sp.wait_ge(x_ready, 4 * NT)
            sp.dma_start(row_bc[:, :], a["final_g_2"].partition_broadcast(P)).then_inc(ld_final, 16)
            sp.wait_ge(pool_w_ready, 1)
            for j in range(PW // P):
                for n in range(2):
                    sp.dma_start(pool_w[n * HD:(n + 1) * HD, j, n * HD:(n + 1) * HD], a["pool_w_2"][0, 2 * j + n])\
                      .then_inc(ld_pool, 16)
            for g in ("fk", "fg", "fv"):
                weights(g)
            full(sp, ("ix", NT - 1, IH - 1))
            sp.dma_start(inv_count, a["c_inv_count"].rearrange("(j p) s -> p j s", p=P)).then_inc(ld_count, 16)
            for g in GROUP_ORDER[group_at["dq"]:]:
                weights(g)
            for t in range(NT):
                sp.wait_ge(out_ready, t + 1)
                sp.dma_start(out_tok[:, t, :], mixed[:, t, :]).then_inc(stored, 16)
            sp.wait_ge(stored, 16 * NT)

        @block.tensor
        def _(pe):
            order = psum_order()
            at_tile = [0]

            def tile(name):
                assert order[at_tile[0]] == name, (order[at_tile[0]], name)
                at_tile[0] += 1
                b, k = BANK[name]
                if k:
                    pe.wait_ge(bank_free[b], k)
                return ps[b]

            def made(ins, name):
                ins.then_inc(bank_full[BANK[name][0]], 1)

            def product(o, left, right, start, stop):
                (lh, ll), (rh, rl) = left, right
                pe.matmul(o, lh, rh, start=start, stop=False)
                pe.matmul(o, lh, rl, start=False, stop=False)
                return pe.matmul(o, ll, rh, start=False, stop=stop)

            def project(g, pieces=range(4)):
                ks = K_ORDER.get(g, range(ND))
                for i in pieces:
                    n = PIECE[g] + i
                    pe.wait_ge(split_ready, n + 1)
                    w = piece_shape(n)[1]
                    for name, kind, c0, cols in GROUPS[g][3]:
                        if i == 0:
                            tile(name)
                        bank = ps[BANK[name][0]]
                        for kk in range(2):
                            k = ks[2 * i + kk]
                            part = [v[:, kk, c0:c0 + cols] for v in w]
                            if kind == "ch":
                                o, left, right = bank[0:cols, :], part, (xh[:, k, :], xl[:, k, :])
                            else:
                                tok = slice(int(kind[3:]) * P, (int(kind[3:]) + 1) * P)
                                o, left, right = bank[:, 0:cols], (xh[:, k, tok], xl[:, k, tok]), part
                            mm = product(o, left, right, i + kk == 0, i == 3 and kk == 1)
                        if i == 3:
                            made(mm, name)
                    if i < 3:
                        mm.then_inc(piece_used, 1)

            def project_by_tile(g, between):
                names = [name for name, *_ in GROUPS[g][3]]
                for name in names:
                    tile(name)
                for t, name in enumerate(names):
                    tok = slice(t * P, (t + 1) * P)
                    for i in range(4):
                        n = PIECE[g] + i
                        pe.wait_ge(split_ready, n + 1)
                        w = piece_shape(n)[1]
                        for kk in range(2):
                            k = 2 * i + kk
                            mm = product(ps[BANK[name][0]][:, :], (xh[:, k, tok], xl[:, k, tok]), [v[:, kk, :] for v in w],
                                         k == 0, k == ND - 1)
                        if i == 1:
                            between(t)
                    made(mm, name)

            def project_renewed(s, pieces, tiles=()):
                turn_norm(s, NT - 2)
                last = turn_tiles(s, NT - 1)
                for name in tiles:
                    tile(name)
                for tokens in (range(NT // 2), range(NT // 2, NT)):
                    wait_x([("nT", s, t, half) for t in tokens for half in range(2)])
                    for i in range(4):
                        if tokens[0] == 0 and i == 2:
                            turn_norm(s, NT - 1, last)
                        pieces(i, slice(tokens[0] * P, (tokens[-1] + 1) * P), tokens)

            def project_first(g, i, cols, tokens):
                n = PIECE[g] + i
                pe.wait_ge(split_ready, n + 1)
                w = piece_shape(n)[1]
                for name, kind, c0, width in GROUPS[g][3]:
                    bank = ps[BANK[name][0]]
                    for kk in range(2):
                        k = 2 * i + kk
                        part = [v[:, kk, c0:c0 + width] for v in w]
                        mm = product(bank[0:width, cols], part, (xh[:, k, cols], xl[:, k, cols]), k == 0, k == ND - 1)
                    if tokens[0] and i == 3:
                        made(mm, name)
                if tokens[0] and i < 3:
                    mm.then_inc(piece_used, 1)

            def wait_x(names):
                for name in names:
                    if name in XL:
                        pe.wait_ge(xl_ready, XL[name])
                    else:
                        taken(pe, name)

            def project_part(g, i):
                wait_x([CHANNELS[g][k] for k in K_ORDER[g][2 * i:2 * i + 2]])
                project(g, [i])

            def turn_tiles(s, t):
                return [tile(("nT", s, t, half)) for half in range(2)]

            def turn_norm(s, t, tiles=None):
                pe.wait_ge(xn_ready, NT * s + t + 1)
                xn = NORMS[s][2]
                for half, o in enumerate(tiles or turn_tiles(s, t)):
                    for d in range(4):
                        mm = pe.transpose(o[:, d * P:(d + 1) * P], xn[:, t, (4 * half + d) * P:(4 * half + d + 1) * P], ident)
                    made(mm, ("nT", s, t, half))

            def turn_earlier(s, t):
                if t >= 2:
                    turn_norm(s, t - 2)

            pe.wait_ge(ld_masks, 16)
            pe.wait_ge(ld_cols, 16 * 8)
            made(pe.transpose(tile(("cols",))[:, 0:N_ROWS], colrows, ident[0:N_ROWS, 0:N_ROWS]), ("cols",))
            for t in range(NT - 1):
                turn_norm(0, t)
            last = turn_tiles(0, NT - 1)
            for name, *_ in GROUPS["hv"][3]:
                tile(name)
            pe.wait_ge(ld_fcols, 16 * 4)
            made(pe.transpose(tile(("fcols",))[0:FHID, 0:6], frows, ident[0:6, 0:6]), ("fcols",))
            pe.wait_ge(ld_filter, 16 * 4)
            made(pe.matmul(tile(("f", 0))[0:FHID, :], filt_w[0], zT, start=True, stop=True), ("f", 0))
            for tokens in (range(NT // 2), range(NT // 2, NT)):
                wait_x([("nT", 0, t, half) for t in tokens for half in range(2)])
                for i in range(4):
                    if tokens[0] == 0 and i == 2:
                        turn_norm(0, NT - 1, last)
                    n = {(0, 3): 1, (NT // 2, 2): 2}.get((tokens[0], i))
                    if n:
                        pe.wait_ge(hidden_ready, n)
                        made(pe.matmul(tile(("f", n))[0:FHID, :], filt_w[n], hidden, start=True, stop=True), ("f", n))
                    project_first("hv", i, slice(tokens[0] * P, (tokens[-1] + 1) * P), tokens)
            pe.wait_ge(gate_w_ready, 4)
            o = tile(("gate",))
            for k in range(ND):
                mm = product(o[0:GF + ND2, :], (gate_wh[:, k, :], gate_wl[:, k, :]), (xh[:, k, :], xl[:, k, :]),
                             k == 0, k == ND - 1)
            made(mm, ("gate",))
            pe.wait_ge(hidden_ready, 3)
            pe.wait_ge(ld_filt_w4, 16)
            for q in range(2):
                for t in range(NT):
                    for d in range(2):
                        j = 2 * d + q
                        made(pe.matmul(tile(("ft", q, t, d))[:, :], hidden[:, t * P:(t + 1) * P],
                                       filt_w4[:, j * HALF:(j + 1) * HALF], start=True, stop=True), ("ft", q, t, d))
            def transform(name, c, f, odd, source):
                o = tile(name)
                for t in (2 * odd, 2 * odd + 1):
                    mm = pe.matmul(o[:, :], dft_in[:, c, t, f * P:(f + 1) * P], source[:, t, :],
                                   start=(t == 2 * odd), stop=(t == 2 * odd + 1))
                made(mm, name)

            pe.wait_ge(ld_dft, 64)
            for q in range(2):
                pe.wait_ge(taps_ready, NT * (q + 1))
                for c in range(2):
                    for f in range(NF):
                        for odd in range(2):
                            transform(("K", q, c, f, odd), c, f, odd, (tap_sum, tap_dif)[c][q])
            def turn_conv(lo):
                for n in range(lo, lo + 4):
                    pe.wait_ge(conv_ready, CONV[n])
                    o = tile(("cvT", n))
                    for t in range(NT):
                        src = conv[n].rearrange("p (m two) -> p two m", two=2)[:, t // NF, (t % NF) * P:(t % NF + 1) * P]
                        mm = pe.transpose(o[:, t * P:(t + 1) * P], src, ident)
                    made(mm, ("cvT", n))

            project("hx1")
            turn_conv(8)
            project("hx2")
            turn_conv(12)
            project("mq")
            turn_conv(16)

            def spectrum(q):
                for n in range(8 + 4 * q, 12 + 4 * q):
                    taken(pe, ("cvT", n))
                if q:
                    pe.wait_ge(long_ready, NT)
                for f in range(NF):
                    for c in range(2):
                        for odd in range(2):
                            transform(("US"[c], q, f, odd), c, f, odd, sig[q])

            def back(q):
                pe.wait_ge(spec_ready, NF * (q + 1))
                for t in range(NT):
                    o = tile(("y", q, t))
                    for c in range(2):
                        for f in range(NF):
                            k = f + NF * ((t // NF + c) % 2)
                            mm = pe.matmul(o[:, :], dft_out[:, c, f, t * P:(t + 1) * P], spec[q][1 - c][:, k, :],
                                           start=(c + f == 0), stop=(c == 1 and f == NF - 1))
                    made(mm, ("y", q, t))

            spectrum(0)
            project("mk")
            back(0)

            pe.wait_ge(rows_ready, 1)
            o = tile(("gcol",))
            for n, row in enumerate((r_i, r_a, r_b, r_lf)):
                for c in range(NT):
                    k = (n * NT + c) * ND2
                    mm = pe.transpose(o[:, k:k + ND2], row[:, c * P:(c + 1) * P], ident8)
            made(mm, ("gcol",))
            pe.wait_ge(dblk_ready, 1)
            made(pe.matmul(tile(("decay",))[:, 0:ND2 * NT], ones8[:, :], dblk[:, :, :].rearrange("k r c -> k (r c)"),
                           start=True, stop=True), ("decay",))

            def turn_keys(h):
                o = tile(("kt", h))
                pe.wait_ge(k_ready, h + 1)
                for c in range(NT):
                    mm = pe.transpose(o[:, c * P:(c + 1) * P], kT[:, h, c * P:(c + 1) * P], ident)
                made(mm, ("kt", h))

            def head_begin(h):
                o = tile(("s", h))
                pe.wait_ge(q_ready, h + 1)
                for c in range(NT):
                    cs = slice(c * P, (c + 1) * P)
                    mm = pe.matmul(o[:, cs], kT[:, h, cs], qT[:, h, cs], start=True, stop=True)
                made(mm, ("s", h))
                for d in range(2):
                    r = d * MH + h
                    o = tile(("bc", h, d))
                    pe.matmul(o[:, :], ident8[:, r:r + 1].broadcast_to([ND2, P]), r_f, start=True, stop=False)
                    cut = (cut_after_one, causal_one)[d].rearrange("p (o l) -> p o l", o=1).broadcast_to([P, NT, P])
                    made(pe.matmul(o[:, :], ident_one, cut, start=False, stop=True), ("bc", h, d))
                    o = tile(("up", h, d))
                    pe.wait_ge(kw_ready, 2 * h + d + 1)
                    for t in range(NT):
                        taken(pe, ("mv", t))
                    for c in range(3):
                        n = c if d == 0 else NT - 1 - c
                        mm = pe.matmul(o[:, c * (P + 1):(c + 1) * (P + 1)], kw[h % 2][d][c], v1[:, n, h, :], start=True, stop=True)
                    made(mm, ("up", h, d))

            def head_end(h):
                for d in range(2):
                    o = tile(("in", h, d))
                    taken(pe, ("up", h, d))
                    for c in range(1, NT):
                        n = c if d == 0 else NT - 1 - c
                        mm = pe.matmul(o[:, (c - 1) * (P + 1):c * (P + 1)], qT[:, h, n * P:(n + 1) * P], state[h % 2][d][:, c - 1, :],
                                       start=True, stop=True)
                    made(mm, ("in", h, d))
                    if d == 0:
                        pe.wait_ge(p_ready, h + 1)
                    else:
                        taken(pe, ("s", h))
                    for m in range(2):
                        o = tile(("nd", h, d, m))
                        for j in range(2):
                            n = 2 * m + j
                            mm = pe.matmul(o[:, j * (P + 1):(j + 1) * (P + 1)], wts[h % 2][d][:, n, :], v1[:, n, h, :],
                                           start=True, stop=True)
                        made(mm, ("nd", h, d, m))

            def turn_out(j):
                if j < MH:
                    pe.wait_ge(yn_m_ready, j + 1)
                else:
                    pe.wait_ge(yn_h_ready, NT)
                source = hm if j < MH else sig[2]
                o = tile(("yT", j))
                for t in range(NT):
                    to = o[:, t * P:(t + 1) * P]
                    if j >= MH:
                        to = o[:, :].rearrange("p (m two) -> p two m", two=2)[:, t // NF, t % NF * P:(t % NF + 1) * P]
                    mm = pe.transpose(to, source[:, t, (j % MH) * P:(j % MH + 1) * P], ident)
                made(mm, ("yT", j))

            pe.wait_ge(masks_ready, 1)
            turn_keys(0)
            project("mv")
            head_begin(0)
            spectrum(1)
            turn_keys(1)
            project("mo")
            back(1)
            head_begin(1)
            turn_keys(2)
            head_end(0)
            head_begin(2)
            turn_keys(3)
            head_end(1)
            head_begin(3)
            head_end(2)
            for j in range(MH, ND):
                turn_out(j)
            head_end(3)
            project_part("out0", 0)
            turn_out(0)
            turn_out(1)
            project_part("out0", 1)
            turn_out(2)
            project_part("out0", 2)
            turn_out(3)
            project_part("out0", 3)
            project_by_tile("out1", lambda t: turn_earlier(1, t))

            first = [BANK[("ff1", f)] for f in range(8)]

            def up_part(j, cols):
                b = first[j % 8][0]
                w = [v.rearrange("p (k n) -> p k n", k=ND) for v in piece_shape(UP + j)[1]]
                for k in range(ND):
                    mm = product(ps[b][:, cols], [v[:, k, :] for v in w], (xh[:, k, cols], xl[:, k, cols]), k == 0, k == ND - 1)
                return mm

            def project_up(j, cols, tokens):
                b, k = first[j]
                pe.wait_ge(split_ready, UP + j + 1)
                pe.wait_ge(bank_free[b], k)
                mm = up_part(j, cols)
                if tokens[0]:
                    mm.then_inc(bank_full[b], 1)

            project_renewed(1, project_up)
            at_tile[0] += NFF
            for j in range(4, 8):
                b, k = first[j]
                pe.wait_ge(split_ready, UP + j + 1)
                pe.wait_ge(bank_free[b], k)
                up_part(j, slice(0, S)).then_inc(bank_full[b], 1)
            with pe.Fori(1, NFF // 8) as i:
                for j in range(8):
                    b, k = first[j]
                    pe.wait_ge(split_ready, 8 * i + (UP + j + 1))
                    pe.wait_ge(bank_free[b], k + i)
                    up_part(8 + j, slice(0, S)).then_inc(bank_full[b], 1)
            down = [tile(("ff2", n)) for n in range(2 * NT)]

            def down_part(f, n):
                t, half = n // 2, n % 2
                w = piece_shape(DOWN + f)[1]
                tok = slice(t * P, (t + 1) * P)
                return product(down[n][:, :], [v[:, tok] for v in act_parts(f)], [v[:, half * 512:(half + 1) * 512] for v in w],
                               f == 0, f == NFF - 1)

            for f in range(NFF):
                pe.wait_ge(split_ready, DOWN + f + 1)
                pe.wait_ge(act_split, f + 1)
                if f < NFF - 4:
                    for n in range(2 * NT):
                        mm = down_part(f, n)
                    mm.then_inc(piece_used, 1)
            for n in range(2 * NT):
                for f in range(NFF - 4, NFF):
                    mm = down_part(f, n)
                made(mm, ("ff2", n))
                if n % 2 == 0:
                    turn_earlier(2, n // 2)

            project_renewed(2, lambda *args: project_first("index", *args), [name for name, *_ in GROUPS["index"][3]])
            project("fq")
            for n in (("iq", 0), ("iq", 1), ("ik", 0)):
                taken(pe, n)
            o = tile(("iw", 0))
            own = slice(ID, ID + IH)
            for t in range(NT):
                mm = pe.transpose(o[:, t * IH:(t + 1) * IH], iw_T[:, t * P:(t + 1) * P], ident[own, own])
            made(mm, ("iw", 0))
            for i, g in enumerate(("fk", "fg", None), 1):
                for h in range(IH):
                    o = tile(("ix", i, h))
                    r = ID * (h % 4)
                    made(pe.matmul(o[:, 0:(i + 1) * P], iqT[r:r + ID, h // 4, i * P:(i + 1) * P],
                                   ikT[r:r + ID, 0:(i + 1) * P], start=True, stop=True), ("ix", i, h))
                if g:
                    project(g)
            o = tile(("ff", 0))
            for t in range(NT):
                taken(pe, ("fg", t))
                mm = pe.transpose(o[0:AH, t * P:(t + 1) * P], fgate_tok[:, t, :], ident)
            made(mm, ("ff", 0))
            project("fv")

            def scores(kind, h):
                if kind == "f":
                    pe.wait_ge(nf_ready, 1)
                    one = ident8[0:AH, h:h + 1].broadcast_to([AH, P])
                    made(pe.matmul(tile(("nF", h))[:, :], one, f_n, start=True, stop=True), ("nF", h))
                if h % 2 == 0:
                    taken(pe, (kind + "q", h // 2))
                    taken(pe, (kind + "k", h // 2))
                r = HD * (h % 2)
                q, k = qkT[kind + "q"], qkT[kind + "k"]
                for i in range(NT):
                    o = tile((kind + "s", h, i))
                    mm = pe.matmul(o[:, 0:(i + 1) * P], q[r:r + HD, h // 2, i * P:(i + 1) * P],
                                   k[r:r + HD, h // 2, 0:(i + 1) * P], start=True, stop=(kind == "d"))
                    if kind == "f":
                        mm = pe.matmul(o[:, i * P:(i + 1) * P], ident_one, causal_one, start=False, stop=True)
                    made(mm, (kind + "s", h, i))

            def values(n, kind, h):
                pr, pt = prob[n % 3], probT[n % 2]
                at0 = 0
                for i in range(NT):
                    o = tile((kind + "T", h, i))
                    pe.wait_ge(prob_ready, NT * n + i + 1)
                    for s in range(i + 1):
                        mm = pe.transpose(o[:, s * P:(s + 1) * P], pr[:, (at0 + s) * P:(at0 + s + 1) * P], ident)
                    made(mm, (kind + "T", h, i))
                    at0 += i + 1
                if h == 0:
                    for t in range(NT):
                        taken(pe, (kind + "v", t))
                o = tile((kind + "o", h))
                at0 = 0
                for i in range(NT):
                    taken(pe, (kind + "T", h, i))
                    for s in range(i + 1):
                        mm = pe.matmul(o[:, i * HD:(i + 1) * HD], pt[:, at0 + s, :], vtok[kind][:, s, h * HD:(h + 1) * HD],
                                       start=(s == 0), stop=(s == i))
                    at0 += i + 1
                made(mm, (kind + "o", h))

            for n, (kind, h) in enumerate(HEADS):
                scores(kind, h)
                if n >= LAG:
                    values(n - LAG, *HEADS[n - LAG])
                if n in BETWEEN:
                    project(BETWEEN[n])
            pe.wait_ge(ld_pool, 16 * 4)
            for j in range(PW // P):
                pe.wait_ge(win_ready, j + 1)
                made(pe.matmul(tile(("mix_pool", j))[:, :], pool_w[:, j, :], win[2 + j], start=True, stop=True),
                     ("mix_pool", j))

            def turn_heads(j):
                kind, c = ("d", j) if j < 3 else ("f", j - 3)
                pe.wait_ge(og_ready, 2 * (c + 1) + AH * (kind == "d"))
                o = tile(("mT", j))
                for t in range(NT):
                    mm = pe.transpose(o[:, t * P:(t + 1) * P], otok[kind][:, t, c * P:(c + 1) * P], ident)
                made(mm, ("mT", j))

            for j in (3, 4, 5):
                turn_heads(j)
            project_part("fin0", 0)
            turn_heads(0)
            turn_heads(1)
            for n in range(len(HEADS) - LAG, len(HEADS)):
                values(n, *HEADS[n])
            project_part("fin0", 1)
            turn_heads(2)
            project_part("fin0", 2)
            project_part("fin0", 3)
            project_by_tile("fin1", lambda t: None)
            assert at_tile[0] == len(order)

        @block.scalar
        def _(ac):
            done = stepper(ac, act_step)

            done_squares = []

            def square(s, half, t, source):
                m = len(done_squares)
                if m >= 4:
                    ac.wait_ge(*done_squares[m - 4])
                ac.activation(junk[s][:, m % 4, :], source, ACT.Square, scale=D ** -0.5, accum_out=sumsq[:, s, half, t:t + 1])\
                  .then_inc(sumsq_ready[s], 1)
                done_squares.append((sumsq_ready[s], 1 + sum(d[0] is sumsq_ready[s] for d in done_squares)))

            def square_x(s, t):
                for half in range(2):
                    if s:
                        ac.wait_ge(x_ready, 2 * NT * (s // 2 - 1) + 2 * t + half + 1)
                    square(s, half, t, x[:, t, half * 512:(half + 1) * 512])

            def normed(s, t):
                _, n, xn = NORMS[s]
                ac.wait_ge(rstd_ready[n], t + 1)
                ac.activation(xn[:, t, :], x[:, t, :], ACT.Copy, scale=rstd[:, n, t:t + 1]).then_inc(xn_ready, 1)

            def take_norm(s, t):
                for half in range(2):
                    name = ("nT", s, t, half)
                    taken(ac, name)
                    v = turned[(XL[name] - 1) % 4].rearrange("p (d n) -> p d n", d=4)
                    ac.activation(xh[:, 4 * half:4 * half + 4, t * P:(t + 1) * P], v, ACT.Copy).then_inc(xh_ready, 1)

            def high(n):
                src, (hi, _) = piece_shape(n)
                ac.wait_ge(raw_loaded[n // 2 % 2], 32 * (n // 4 + 1))
                place_free(ac, n)
                ac.activation(hi, src, ACT.Copy).then_inc(high_ready, 1)

            def highs(g, *pieces):
                for i in pieces:
                    high(PIECE[g] + i)

            def renew(s, product, after):
                def square_first(t):
                    if s == 2:
                        square(2 * s - 1, 0, t, full(ac, product(t, 0))[:, :])

                square_first(0)
                for t in range(NT):
                    square(2 * s - 1, 1, t, full(ac, product(t, 1))[:, :])
                    if t >= 1:
                        normed(s, t - 1)
                    if t >= 2:
                        take_norm(s, t - 2)
                    if t + 1 < NT:
                        square_first(t + 1)
                    square_x(2 * s, t)
                normed(s, NT - 1)
                high(after)
                take_norm(s, NT - 2)
                high(after + 1)
                take_norm(s, NT - 1)

            def sine(n):
                ac.wait_ge(sin_arg_ready, n + 1)
                ac.activation(hidden, sin_arg, ACT.Sin).then_inc(hidden_ready, 1)

            def conv_bias(n):
                if n >= 16:
                    full(ac, ("cvT", n - 8))
                if n < 8:
                    full(ac, ("cvT", n + 12))
                name = ("cv", n)
                o = full(ac, name)[:, :]
                ac.activation(conv[n], o, ACT.Identity, bias=scol(ROW_CONV_B + n), scale=scol(ROW_CONV_W + NCT + n))
                if CONV[n] > 4:
                    ac.wait_ge(conv_ready, CONV[n] - 4)
                else:
                    ac.wait_ge(xn_ready, NT)
                free(ac.activation(proj[:, n % 4, :], o, ACT.Copy), name)

            def take_turned(n):
                name = ("cvT", n)
                q, j = (n - 8) // 4, n % 4
                full(ac, ("K", q if n < 12 else 1, 1, NF - 1, 1))
                free(ac.activation(sig[q][:, :, j * P:(j + 1) * P],
                                   full(ac, name)[:, :].rearrange("p (t c) -> p t c", t=NT), ACT.Copy), name)

            for t in range(NT + 1):
                if t < NT:
                    ac.wait_ge(ld_x[t], 16)
                    square_x(0, t)
                if t >= 1:
                    normed(0, t - 1)
            take_norm(0, 0)
            take_norm(0, 1)
            highs("hv", 0)
            take_norm(0, 2)
            highs("hv", 1, 2, 3)
            sine(0)
            take_norm(0, 3)
            sine(1)
            sine(2)
            highs("hx1", 0, 1)
            for n in range(8, 12):
                conv_bias(n)
            def take_even(o, name):
                free(ac.activation(o, full(ac, name)[:, :], ACT.Copy), name)

            def take_spectrum(q):
                for f in range(NF):
                    if q or f:
                        ac.wait_ge(wave_used, NF * q + f)
                    for c in range(2):
                        take_even(wave[c], ("US"[c], q, f, 0))

            for q in range(2):
                for c in range(2):
                    for f in range(NF):
                        take_even(spec[q][c][:, f, :], ("K", q, c, f, 0))
            highs("hx1", 2, 3)
            highs("hx2", 0, 1)
            for n in range(12, 16):
                conv_bias(n)
            for n in range(8, 12):
                take_turned(n)
            ac.wait_ge(gate_abs, 1)
            done(ac.activation(r_a, r_a, ACT.Exp, scale=-1.0))
            ac.activation(r_a, r_a, ACT.Ln, bias=one_col[0:ND2, :]).then_inc(softplus_ready, 1)
            highs("hx2", 2, 3)
            highs("mq", 0, 1)
            for n in range(16, 20):
                conv_bias(n)
            for n in range(12, 16):
                take_turned(n)
            ac.wait_ge(exp_args, 1)
            ac.activation(r_den, r_den, ACT.Exp, scale=-1.0).then_inc(exps_ready, 1)
            ac.activation(r_in, r_in, ACT.Exp).then_inc(exps_ready, 1)
            ac.activation(r_w, r_w, ACT.Exp).then_inc(exps_ready, 1)
            ac.activation(dec8[:, :], dec8[:, :], ACT.Exp).then_inc(exps_ready, 1)
            highs("mq", 2, 3)
            highs("mk", 0, 1)
            for n in range(4):
                conv_bias(n)
            for n in range(16, 20):
                take_turned(n)
            take_spectrum(0)
            highs("mk", 2, 3)
            highs("mv", 0, 1)
            for n in range(4, 8):
                conv_bias(n)
            for n in range(8):
                ac.wait_ge(conv_ready, CONV[n])
                if n < 4:
                    ac.activation(qT[:, n, :], conv[n], ACT.Silu).then_inc(q_ready, 1)
                else:
                    ac.activation(kT[:, n - 4, :], conv[n], ACT.Silu).then_inc(k_silu, 1)

            def take_keys(h):
                name = ("kt", h)
                if h < 2:
                    ac.wait_ge(long_ready, NT)
                else:
                    ac.wait_ge(kw_ready, 2 * h - 2)
                free(ac.activation(ktok[h % 2], full(ac, name)[:, :].rearrange("p (c d) -> p c d", c=NT), ACT.Copy), name)

            def head_begin(h):
                taken(ac, ("gcol",))
                for d in range(2):
                    r = d * MH + h
                    name = ("bc", h, d)
                    o = full(ac, name)
                    if h >= 2:
                        full(ac, ("nd", h - 2, d, 1))
                    for c in range(NT):
                        i = ac.activation(wts[h % 2][d][:, c, :], o[:, c * P:(c + 1) * P], ACT.Exp, bias=gcol[:, 0, c, r:r + 1])
                    free(i, name)
                    o = full(ac, ("up", h, d))
                    if h >= 2:
                        full(ac, ("in", h - 2, d))
                    ac.activation(state[h % 2][d][:, 0, :], o[:, 0:P + 1], ACT.Copy).then_inc(first_state, 1)

            def square_head(h):
                ac.wait_ge(gated, h + 1)
                for t in range(NT):
                    ac.activation(sq_m[:, t, h * P:(h + 1) * P], hm[:, t, h * P:(h + 1) * P], ACT.Square, scale=P ** -0.5,
                                  accum_out=sumsq_m[:, h, t:t + 1]).then_inc(sumsq_m_ready, 1)

            def head_end(h):
                for d in range(2):
                    name = ("in", h, d)
                    o = full(ac, name)
                    if d or h >= 2:
                        for m in range(2):
                            taken(ac, ("nd", h, 0, m) if d else ("nd", h - 2, 1, m))
                    for c in range(1, NT):
                        n = c if d == 0 else NT - 1 - c
                        i = ac.activation(inter[h % 2][:, n, :], o[:, (c - 1) * (P + 1):c * (P + 1)], ACT.Copy,
                                          scale=gcol[:, 2, n, d * MH + h:d * MH + h + 1])
                    free(i, name)

            def take_out(j):
                name = ("yT", j)
                row = ROW_MLSTM_W + j if j < MH else ROW_HYENA_W + j - MH
                ac.activation(xh[:, j, :], full(ac, name)[:, :], ACT.Copy, scale=scol(row)).then_inc(xh_ready, 1)

            take_keys(0)
            highs("mv", 2, 3)
            highs("mo", 0, 1)
            ac.wait_ge(v1_ones, 1)
            for t in range(NT):
                name = ("mv", t)
                free(ac.activation(v1[:, t, :, 0:P], full(ac, name)[:, :].rearrange("p (h c) -> p h c", h=MH), ACT.Copy), name)
            head_begin(0)
            take_spectrum(1)
            take_keys(1)
            highs("mo", 2, 3)
            highs("out0", 0, 1)
            ac.wait_ge(xn_ready, NT)
            for t in range(NT):
                name = ("mo", t)
                free(ac.activation(o_gate[:, t, :], full(ac, name)[:, :], ACT.Sigmoid), name)
            head_begin(1)
            take_keys(2)
            head_end(0)
            head_begin(2)
            take_keys(3)
            head_end(1)
            square_head(0)
            head_begin(3)
            head_end(2)
            square_head(1)
            for j in range(MH, ND):
                take_out(j)
            head_end(3)
            square_head(2)
            square_head(3)
            take_out(0)
            take_out(1)
            highs("out0", 2)
            highs("out0", 3)
            take_out(2)
            take_out(3)
            highs("out1", 0, 1)
            for t in range(NT):
                square(1, 0, t, full(ac, ("mx00", t))[:, :])
            highs("out1", 2, 3)
            high(UP)
            high(UP + 1)
            renew(1, lambda t, half: ("mx01", t), UP + 2)
            first = [BANK[("ff1", f)] for f in range(8)]

            def relu_up(i, j):
                b, k = first[j]
                ac.wait_ge(bank_full[b], i + (k + 1))
                ac.wait_ge(act_ready, 8 * i + (j + 1))
                ac.activation(relu[j % 4], ps[b][:, :], ACT.Relu).then_inc(bank_free[b], 1)

            for j in range(8):
                relu_up(0, j)
                if j >= 2:
                    high(UP + j + 2)
            with ac.Fori(1, NFF // 8 - 1) as i:
                for j in range(8):
                    relu_up(i, j)
                    src, (hi, _) = piece_shape(UP + j + 2 + 8)
                    ac.wait_ge(raw_loaded[(j + 2) // 2 % 2], 64 * i + 32 * ((UP + j + 2) // 4 + 1))
                    ac.activation(hi, src, ACT.Copy).then_inc(high_ready, 1)

            def act_part(f):
                ac.wait_ge(act_ready, 4 + f + 1)
                if AHEAD <= f < AHEAD + ND:
                    full(ac, ("ff1", NFF - 1))
                elif f >= AHEAD:
                    used(ac, DOWN + f - ND)
                ac.activation(act_parts(f)[0], act[:, f, :], ACT.Copy).then_inc(act_high, 1)

            for j in range(8):
                relu_up(NFF // 8 - 1, j)
                high(DOWN - 8 + j + 2)
                if j >= 8 - AHEAD:
                    act_part(j - 8 + AHEAD)
            for f in range(NFF):
                if f + AHEAD < NFF:
                    act_part(f + AHEAD)
                if f + 2 < NFF:
                    if f + 2 == NFF - 4:
                        ac.wait_ge(act_split, 8)
                    high(DOWN + f + 2)
            ac.wait_ge(act_split, 24)
            highs("index", 0, 1, 2, 3)
            renew(2, lambda t, half: ("ff2", 2 * t + half), PIECE["fq"])
            for j in range(2):
                name = ("iq", j)
                free(ac.activation(iqT[:, j, :], full(ac, name)[:, :], ACT.Copy), name)
            name = ("ik", 0)
            o = full(ac, name)
            for r in range(4):
                ac.activation(ikT[r * ID:(r + 1) * ID, :], o[0:ID, :], ACT.Copy)
            free(ac.activation(iw_T, o[ID:ID + IH, :], ACT.Copy, scale=IH ** -0.5), name)

            def relus(i):
                for h in range(IH):
                    n = (i - 1) * IH + h
                    name = ("ix", i, h)
                    o = full(ac, name)
                    if n >= 2:
                        ac.wait_ge(rdot_used, n - 1)
                    free(ac.activation(rdot[n % 2][:, 0:(i + 1) * P], o[:, 0:(i + 1) * P], ACT.Relu), name)

            def take(g):
                for name, kind, _, _ in GROUPS[g][3]:
                    o = full(ac, name)
                    what, j = name
                    if what in ("fq", "dq"):
                        i = ac.activation(qkT[what][:, j, :], o[:, :], ACT.Copy, scale=HD ** -0.5)
                    elif what in ("fk", "dk"):
                        i = ac.activation(qkT[what][:, j, :], o[:, :], ACT.Copy)
                    elif what in ("fv", "dv"):
                        i = ac.activation(vtok[what[0]][:, j, :], o[:, 0:AW], ACT.Copy)
                    elif what in ("fg", "dg"):
                        i = ac.activation(gtok[what[0]][:, j, :], o[:, 0:AW], ACT.Silu)
                        if what == "fg":
                            i = ac.activation(fgate_tok[:, j, :], o[:, AW:AW + AH], ACT.Copy)
                    elif what == "pv":
                        ac.wait_ge(sel_ready, NT - 1)
                        i = ac.activation(pvT[:, j, :], o[:, :], ACT.Copy)
                    elif what == "pg":
                        i = ac.activation(pgT[:, j, :], o[:, :], ACT.Silu)
                    else:
                        continue
                    free(i, name)

            highs("fq", 2, 3)
            highs("fk", 0, 1)
            take("fq")
            relus(1)
            highs("fk", 2, 3)
            highs("fg", 0, 1)
            take("fk")
            relus(2)
            highs("fg", 2, 3)
            highs("fv", 0, 1)
            take("fg")
            relus(3)
            ac.wait_ge(fgate_abs, 1)
            done(ac.activation(f_a, f_a, ACT.Exp, scale=-1.0))
            ac.activation(f_a, f_a, ACT.Ln, bias=one_col[0:AH, :]).then_inc(fsoft_ready, 1)
            highs("fv", 2, 3)
            highs("dq", 0, 1)
            take("fv")

            def forget_rows(n, h):
                name = ("nF", h)
                if n >= 2:
                    ac.wait_ge(smax_ready, n - 1)
                free(ac.activation(nf_bc[n % 2], full(ac, name)[:, :], ACT.Copy), name)

            def exps(n, kind, h):
                ac.wait_ge(smax_ready, n + 1)
                at0 = 0
                for i in range(NT):
                    w = (i + 1) * P
                    p = prob[n % 3][:, at0 * P:at0 * P + w]
                    ac.activation(p, p, ACT.Exp, bias=smax[:, n % 3, i:i + 1], accum_out=ssum[:, n % 3, i:i + 1])\
                      .then_inc(prob_ready, 1)
                    at0 += i + 1

            def take_probs(n, kind, h):
                at0 = 0
                for i in range(NT):
                    name = (kind + "T", h, i)
                    o = full(ac, name)
                    if n >= 2:
                        k2, h2 = HEADS[n - 2]
                        full(ac, (k2 + "o", h2))
                    free(ac.activation(probT[n % 2][:, at0:at0 + i + 1, :],
                                       o[:, 0:(i + 1) * P].rearrange("p (s c) -> p s c", s=i + 1), ACT.Copy), name)
                    at0 += i + 1

            for n, (kind, h) in enumerate(HEADS):
                if kind == "f":
                    forget_rows(n, h)
                if n >= LAG:
                    take_probs(n - LAG, *HEADS[n - LAG])
                exps(n, kind, h)
                if n in BETWEEN:
                    g = BETWEEN[n]
                    highs(g, 2, 3)
                    highs(GROUP_ORDER[group_at[g] + 1], 0, 1)
                    take(g)
            for j in range(PW // P):
                taken(ac, ("mix_pool", j))
                ac.activation(xh[:, j, :], pooled[j], ACT.Copy).then_inc(xh_ready, 1)

            def take_heads(j):
                ac.activation(xh[:, 2 + j, :], full(ac, ("mT", j))[:, :], ACT.Copy).then_inc(xh_ready, 1)

            for j in (3, 4, 5, 0, 1):
                take_heads(j)
            take_probs(len(HEADS) - 2, *HEADS[-2])
            highs("fin0", 2)
            take_probs(len(HEADS) - 1, *HEADS[-1])
            highs("fin0", 3)
            take_heads(2)
            highs("fin1", 0, 1, 2, 3)
            for half in range(2):
                for t in range(NT):
                    taken(ac, (f"fx{half}", t))
                    square(5, half, t, x[:, t, half * 512:(half + 1) * 512])

        @block.vector
        def _(ve):
            done = stepper(ve, dve_step)

            def take_norm(s, t):
                row = NORMS[s][0]
                for half in range(2):
                    name = ("nT", s, t, half)
                    n = XL[name] - 1
                    weight = scol(row + 4 * half, 4).rearrange("p (d o) -> p d o", o=1).broadcast_to([P, 4, P])
                    if n >= 4:
                        ve.wait_ge(xl_ready, n - 3)
                    free(ve.tensor_tensor(turned[n % 4].rearrange("p (d n) -> p d n", d=4),
                                          full(ve, name)[:, :].rearrange("p (d n) -> p d n", d=4), weight, ALU.mult), name)

            def split_norm(s, t):
                for half in range(2):
                    name = ("nT", s, t, half)
                    v = turned[(XL[name] - 1) % 4].rearrange("p (d n) -> p d n", d=4)
                    at_x = (slice(None), slice(4 * half, 4 * half + 4), slice(t * P, (t + 1) * P))
                    ve.wait_ge(xh_ready, XH[name])
                    ve.tensor_tensor(xl[at_x], v, xh[at_x].bitcast(F32), ALU.subtract).then_inc(xl_ready, 1)

            def lows(g, *pieces):
                for i in pieces:
                    low_part(ve, PIECE[g] + i)

            def split_out(j):
                name = ("yT", j)
                row = ROW_MLSTM_W + j if j < MH else ROW_HYENA_W + j - MH
                o = full(ve, name)
                ve.wait_ge(xh_ready, XH[name])
                free(ve.scalar_tensor_tensor(out=xl[:, j, :], in0=o[:, :], scalar=scol(row), in1=xh[:, j, :].bitcast(F32),
                                             op0=ALU.mult, op1=ALU.subtract), name)

            def sine_arg(n):
                name = ("f", n)
                free(ve.tensor_scalar(sin_arg, full(ve, name)[0:FHID, :], fcol[:, n:n + 1], fcol[:, 3 + n:4 + n],
                                      ALU.add, ALU.mult), name)
                taken(ve, name)
                done(ve.tensor_scalar(sin_turn, sin_arg, 1.0 / (2 * np.pi), MAGIC, ALU.mult, ALU.add))
                done(ve.tensor_scalar(sin_turn, sin_turn, MAGIC, None, ALU.subtract))
                for part in (TWO_PI_HI, TWO_PI_LO):
                    done(ve.scalar_tensor_tensor(out=sin_arg, in0=sin_turn, scalar=-part, in1=sin_arg,
                                                 op0=ALU.mult, op1=ALU.add))
                ve.tensor_scalar(sin_arg, sin_arg, PI, -PI, ALU.min, ALU.max).then_inc(sin_arg_ready, 1)

            free(ve.tensor_copy(colv[:, :], full(ve, ("cols",))[:, 0:N_ROWS]), ("cols",))
            taken(ve, ("cols",))
            take_norm(0, 0)
            take_norm(0, 1)
            split_norm(0, 0)
            split_norm(0, 1)
            take_norm(0, 2)
            free(ve.tensor_copy(fcol[:, :], full(ve, ("fcols",))[0:FHID, 0:6]), ("fcols",))
            taken(ve, ("fcols",))
            sine_arg(0)
            split_norm(0, 2)
            take_norm(0, 3)
            split_norm(0, 3)
            sine_arg(1)
            sine_arg(2)
            ve.wait_ge(ld_rows, 16 * 6)
            ve.wait_ge(xn_ready, NT)
            o = full(ve, ("gate",))
            ve.tensor_scalar(r_i, o[0:ND2, :], gbias[:, 0:1], None, ALU.add)
            free(ve.tensor_scalar(r_f, o[GF:GF + ND2, :], gbias[:, 1:2], None, ALU.add), ("gate",))
            def short_conv(lo):
                for n in range(lo, lo + 4):
                    taken(ve, ("cv", n))
                    u, c = proj[:, n % 4, :], conv[n]
                    done(ve.scalar_tensor_tensor(out=c[:, 1:S], in0=u[:, 0:S - 1], scalar=scol(ROW_CONV_W + n),
                                                 in1=c[:, 1:S], op0=ALU.mult, op1=ALU.add))
                    ve.scalar_tensor_tensor(out=c[:, 0:S - 1], in0=u[:, 1:S], scalar=scol(ROW_CONV_W + 2 * NCT + n),
                                            in1=c[:, 0:S - 1], op0=ALU.mult, op1=ALU.add).then_inc(conv_ready, 1)

            ve.wait_ge(ld_window, 32)
            n = 0
            for q in range(2):
                for t in range(NT):
                    name = ("ft", q, t, 0)
                    free(ve.tensor_tensor(tap_sum[q][:, t, :], full(ve, name)[:, :], window[:, t, :], ALU.mult), name)
                    name = ("ft", q, t, 1)
                    if n >= 2:
                        ve.wait_ge(taps_ready, n - 1)
                    w = window_b if t == 0 else window[:, t, :]
                    free(ve.tensor_tensor(taps_b[n % 2], full(ve, name)[:, :], w, ALU.mult), name)
                    n += 1
            lows("hx1", 0, 1)
            short_conv(8)

            def add_odd(even, odd, plus, minus, sign):
                taken(ve, even)
                o = full(ve, odd)[:, :]
                a, b = (plus, o) if sign > 0 else (o, plus)
                done(ve.tensor_tensor(minus, a, b, ALU.subtract))
                free(ve.tensor_tensor(plus, plus, o, ALU.add), odd)

            for q in range(2):
                for c in range(2):
                    for f in range(NF):
                        add_odd(("K", q, c, f, 0), ("K", q, c, f, 1), spec[q][c][:, f, :], spec[q][c][:, NF + f, :], 1 - 2 * c)

            def products(q, f):
                n = NF * q + f
                up, sp = wave
                for c, (plus, minus) in enumerate(zip(wave, wave_minus[f])):
                    even, odd = ("US"[c], q, f, 0), ("US"[c], q, f, 1)
                    taken(ve, even)
                    o = full(ve, odd)[:, :]
                    a, b = (plus, o) if c == 0 else (o, plus)
                    ve.tensor_tensor(minus, a, b, ALU.subtract).then_inc(minus_ready, 1)
                    ve.wait_ge(minus_ready, 2 * n + c + 1)
                    free(ve.tensor_tensor(plus, plus, o, ALU.add), odd)
                for c in range(2):
                    taken(ve, ("US"[c], q, f, 1))
                k0, k1 = (spec[q][c][:, f, :] for c in range(2))
                for c in range(2):
                    taken(ve, ("K", q, c, f, 1))
                done(ve.tensor_tensor(wave_tmp[0], up, k1, ALU.mult))
                ve.tensor_tensor(k1, sp, k1, ALU.mult)
                done(ve.tensor_tensor(up, up, k0, ALU.mult))
                ve.tensor_tensor(k0, sp, k0, ALU.mult)
                ve.tensor_tensor(k1, k1, up, ALU.add).then_inc(wave_used, 1)
                ve.wait_ge(wave_used, n + 1)
                done(ve.tensor_tensor(k0, k0, wave_tmp[0], ALU.subtract))

            def combine(q, f):
                n = NF * q + f
                k0, k1, k0m, k1m = (spec[q][c][:, i, :] for i in (f, NF + f) for c in range(2))
                ve.wait_ge(mirror_ready, n + 1)
                for a, b in ((k1, k1m), (k0, k0m)):
                    done(ve.tensor_tensor(b, a, b, ALU.subtract))
                for a, b in ((k1, k1m), (k0, k0m)):
                    i = ve.scalar_tensor_tensor(out=a, in0=a, scalar=2.0, in1=b, op0=ALU.mult, op1=ALU.subtract)
                i.then_inc(spec_ready, 1)

            def long_conv(q, t):
                ve.wait_ge(skip_ready, NT * q + t + 1)
                name = ("y", q, t)
                g = sig[q + 1][:, t, :]
                z = sig[q][:, t, :]
                for n in range(12, 20):
                    taken(ve, ("cvT", n))
                free(ve.tensor_tensor(z, full(ve, name)[:, :], z, ALU.add), name)
                taken(ve, name)
                ve.tensor_tensor(g, z, g, ALU.mult).then_inc(long_ready, 1)

            lows("hx1", 2, 3)
            lows("hx2", 0)

            def unflip(o, i):
                done(ve.tensor_scalar(o, i, is_f, None, ALU.mult))
                return ve.scalar_tensor_tensor(out=o, in0=i[:, ::-1], scalar=is_b, in1=o, op0=ALU.mult, op1=ALU.add)

            def chunks(r):
                return r.rearrange("k (c l) -> k c l", c=NT)

            taken(ve, ("gate",))
            full(ve, ("K", 1, 1, NF - 1, 1))
            done(unflip(r_e, r_i))
            done(unflip(r_lf, r_f))
            ve.scalar_tensor_tensor(out=r_a, in0=r_lf, scalar=-1.0, in1=r_lf, op0=ALU.mult, op1=ALU.max).then_inc(gate_abs, 1)
            done(ve.tensor_scalar(r_lf, r_lf, 0.0, None, ALU.min))
            lows("hx2", 1)
            short_conv(12)
            lows("hx2", 2)
            ve.wait_ge(softplus_ready, 1)
            done(ve.tensor_tensor(r_lf, r_lf, r_a, ALU.subtract))
            done(ve.tensor_tensor_scan(r_b, chunk_reset, r_lf, 0.0, ALU.mult, ALU.add))
            done(ve.tensor_tensor(r_e, r_e, r_b, ALU.subtract))
            done(ve.memset(m_start[:, :], 0.0))
            for c in range(NT):
                cs = slice(c * P, (c + 1) * P)
                done(ve.tensor_tensor_scan(r_m[:, cs], r_e[:, cs], r_e[:, cs], m_start[:, c:c + 1], ALU.max, ALU.max))
                last = slice((c + 1) * P - 1, (c + 1) * P)
                done(ve.tensor_tensor(m_start[:, c + 1:c + 2], r_m[:, last], r_b[:, last], ALU.add))
            lows("hx2", 3)
            lows("mq", 0, 1)
            short_conv(16)
            m_last = chunks(r_m)[:, :, P - 1:P]
            ve.tensor_tensor(r_den, r_m, r_b, ALU.add)
            ve.tensor_tensor(chunks(r_in), m_start[:, 0:NT].rearrange("k (c o) -> k c o", o=1).broadcast_to([ND2, NT, P]),
                             chunks(r_m), ALU.subtract)
            ve.tensor_tensor(chunks(r_w), chunks(r_e), m_last.broadcast_to([ND2, NT, P]), ALU.subtract)
            ve.tensor_tensor(dec8[:, :].rearrange("k (c o) -> k c o", o=1),
                             m_start[:, 0:NT].rearrange("k (c o) -> k c o", o=1), m_last, ALU.subtract).then_inc(exp_args, 1)
            ve.wait_ge(exp_args, 1)
            done(ve.tensor_scalar(r_m, r_m, -1.0, None, ALU.mult))
            lows("mq", 2)
            ve.wait_ge(exps_ready, 4)
            done(unflip(r_i, r_e))
            done(unflip(r_f, r_m))
            done(unflip(r_a, r_den))
            done(unflip(r_b, r_in))
            unflip(r_lf, r_w).then_inc(rows_ready, 1)
            ve.tensor_tensor(dblk[:, :, :], dec8[:, :].rearrange("k (o c) -> k o c", o=1).broadcast_to([ND2, ND2, NT]),
                             ident8.rearrange("k (r o) -> k r o", o=1).broadcast_to([ND2, ND2, NT]), ALU.mult)\
              .then_inc(dblk_ready, 1)
            lows("mq", 3)
            lows("mk", 0, 1)
            short_conv(0)
            products(0, 0)
            lows("mk", 2)
            products(0, 1)
            lows("mk", 3)
            combine(0, 0)
            combine(0, 1)
            lows("mv", 0, 1)
            short_conv(4)
            for t in range(NT):
                long_conv(0, t)
            lows("mv", 2, 3)
            lows("mo", 0, 1)
            name = ("gcol",)
            free(ve.tensor_copy(gcol[:, :, :, :].rearrange("p a c r -> p (a c r)"),
                                full(ve, name)[:, 0:4 * NT * ND2]), name)
            name = ("decay",)
            free(ve.tensor_copy(decay[:, :, :].rearrange("p r c -> p (r c)"), full(ve, name)[:, 0:ND2 * NT]), name)
            taken(ve, ("gcol",))
            taken(ve, name)

            def head_begin(h):
                o = full(ve, ("s", h))[:, :].rearrange("p (c l) -> p c l", c=NT)
                for d in range(2):
                    r = d * MH + h
                    taken(ve, ("bc", h, d))
                    w = wts[h % 2][d]
                    i = ve.tensor_tensor(w, o, w, ALU.mult)
                    if d == 0:
                        i.then_inc(p_ready, 1)
                    else:
                        free(i, ("s", h))
                    name = ("up", h, d)
                    o_up = full(ve, name)
                    st = state[h % 2][d]
                    ve.wait_ge(first_state, 2 * h + d + 1)
                    done(ve.scalar_tensor_tensor(out=st[:, 1, :], in0=st[:, 0, :], scalar=decay[:, r, 1:2],
                                                 in1=o_up[:, P + 1:2 * (P + 1)], op0=ALU.mult, op1=ALU.add))
                    free(ve.scalar_tensor_tensor(out=st[:, 2, :], in0=st[:, 1, :], scalar=decay[:, r, 2:3],
                                                 in1=o_up[:, 2 * (P + 1):3 * (P + 1)], op0=ALU.mult, op1=ALU.add), name)

            def head_end(h):
                nd_h, inter_h = nd[h % 2], inter[h % 2]
                for d in range(2):
                    r = d * MH + h
                    first_n = 0 if d == 0 else NT - 1
                    taken(ve, ("in", h, d))
                    for m in range(2):
                        name = ("nd", h, d, m)
                        o = full(ve, name)
                        for j in range(2):
                            n = 2 * m + j
                            src = o[:, j * (P + 1):(j + 1) * (P + 1)]
                            if n == first_n:
                                i = ve.tensor_copy(nd_h[:, n, :], src)
                            else:
                                i = ve.tensor_tensor(nd_h[:, n, :], src, inter_h[:, n, :], ALU.add)
                        free(i, name)
                    taken(ve, ("nd", h, d, 0))
                    taken(ve, ("nd", h, d, 1))
                    dn = nd_h[:, :, P:P + 1]
                    q = den[:, 0, :].rearrange("p (c o) -> p c o", o=1)
                    done(ve.scalar_tensor_tensor(out=q, in0=dn, scalar=-1.0, in1=dn, op0=ALU.mult, op1=ALU.max))
                    done(ve.tensor_tensor(q, q, gcol[:, 1, :, r:r + 1], ALU.max))
                    done(ve.reciprocal(den[:, 1, :], den[:, 0, :]))
                    rec = den[:, 1, :].rearrange("p (c o) -> p c o", o=1).broadcast_to([P, NT, P])
                    hs = hm[:, :, h * P:(h + 1) * P]
                    if d == 0:
                        done(ve.tensor_tensor(hs, nd_h[:, :, 0:P], rec, ALU.mult))
                    else:
                        done(ve.tensor_tensor(nd_h[:, :, 0:P], nd_h[:, :, 0:P], rec, ALU.mult))
                        ve.tensor_tensor(hs, hs, nd_h[:, :, 0:P], ALU.add).then_inc(h_ready, 1)

            def hyena_sums():
                ve.wait_ge(sq_h_ready, NT)
                ve.tensor_reduce(sumsq_h[:, :], sq_h.rearrange("p t (g c) -> p (t g) c", g=HG), AX_X, ALU.add)\
                  .then_inc(gsum_h_ready, 1)

            def hyena_norm():
                ve.wait_ge(rstd_h_ready, 1)
                for t in range(NT):
                    y = sig[2][:, t, :].rearrange("p (g c) -> p g c", g=HG)
                    r = rstd_h[:, t * HG:(t + 1) * HG].rearrange("p (g o) -> p g o", o=1)
                    ve.tensor_tensor(y, y, r.broadcast_to([P, HG, HALF // HG]), ALU.mult).then_inc(yn_h_ready, 1)

            def mlstm_norm(h):
                ve.wait_ge(rstd_m_ready, h + 1)
                y = hm[:, :, h * P:(h + 1) * P]
                r = rstd_m[:, h, :].rearrange("p (t o) -> p t o", o=1)
                ve.tensor_tensor(y, y, r.broadcast_to([P, NT, P]), ALU.mult).then_inc(yn_m_ready, 1)

            head_begin(0)
            products(1, 0)
            products(1, 1)
            lows("mo", 2)
            combine(1, 0)
            lows("mo", 3)
            combine(1, 1)
            lows("out0", 0, 1)
            for t in range(NT):
                long_conv(1, t)
            head_begin(1)
            head_end(0)
            hyena_sums()
            head_begin(2)
            head_end(1)
            head_begin(3)
            hyena_norm()
            mlstm_norm(0)
            head_end(2)
            mlstm_norm(1)
            for j in range(MH, ND):
                split_out(j)
            head_end(3)
            split_out(0)
            split_out(1)
            mlstm_norm(2)
            lows("out0", 2)
            mlstm_norm(3)
            split_out(2)
            lows("out0", 3)
            split_out(3)
            lows("out1", 0, 1)

            def weigh(s, t, half, name, count):
                cols = slice(half * 512, (half + 1) * 512)
                ve.wait_ge(sumsq_ready[2 * s - 1], count)
                free(ve.tensor_tensor(mixed[:, t, cols], full(ve, name)[:, :], row_bc[:, cols], ALU.mult), name)

            def add(s, t):
                for _, name, _ in products_of(s, t):
                    taken(ve, name)
                ve.wait_ge(rstd_ready[2 * s - 1], t + 1)
                ve.wait_ge(ld_x[t], 32)
                for half in range(2):
                    cols = slice(half * 512, (half + 1) * 512)
                    ve.scalar_tensor_tensor(out=x[:, t, cols], in0=mixed[:, t, cols], scalar=rstd[:, 2 * s - 1, t:t + 1],
                                            in1=x[:, t, cols], op0=ALU.mult, op1=ALU.add).then_inc(x_ready, 1)

            def renew(s, after):
                def weigh_first(t):
                    if s == 2:
                        weigh(s, t, *products_of(s, t)[0])

                weigh_first(0)
                for t in range(NT):
                    weigh(s, t, *products_of(s, t)[1])
                    add(s, t)
                    if t >= 2:
                        split_norm(s, t - 2)
                    if t + 1 < NT:
                        weigh_first(t + 1)
                    if t >= 1:
                        take_norm(s, t - 1)
                low_part(ve, after)
                split_norm(s, NT - 2)
                take_norm(s, NT - 1)
                low_part(ve, after + 1)
                split_norm(s, NT - 1)

            def products_of(s, t):
                if s == 1:
                    return [(half, (f"mx0{half}", t), NT * half + t + 1) for half in range(2)]
                return [(half, ("ff2", 2 * t + half), 2 * t + half + 1) for half in range(2)]

            ve.wait_ge(ld_mix_post, 16)
            for t in range(NT):
                weigh(1, t, *products_of(1, t)[0])
            lows("out1", 2, 3)
            low_part(ve, UP)
            low_part(ve, UP + 1)
            renew(1, UP + 2)
            for j in range(2, 8):
                low_part(ve, UP + j + 2)
            with ve.Fori(1, NFF // 8 - 1) as i:
                for j in range(8):
                    src, (hi, lo) = piece_shape(UP + j + 2 + 8)
                    ve.wait_ge(high_ready, 8 * i + (UP + j + 3))
                    ve.tensor_tensor(lo, src, hi.bitcast(F32), ALU.subtract).then_inc(split_ready, 1)

            def act_part(f):
                hi, lo = act_parts(f)
                ve.wait_ge(act_high, f + 1)
                ve.tensor_tensor(lo, act[:, f, :], hi.bitcast(F32), ALU.subtract).then_inc(act_split, 1)

            for j in range(8):
                low_part(ve, DOWN - 8 + j + 2)
                if j >= 8 - AHEAD:
                    act_part(j - 8 + AHEAD)
            for f in range(NFF):
                if f + AHEAD < NFF:
                    act_part(f + AHEAD)
                if f + 2 < NFF:
                    low_part(ve, DOWN + f + 2)
            lows("index", 0, 1, 2, 3)
            ve.wait_ge(ld_mlp_post, 16)
            renew(2, PIECE["fq"])
            name = ("iw", 0)
            free(ve.tensor_copy(iw[:, :, :].rearrange("p t h -> p (t h)"), full(ve, name)[:, 0:NT * IH]), name)
            taken(ve, name)
            def choose(lo, hi):
                rounds = TOPK // 8
                for m in range(lo, hi):
                    i, n = 1 + m // rounds, m % rounds
                    w = (i + 1) * P
                    sc, wk = score[:, i - 1, 0:w], work[:, i - 1, 0:w]
                    src = sc if n == 0 else wk
                    done(ve.max(top8[:, :], src))
                    done(ve.match_replace(wk, top8[:, :], src, TAKEN))
                    if n == rounds - 1:
                        done(ve.tensor_tensor(sc, wk, sc, ALU.is_equal))
                        ve.tensor_scalar(sc, sc, NEG, None, ALU.mult).then_inc(sel_ready, 1)

            n = 0
            for i in range(1, NT):
                w = (i + 1) * P
                sc = score[:, i - 1, 0:w]
                for h in range(IH):
                    n += 1
                    taken(ve, ("ix", i, h))
                    r = rdot[(n - 1) % 2][:, 0:w]
                    if h == 0:
                        ins = ve.tensor_scalar(sc, r, iw[:, i, h:h + 1], None, ALU.mult)
                    else:
                        ins = ve.scalar_tensor_tensor(out=sc, in0=r, scalar=iw[:, i, h:h + 1], in1=sc, op0=ALU.mult, op1=ALU.add)
                    ins.then_inc(rdot_used, 1)
                    ve.wait_ge(rdot_used, n)
                done(ve.memset(score[0:HD, i - 1, w - HD:w], LOWEST))
                if i < NT - 1:
                    choose(0 if i == 1 else CHOICE_TILE[i - 2], CHOICE_TILE[i - 1])

            name = ("ff", 0)
            free(ve.tensor_scalar(f_f, full(ve, name)[0:AH, :], fbias[:, :], None, ALU.add), name)
            taken(ve, name)
            ve.scalar_tensor_tensor(out=f_a, in0=f_f, scalar=-1.0, in1=f_f, op0=ALU.mult, op1=ALU.max).then_inc(fgate_abs, 1)
            done(ve.tensor_scalar(f_f, f_f, 0.0, None, ALU.min))
            ve.wait_ge(fsoft_ready, 1)
            done(ve.tensor_tensor(f_f, f_a, f_f, ALU.subtract))
            ve.tensor_tensor_scan(f_n, one_col[0:AH, :].broadcast_to([AH, S]), f_f, 0.0, ALU.mult, ALU.add).then_inc(nf_ready, 1)

            choose(*CHOICE_TILE[-2:])

            def maxima(n, kind, h):
                at0 = 0
                if n >= 3:
                    ve.wait_ge(prob_ready, NT * (n - 2))
                    k2, h2 = HEADS[n - 3]
                    for i in range(NT):
                        full(ve, (k2 + "T", h2, i))
                if kind == "f":
                    taken(ve, ("nF", h))
                for i in range(NT):
                    w = (i + 1) * P
                    name = (kind + "s", h, i)
                    if kind == "f":
                        bias = nf_bc[n % 2][:, 0:w]
                    else:
                        bias = chunk_bias if i == 0 else score[:, i - 1, 0:w]
                        if i and h == 0:
                            ve.wait_ge(sel_ready, i)
                    free(ve.tensor_tensor_reduce(prob[n % 3][:, at0 * P:at0 * P + w], full(ve, name)[:, 0:w], bias, 1.0,
                                                 LOWEST, ALU.add, ALU.max, smax[:, n % 3, i:i + 1]), name)
                    at0 += i + 1
                for i in range(NT):
                    taken(ve, (kind + "s", h, i))
                ve.tensor_scalar(smax[:, n % 3, :], smax[:, n % 3, :], -1.0, None, ALU.mult).then_inc(smax_ready, 1)

            def outputs(n, kind, h):
                ve.wait_ge(prob_ready, NT * (n + 1))
                done(ve.reciprocal(ssum[:, n % 3, :], ssum[:, n % 3, :]))
                name = (kind + "o", h)
                o = full(ve, name)[:, 0:NT * HD].rearrange("p (t c) -> p t c", t=NT)
                rec = ssum[:, n % 3, :].rearrange("p (t o) -> p t o", o=1).broadcast_to([P, NT, HD])
                free(ve.tensor_tensor(otok[kind][:, :, h * HD:(h + 1) * HD], o, rec, ALU.mult), name)

            for n, (kind, h) in enumerate(HEADS):
                maxima(n, kind, h)
                if n >= LAG:
                    outputs(n - LAG, *HEADS[n - LAG])
                if BETWEEN.get(n) == "dg":
                    ve.wait_ge(split_ready, PIECE["dg"] + 2)
                    lows("dg", 2, 3)
                    lows("fin0", 0, 1)
                if n < len(CHOICE_HEAD):
                    choose(CHOICE_HEAD[n - 1] if n else CHOICE_TILE[-1], CHOICE_HEAD[n])
            for j in range(PW // P):
                name = ("mix_pool", j)
                o = full(ve, name)
                taken(ve, ("pg", j))
                free(ve.scalar_tensor_tensor(out=pooled[j], in0=o[:, :], scalar=scol(ROW_POOL + j), in1=pgT[:, j, :],
                                             op0=ALU.mult, op1=ALU.mult), name)
            for j in range(PW // P):
                ve.wait_ge(xh_ready, XH["mix_pool", j])
                ve.tensor_tensor(xl[:, j, :], pooled[j], xh[:, j, :].bitcast(F32), ALU.subtract).then_inc(xl_ready, 1)

            def split_heads(j):
                name = ("mT", j)
                o = full(ve, name)
                ve.wait_ge(xh_ready, XH[name])
                free(ve.tensor_tensor(xl[:, 2 + j, :], o[:, :], xh[:, 2 + j, :].bitcast(F32), ALU.subtract), name)

            for j in (3, 4, 5, 0, 1):
                split_heads(j)
            outputs(len(HEADS) - 2, *HEADS[-2])
            lows("fin0", 2)
            outputs(len(HEADS) - 1, *HEADS[-1])
            lows("fin0", 3)
            split_heads(2)
            lows("fin1", 0, 1, 2, 3)
            def add_last(half, t):
                name = (f"fx{half}", t)
                xs = x[:, t, half * 512:(half + 1) * 512]
                free(ve.tensor_tensor(xs, xs, full(ve, name)[:, :], ALU.add), name)

            def norm_last(t):
                taken(ve, ("fx1", t))
                ve.wait_ge(rstd_ready[5], t + 1)
                ve.scalar_tensor_tensor(out=mixed[:, t, :], in0=x[:, t, :], scalar=rstd[:, 5, t:t + 1], in1=row_bc[:, :],
                                        op0=ALU.mult, op1=ALU.mult).then_inc(out_ready, 1)

            for t in range(NT):
                add_last(0, t)
            ve.wait_ge(ld_final, 16)
            for t in range(NT):
                add_last(1, t)
                if t:
                    norm_last(t - 1)
            norm_last(NT - 1)

        @block.gpsimd
        def _(po):
            done = stepper(po, pool_step)

            def root(o, i, n, ready):
                done(po.tensor_scalar(o, i, 1.0 / n, EPS, ALU.mult, ALU.add))
                po.tensor_tensor(o, o, minus_half[:, 0:o.shape[1]], ALU.pow).then_inc(ready, 1)

            def norm_root(s, t, count):
                po.wait_ge(sumsq_ready[s], count)
                r = rstd[:, s, t:t + 1]
                done(po.tensor_scalar(r, sumsq[:, s, 0, t:t + 1], sumsq[:, s, 1, t:t + 1], EPS, ALU.add, ALU.add))
                po.tensor_tensor(r, r, minus_half[:, 0:1], ALU.pow).then_inc(rstd_ready[s], 1)

            def renew_roots(s, count):
                for t in range(NT):
                    norm_root(2 * s - 1, t, count(t))
                    norm_root(2 * s, t, 2 * (t + 1))

            def lows(g, *pieces):
                for i in pieces:
                    low_part(po, PIECE[g] + i)

            for tile, value in ((minus_half, -0.5), (one_col, 1.0), (ones8, 1.0)):
                po.memset(tile[:, :], value).then_inc(consts_set, 1)
            po.memset(pool_w[:, :, :], 0.0).then_inc(pool_w_ready, 1)
            po.wait_ge(consts_set, 3)
            for t in range(NT):
                norm_root(0, t, 2 * t + 2)
            for w in (gate_wh, gate_wl):
                po.memset(w[:, :, ND2:GF].bitcast(F32), 0.0).then_inc(gate_w_ready, 1)
            po.wait_ge(ld_gate, 16)
            for kind in range(2):
                src = gate_w[:, :, :].rearrange("p k (d j c) -> p k d j c", d=2, j=2)[:, :, :, kind, :]
                hi, lo = (w[:, :, GF * kind:GF * kind + ND2].rearrange("p k (d c) -> p k d c", d=2) for w in (gate_wh, gate_wl))
                done(po.tensor_copy(hi, src))
                po.tensor_tensor(lo, src, hi.bitcast(F32), ALU.subtract).then_inc(gate_w_ready, 1)
            lows("hv", 0, 1, 2, 3)
            po.wait_ge(ld_masks, 16)
            po.tensor_copy(masks_one[:, :, :], masks[:, 0:3, :]).then_inc(masks_ready, 1)
            n = 0
            for q in range(2):
                for t in range(NT):
                    taken(po, ("ft", q, t, 0))
                    taken(po, ("ft", q, t, 1))
                    f, b = tap_sum[q][:, t, :], taps_b[n % 2]
                    po.tensor_tensor(tap_dif[q][:, t, :], b, f, ALU.subtract)
                    po.tensor_tensor(f, f, b, ALU.add).then_inc(taps_ready, 1)
                    n += 1
            def mirror(q, f):
                n = NF * q + f
                um, sm = wave_minus[f]
                k0, k1 = spec[q][0][:, NF + f, :], spec[q][1][:, NF + f, :]
                po.wait_ge(minus_ready, 2 * n + 2)
                for c in range(2):
                    taken(po, ("K", q, c, f, 1))
                if n:
                    po.wait_ge(mirror_ready, n)
                done(po.tensor_tensor(wave_tmp[1], um, k1, ALU.mult))
                po.tensor_tensor(k1, sm, k1, ALU.mult)
                done(po.tensor_tensor(um, um, k0, ALU.mult))
                po.tensor_tensor(k0, sm, k0, ALU.mult)
                done(po.tensor_tensor(k1, k1, um, ALU.add))
                po.tensor_tensor(k0, k0, wave_tmp[1], ALU.subtract).then_inc(mirror_ready, 1)

            def skip(q):
                full(po, ("S", q, NF - 1, 1))
                po.wait_ge(ld_fb, 16)
                for t in range(NT):
                    z = sig[q][:, t, :]
                    po.tensor_tensor(z, z, row_bc[:, q * HALF:(q + 1) * HALF], ALU.mult).then_inc(skip_ready, 1)

            def state_keys(h):
                taken(po, ("kt", h))
                taken(po, ("gcol",))
                for d in range(2):
                    if h >= 2:
                        full(po, ("up", h - 2, d))
                    for c in range(3):
                        n = c if d == 0 else NT - 1 - c
                        i = po.tensor_scalar(kw[h % 2][d][c], ktok[h % 2][:, n, :], gcol[:, 3, n, d * MH + h:d * MH + h + 1],
                                             None, ALU.mult)
                    i.then_inc(kw_ready, 1)

            def gate_head(h):
                y = hm[:, :, h * P:(h + 1) * P]
                po.wait_ge(h_ready, h + 1)
                for t in range(NT):
                    taken(po, ("mo", t))
                po.tensor_tensor(y, y, o_gate[:, :, h * P:(h + 1) * P], ALU.mult).then_inc(gated, 1)

            def head_root(h):
                po.wait_ge(sumsq_m_ready, NT * (h + 1))
                root(rstd_m[:, h, :], sumsq_m[:, h, :], 1, rstd_m_ready)

            for f in range(NF):
                mirror(0, f)
            skip(0)
            for h in range(MH):
                po.wait_ge(k_silu, h + 1)
                po.tensor_scalar(kT[:, h, :], kT[:, h, :], P ** -0.5, None, ALU.mult).then_inc(k_ready, 1)
            full(po, ("y", 0, NT - 1))
            po.memset(v1[:, :, :, P:P + 1], 1.0).then_inc(v1_ones, 1)
            state_keys(0)
            for f in range(NF):
                mirror(1, f)
            skip(1)
            state_keys(1)
            po.wait_ge(long_ready, 2 * NT)
            for t in range(NT):
                po.tensor_tensor(sq_h[:, t, :], sig[2][:, t, :], sig[2][:, t, :], ALU.mult).then_inc(sq_h_ready, 1)
            state_keys(2)
            state_keys(3)
            gate_head(0)
            po.wait_ge(gsum_h_ready, 1)
            root(rstd_h[:, :], sumsq_h[:, :], HALF // HG, rstd_h_ready)
            head_root(0)
            for h in range(1, MH):
                gate_head(h)
                head_root(h)
            renew_roots(1, lambda t: NT + t + 1)
            first = [BANK[("ff1", f)] for f in range(8)]
            for n in range(4):
                po.engine_nop().then_inc(act_ready, 1)
            with po.Fori(0, NFF // 8) as i:
                for j in range(8):
                    b, k = first[j]
                    po.wait_ge(bank_free[b], i + (k + 1))
                    r = relu[j % 4]
                    ins = po.tensor_tensor(act[:, bass.ds(8 * i + j, 1), :], r, r, ALU.mult)
                    ins.then_inc(act_ready, 1)
            renew_roots(2, lambda t: 2 * t + 2)
            po.wait_ge(split_ready, PIECE["fq"] + 2)
            lows("fq", 2, 3)
            for g in ("fk", "fg", "fv", "dq", "dk", "dv", "pool"):
                lows(g, 0, 1, 2, 3)
            lows("dg", 0, 1)

            def gate(kind):
                for n in range(AH):
                    taken(po, (kind + "o", n))
                    for t in range(NT):
                        taken(po, (kind + "g", t))
                    o = otok[kind][:, :, n * HD:(n + 1) * HD]
                    po.tensor_tensor(o, o, gtok[kind][:, :, n * HD:(n + 1) * HD], ALU.mult).then_inc(og_ready, 1)

            def add_back(o, i, by):
                done(po.tensor_copy(o[:, 0:by], i[:, 0:by]))
                done(po.tensor_tensor(o[:, by:S], i[:, by:S], i[:, 0:S - by], ALU.add))

            po.wait_ge(ld_count, 16)
            for j in range(2):
                taken(po, ("pv", j))
                v, (s2, s4, w) = pvT[:, j, :], (win[0], win[1], win[2 + j])
                add_back(s2, v, 1)
                if j == 1:
                    add_back(s4, s2, 2)
                    add_back(s2, s4, 4)
                done(po.tensor_copy(w[0:HD, :], s2[0:HD, :]))
                add_back(w[HD:P, :], s2[HD:P, :], 2 if j == 0 else 8)
                done(po.tensor_tensor(w, w, inv_count[:, j, :], ALU.mult))
                po.tensor_tensor(w, w, v, ALU.subtract).then_inc(win_ready, 1)
            gate("f")
            gate("d")
            for t in range(NT):
                norm_root(5, t, NT + t + 1)


def kernel(**inputs):
    import concourse.bacc as bacc
    from concourse.bass_utils import run_bass_kernel_spmd

    nc = bacc.Bacc("TRN2", target_bir_lowering=False, num_devices=1)
    arrays, aps = {}, {}
    for name, value in {**inputs, **constants()}.items():
        arr = np.ascontiguousarray(value)
        arrays["in_" + name] = arr
        aps[name] = nc.dram_tensor("in_" + name, arr.shape, mybir.dt.from_np(arr.dtype), kind="ExternalInput").ap()
    out = nc.dram_tensor("out", (1, S, D), F32, kind="ExternalOutput").ap()
    build_program(nc, aps, out)
    result = run_bass_kernel_spmd(nc, [arrays], core_ids=[0])
    return np.asarray(result.results[0]["out"])
```
